# Optimizing a Trainium2 kernel written in Bass

```python
import jax, jax.numpy as jnp
from jax import lax
import numpy as np
import math

D_MODEL = 1024
BATCH = 1
SEQ = 512
DEPTH = 1

CHUNK = 64
LEFT_CHUNKS = 8
BAND = LEFT_CHUNKS + 1
EPS = 1e-5
D_FF = 2816
SSD_HEADS = 16
SSD_HEAD_DIM = 64
SSD_INNER = SSD_HEADS * SSD_HEAD_DIM
SSD_GROUPS = 2
SSD_STATE = 128
CONV_WIDTH = 4
CONV_DIM = SSD_INNER + 2 * SSD_GROUPS * SSD_STATE
ATT_HEADS = 8
ATT_HEAD_DIM = 64
ATT_INNER = ATT_HEADS * ATT_HEAD_DIM
MAX_REL = 256
MIX_WIDTH = SSD_INNER + ATT_INNER
PROJ_DIM = SSD_INNER + CONV_DIM + SSD_HEADS + 3 * ATT_INNER


def rms_norm(x, w):
    xf = x.astype(jnp.float32)
    y = xf * lax.rsqrt(jnp.mean(xf * xf, axis=-1, keepdims=True) + EPS)
    return (y * w.astype(jnp.float32)).astype(x.dtype)

def swiglu(h, w_gate, w_up, w_down):
    return (jax.nn.silu(h @ w_gate) * (h @ w_up)) @ w_down

def causal_depthwise_conv(u, w, b):
    k = w.shape[0]
    out = lax.conv_general_dilated(
        u, w.astype(u.dtype)[:, None, :], window_strides=(1,), padding=[(k - 1, 0)],
        dimension_numbers=('NWC', 'WIO', 'NWC'), feature_group_count=u.shape[-1])
    return out + b.astype(u.dtype)

def ssd_chunked(xs, dt, a, bmat, cmat, d_skip):
    bsz, seqlen, n_heads, hd = xs.shape
    n_groups, n_state = bmat.shape[-2], bmat.shape[-1]
    m = n_heads // n_groups
    nc = seqlen // CHUNK
    xf = xs.astype(jnp.float32)
    xdt = (xf * dt[..., None]).reshape(bsz, nc, CHUNK, n_groups, m, hd)
    a_cs = jnp.cumsum((dt * a).reshape(bsz, nc, CHUNK, n_groups, m), axis=2)
    bc = bmat.astype(jnp.float32).reshape(bsz, nc, CHUNK, n_groups, n_state)
    cc = cmat.astype(jnp.float32).reshape(bsz, nc, CHUNK, n_groups, n_state)
    causal = jnp.tril(jnp.ones((CHUNK, CHUNK), dtype=bool))[:, :, None, None]
    seg = a_cs[:, :, :, None] - a_cs[:, :, None, :]
    decay = jnp.exp(jnp.where(causal, seg, -jnp.inf))
    cb = jnp.einsum('bclgn,bcsgn->bclsg', cc, bc)
    y_diag = jnp.einsum('bclsg,bclsgm,bcsgmp->bclgmp', cb, decay, xdt)
    decay_out = jnp.exp(a_cs[:, :, -1:] - a_cs)
    states = jnp.einsum('bclgn,bclgm,bclgmp->bcgmpn', bc, decay_out, xdt)
    chunk_decay = jnp.exp(a_cs[:, :, -1])

    def step(h, inp):
        s_c, d_c = inp
        return h * d_c[..., None, None] + s_c, h

    h0 = jnp.zeros((bsz, n_groups, m, hd, n_state), jnp.float32)
    _, prev = lax.scan(step, h0, (jnp.moveaxis(states, 1, 0), jnp.moveaxis(chunk_decay, 1, 0)))
    prev = jnp.moveaxis(prev, 0, 1)
    y_off = jnp.einsum('bclgn,bcgmpn,bclgm->bclgmp', cc, prev, jnp.exp(a_cs))
    y = (y_diag + y_off).reshape(bsz, seqlen, n_heads, hd)
    return y + xf * d_skip.astype(jnp.float32)[:, None]

def chunked_rel_attention(q, k, v, rel_bias):
    bsz, seqlen, n_heads, hd = q.shape
    nc = seqlen // CHUNK
    qc = q.reshape(bsz, nc, CHUNK, n_heads, hd)
    pad = ((0, 0), (LEFT_CHUNKS * CHUNK, 0), (0, 0), (0, 0))
    kp = jnp.pad(k, pad).reshape(bsz, nc + LEFT_CHUNKS, CHUNK, n_heads, hd)
    vp = jnp.pad(v, pad).reshape(bsz, nc + LEFT_CHUNKS, CHUNK, n_heads, hd)
    kb = jnp.stack([kp[:, o:o + nc] for o in range(BAND)], axis=2).reshape(bsz, nc, BAND * CHUNK, n_heads, hd)
    vb = jnp.stack([vp[:, o:o + nc] for o in range(BAND)], axis=2).reshape(bsz, nc, BAND * CHUNK, n_heads, hd)
    qpos = LEFT_CHUNKS * CHUNK + jnp.arange(CHUNK)
    kpos = jnp.arange(BAND * CHUNK)
    rel = jnp.clip(qpos[:, None] - kpos[None, :], -MAX_REL, MAX_REL) + MAX_REL
    bias = rel_bias.astype(jnp.float32)[:, rel]
    s = jnp.einsum('bcqhd,bckhd->bhcqk', qc, kb).astype(jnp.float32) * (hd ** -0.5) + bias[None, :, None]
    valid = (jnp.arange(nc)[:, None] - LEFT_CHUNKS + jnp.arange(BAND)[None, :]) >= 0
    valid = jnp.repeat(valid, CHUNK, axis=1)
    s = jnp.where(valid[None, None, :, None, :], s, jnp.finfo(jnp.float32).min)
    p = jax.nn.softmax(s, axis=-1).astype(v.dtype)
    o = jnp.einsum('bhcqk,bckhd->bcqhd', p, vb)
    return o.reshape(bsz, seqlen, n_heads * hd)

def hybrid_mixer(x, mix_norm, w_in, conv_w, conv_b, dt_bias, a_log, d_skip, ssd_norm, rel_bias, w_out):
    bsz, seqlen, _ = x.shape
    h = rms_norm(x, mix_norm)
    proj = h @ w_in
    o1 = SSD_INNER
    o2 = o1 + CONV_DIM
    o3 = o2 + SSD_HEADS
    o4 = o3 + ATT_INNER
    o5 = o4 + ATT_INNER
    z, xbc, dt_raw = proj[..., :o1], proj[..., o1:o2], proj[..., o2:o3]
    q, k, v = proj[..., o3:o4], proj[..., o4:o5], proj[..., o5:]
    xbc = jax.nn.silu(causal_depthwise_conv(xbc, conv_w, conv_b))
    gn = SSD_GROUPS * SSD_STATE
    xs = xbc[..., :SSD_INNER].reshape(bsz, seqlen, SSD_HEADS, SSD_HEAD_DIM)
    bm = xbc[..., SSD_INNER:SSD_INNER + gn].reshape(bsz, seqlen, SSD_GROUPS, SSD_STATE)
    cm = xbc[..., SSD_INNER + gn:].reshape(bsz, seqlen, SSD_GROUPS, SSD_STATE)
    dt = jax.nn.softplus(dt_raw.astype(jnp.float32) + dt_bias.astype(jnp.float32))
    a = -jnp.exp(a_log.astype(jnp.float32))
    y = ssd_chunked(xs, dt, a, bm, cm, d_skip).reshape(bsz, seqlen, SSD_INNER)
    y = rms_norm(y * jax.nn.silu(z.astype(jnp.float32)), ssd_norm).astype(x.dtype)
    att = chunked_rel_attention(
        q.reshape(bsz, seqlen, ATT_HEADS, ATT_HEAD_DIM),
        k.reshape(bsz, seqlen, ATT_HEADS, ATT_HEAD_DIM),
        v.reshape(bsz, seqlen, ATT_HEADS, ATT_HEAD_DIM), rel_bias).astype(x.dtype)
    return jnp.concatenate([y, att], axis=-1) @ w_out

def first_inputs(seed: int = 0) -> dict:
    key = jax.random.key(seed)
    ks = jax.random.split(key, 24)

    def nrm(k, shape, scale):
        return jax.random.normal(k, shape, jnp.float32) * scale

    def gain(k, n):
        return 1.0 + nrm(k, (DEPTH, n), 0.02)

    u = jax.random.uniform(ks[10], (DEPTH, SSD_HEADS), jnp.float32)
    dt0 = jnp.exp(u * (np.log(0.1) - np.log(0.001)) + np.log(0.001))
    dt_bias = dt0 + jnp.log(-jnp.expm1(-dt0))
    a_log = jnp.log(jax.random.uniform(ks[11], (DEPTH, SSD_HEADS), jnp.float32, 1.0, 16.0))
    return {
        "x": nrm(ks[0], (BATCH, SEQ, D_MODEL), 1.0),
        "ffn1_norm": gain(ks[1], D_MODEL),
        "ffn1_w_gate": nrm(ks[2], (DEPTH, D_MODEL, D_FF), D_MODEL ** -0.5),
        "ffn1_w_up": nrm(ks[3], (DEPTH, D_MODEL, D_FF), D_MODEL ** -0.5),
        "ffn1_w_down": nrm(ks[4], (DEPTH, D_FF, D_MODEL), D_FF ** -0.5),
        "mix_norm": gain(ks[5], D_MODEL),
        "w_in": nrm(ks[6], (DEPTH, D_MODEL, PROJ_DIM), D_MODEL ** -0.5),
        "conv_w": nrm(ks[7], (DEPTH, CONV_WIDTH, CONV_DIM), CONV_WIDTH ** -0.5),
        "conv_b": nrm(ks[8], (DEPTH, CONV_DIM), 0.02),
        "dt_bias": dt_bias,
        "a_log": a_log,
        "d_skip": 1.0 + nrm(ks[12], (DEPTH, SSD_HEADS), 0.1),
        "ssd_norm": gain(ks[13], SSD_INNER),
        "rel_bias": nrm(ks[14], (DEPTH, ATT_HEADS, 2 * MAX_REL + 1), 0.1),
        "w_out": nrm(ks[15], (DEPTH, MIX_WIDTH, D_MODEL), MIX_WIDTH ** -0.5),
        "ffn2_norm": gain(ks[16], D_MODEL),
        "ffn2_w_gate": nrm(ks[17], (DEPTH, D_MODEL, D_FF), D_MODEL ** -0.5),
        "ffn2_w_up": nrm(ks[18], (DEPTH, D_MODEL, D_FF), D_MODEL ** -0.5),
        "ffn2_w_down": nrm(ks[19], (DEPTH, D_FF, D_MODEL), D_FF ** -0.5),
        "final_norm": 1.0 + nrm(ks[20], (D_MODEL,), 0.02),
    }

def first_block(x, ffn1_norm, ffn1_w_gate, ffn1_w_up, ffn1_w_down, mix_norm, w_in, conv_w, conv_b,
              dt_bias, a_log, d_skip, ssd_norm, rel_bias, w_out, ffn2_norm, ffn2_w_gate, ffn2_w_up,
              ffn2_w_down, final_norm):
    for i in range(DEPTH):
        x = x + 0.5 * swiglu(rms_norm(x, ffn1_norm[i]), ffn1_w_gate[i], ffn1_w_up[i], ffn1_w_down[i])
        x = x + hybrid_mixer(x, mix_norm[i], w_in[i], conv_w[i], conv_b[i], dt_bias[i], a_log[i],
                             d_skip[i], ssd_norm[i], rel_bias[i], w_out[i])
        x = x + 0.5 * swiglu(rms_norm(x, ffn2_norm[i]), ffn2_w_gate[i], ffn2_w_up[i], ffn2_w_down[i])
    return rms_norm(x, final_norm)


DEPTH_2 = 2

PLE_DIM = 256
N_A_LAYERS = DEPTH_2 // 2
N_B_LAYERS = DEPTH_2 - N_A_LAYERS
GDN_HEADS = 8
GDN_HEAD_DIM = 128
GDN_WIDTH = GDN_HEADS * GDN_HEAD_DIM
GDN_CHUNK = 64
SB_HEADS = 8
SB_HEAD_DIM = 128
SB_WIDTH = SB_HEADS * SB_HEAD_DIM
SB_BLOCK = 128
FFN_HIDDEN = -(-8 * D_MODEL // (3 * 256)) * 256
EPS_2 = 1e-6


def rms_norm_2(x, g):
    xf = x.astype(jnp.float32)
    y = xf * lax.rsqrt(jnp.mean(xf * xf, axis=-1, keepdims=True) + EPS_2)
    return (y * g.astype(jnp.float32)).astype(x.dtype)

def l2_norm(x):
    return x * lax.rsqrt(jnp.sum(x * x, axis=-1, keepdims=True) + EPS_2)

def causal_conv(x, w):
    k_w, c = w.shape
    return lax.conv_general_dilated(x, w[:, None, :], window_strides=(1,), padding=[(k_w - 1, 0)],
                                    dimension_numbers=('NWC', 'WIO', 'NWC'), feature_group_count=c)

def to_chunks(t):
    b, s, h = t.shape[:3]
    t = t.reshape((b, s // GDN_CHUNK, GDN_CHUNK, h) + t.shape[3:])
    return jnp.swapaxes(t, 2, 3)

def gated_delta_rule(q, k, v, g, beta):
    b_, s_, h_, dk = q.shape
    dv = v.shape[-1]
    c = GDN_CHUNK
    q, k, v, g, beta = to_chunks(q), to_chunks(k), to_chunks(v), to_chunks(g), to_chunks(beta)
    G = jnp.cumsum(g, axis=-1)
    causal = jnp.tril(jnp.ones((c, c), dtype=bool))
    strict = jnp.tril(jnp.ones((c, c), dtype=bool), -1)
    decay_mat = jnp.exp(jnp.where(causal, G[..., :, None] - G[..., None, :], -jnp.inf))
    kk = jnp.einsum('bnhrd,bnhsd->bnhrs', k, k)
    a_low = jnp.where(strict, beta[..., None] * kk * decay_mat, 0.0)
    eye = jnp.eye(c, dtype=q.dtype)
    rhs = jnp.concatenate([v * beta[..., None], k * (beta * jnp.exp(G))[..., None]], axis=-1)
    sol = lax.linalg.triangular_solve(a_low + eye, rhs, left_side=True, lower=True, unit_diagonal=True)
    u, w = sol[..., :dv], sol[..., dv:]
    qk = jnp.einsum('bnhrd,bnhsd->bnhrs', q, k) * decay_mat
    q_dec = q * jnp.exp(G)[..., None]
    k_dec = k * jnp.exp(G[..., -1:] - G)[..., None]
    g_last = jnp.exp(G[..., -1])

    def step(state, xs):
        q_c, k_c, qk_c, u_c, w_c, gl_c = xs
        v_new = u_c - jnp.einsum('bhcd,bhde->bhce', w_c, state)
        o = jnp.einsum('bhcd,bhde->bhce', q_c, state) + jnp.einsum('bhrs,bhse->bhre', qk_c, v_new)
        state = state * gl_c[..., None, None] + jnp.einsum('bhcd,bhce->bhde', k_c, v_new)
        return state, o

    xs = tuple(jnp.moveaxis(t, 1, 0) for t in (q_dec, k_dec, qk, u, w, g_last))
    s0 = jnp.zeros((b_, h_, dk, dv), q.dtype)
    _, o = lax.scan(step, s0, xs)
    return o.transpose(1, 0, 3, 2, 4).reshape(b_, s_, h_, dv)

def gdn_mixer(hn, w_in, w_conv, a_log, dt_bias, norm_g, w_out):
    b_, s_, _ = hn.shape
    proj = hn @ w_in
    qkv = jax.nn.silu(causal_conv(proj[..., :3 * GDN_WIDTH], w_conv))
    gate = proj[..., 3 * GDN_WIDTH:4 * GDN_WIDTH].reshape(b_, s_, GDN_HEADS, GDN_HEAD_DIM)
    a_in = proj[..., 4 * GDN_WIDTH:4 * GDN_WIDTH + GDN_HEADS].astype(jnp.float32)
    b_in = proj[..., 4 * GDN_WIDTH + GDN_HEADS:].astype(jnp.float32)
    qkv = qkv.astype(jnp.float32).reshape(b_, s_, 3, GDN_HEADS, GDN_HEAD_DIM)
    q = l2_norm(qkv[:, :, 0]) * (GDN_HEAD_DIM ** -0.5)
    k = l2_norm(qkv[:, :, 1])
    v = qkv[:, :, 2]
    beta = jax.nn.sigmoid(b_in)
    g = -jnp.exp(a_log.astype(jnp.float32)) * jax.nn.softplus(a_in + dt_bias.astype(jnp.float32))
    o = gated_delta_rule(q, k, v, g, beta).astype(hn.dtype)
    o = rms_norm_2(o, norm_g) * jax.nn.silu(gate)
    return o.reshape(b_, s_, GDN_WIDTH) @ w_out

def shared_kv(h, kv_norm, w_kv, k_norm):
    b_, s_, _ = h.shape
    kv = (rms_norm_2(h, kv_norm) @ w_kv).reshape(b_, s_, 2, SB_HEADS, SB_HEAD_DIM)
    k = rms_norm_2(kv[:, :, 0], k_norm).transpose(0, 2, 1, 3)
    v = kv[:, :, 1].transpose(0, 2, 1, 3)
    return k, v

def stick_breaking(q, k, v):
    s_ = q.shape[2]
    outs = []
    for blk in range(s_ // SB_BLOCK):
        t0, t1 = blk * SB_BLOCK, (blk + 1) * SB_BLOCK
        z = jnp.einsum('bhtd,bhsd->bhts', q[:, :, t0:t1], k[:, :, :t1]).astype(jnp.float32)
        t_idx = t0 + jnp.arange(SB_BLOCK)[:, None]
        s_idx = jnp.arange(t1)[None, :]
        mask = s_idx < t_idx
        log_not = jnp.where(mask, jax.nn.log_sigmoid(-z), 0.0)
        suffix = lax.cumsum(log_not, axis=3, reverse=True) - log_not
        log_w = jnp.where(mask, jax.nn.log_sigmoid(z) + suffix, -jnp.inf)
        wgt = jnp.exp(log_w).astype(v.dtype)
        outs.append(jnp.einsum('bhts,bhsd->bhtd', wgt, v[:, :, :t1]))
    return jnp.concatenate(outs, axis=2)

def sb_mixer(hn, k_sh, v_sh, w_q, q_norm, w_out):
    b_, s_, _ = hn.shape
    q = (hn @ w_q).reshape(b_, s_, SB_HEADS, SB_HEAD_DIM)
    q = (rms_norm_2(q, q_norm) * (SB_HEAD_DIM ** -0.5)).transpose(0, 2, 1, 3)
    o = stick_breaking(q, k_sh, v_sh)
    return o.transpose(0, 2, 1, 3).reshape(b_, s_, SB_WIDTH) @ w_out

def swiglu_2(hn, w_in, w_out):
    gu = hn @ w_in
    return (jax.nn.silu(gu[..., :FFN_HIDDEN]) * gu[..., FFN_HIDDEN:]) @ w_out

def second_inputs(seed: int = 0) -> dict:
    key = jax.random.key(seed)
    ks = jax.random.split(key, 24)
    f32 = jnp.float32

    def nrm(k, shape, fan_in):
        return jax.random.normal(k, shape, f32) * (fan_in ** -0.5)

    def gain(k, shape):
        return 1.0 + 0.02 * jax.random.normal(k, shape, f32)

    dt = jnp.exp(jax.random.uniform(ks[8], (N_A_LAYERS, GDN_HEADS), f32, math.log(1e-3), math.log(1e-1)))
    return {
        "x": jax.random.normal(ks[0], (BATCH, SEQ, D_MODEL), f32),
        "p": jax.random.normal(ks[1], (DEPTH_2, BATCH, SEQ, PLE_DIM), f32),
        "ln_mix": gain(ks[2], (DEPTH_2, D_MODEL)),
        "ln_ffn": gain(ks[3], (DEPTH_2, D_MODEL)),
        "ln_ple": gain(ks[4], (DEPTH_2, D_MODEL)),
        "gdn_w_in": nrm(ks[5], (N_A_LAYERS, D_MODEL, 4 * GDN_WIDTH + 2 * GDN_HEADS), D_MODEL),
        "gdn_conv": nrm(ks[6], (N_A_LAYERS, CONV_WIDTH, 3 * GDN_WIDTH), CONV_WIDTH),
        "gdn_a_log": jnp.log(jax.random.uniform(ks[7], (N_A_LAYERS, GDN_HEADS), f32, 1.0, 16.0)),
        "gdn_dt_bias": dt + jnp.log(-jnp.expm1(-dt)),
        "gdn_norm": gain(ks[9], (N_A_LAYERS, GDN_HEAD_DIM)),
        "gdn_w_out": nrm(ks[10], (N_A_LAYERS, GDN_WIDTH, D_MODEL), GDN_WIDTH),
        "kv_norm": gain(ks[11], (D_MODEL,)),
        "w_kv": nrm(ks[12], (D_MODEL, 2 * SB_WIDTH), D_MODEL),
        "k_norm": gain(ks[13], (SB_HEAD_DIM,)),
        "sb_w_q": nrm(ks[14], (N_B_LAYERS, D_MODEL, SB_WIDTH), D_MODEL),
        "sb_q_norm": gain(ks[15], (N_B_LAYERS, SB_HEAD_DIM)),
        "sb_w_out": nrm(ks[16], (N_B_LAYERS, SB_WIDTH, D_MODEL), SB_WIDTH),
        "ffn_w_in": nrm(ks[17], (DEPTH_2, D_MODEL, 2 * FFN_HIDDEN), D_MODEL),
        "ffn_w_out": nrm(ks[18], (DEPTH_2, FFN_HIDDEN, D_MODEL), FFN_HIDDEN),
        "ple_w_proj": nrm(ks[19], (DEPTH_2, PLE_DIM, D_MODEL), PLE_DIM),
        "ple_w_gate": nrm(ks[20], (DEPTH_2, D_MODEL, D_MODEL), D_MODEL),
    }

def second_block(x, p, ln_mix, ln_ffn, ln_ple, gdn_w_in, gdn_conv, gdn_a_log, gdn_dt_bias, gdn_norm,
              gdn_w_out, kv_norm, w_kv, k_norm, sb_w_q, sb_q_norm, sb_w_out, ffn_w_in, ffn_w_out,
              ple_w_proj, ple_w_gate):
    h = x
    k_sh, v_sh = None, None
    for i in range(DEPTH_2):
        hn = rms_norm_2(h, ln_mix[i])
        if i < N_A_LAYERS:
            h = h + gdn_mixer(hn, gdn_w_in[i], gdn_conv[i], gdn_a_log[i], gdn_dt_bias[i],
                              gdn_norm[i], gdn_w_out[i])
        else:
            j = i - N_A_LAYERS
            h = h + sb_mixer(hn, k_sh, v_sh, sb_w_q[j], sb_q_norm[j], sb_w_out[j])
        h = h + swiglu_2(rms_norm_2(h, ln_ffn[i]), ffn_w_in[i], ffn_w_out[i])
        h = h + (p[i] @ ple_w_proj[i]) * jax.nn.sigmoid(rms_norm_2(h, ln_ple[i]) @ ple_w_gate[i])
        if i == N_A_LAYERS - 1:
            k_sh, v_sh = shared_kv(h, kv_norm, w_kv, k_norm)
    return h


def setup_inputs(seed=0):
    out = dict(first_inputs(seed))
    for name, value in second_inputs(seed + 1).items():
        if name != "x":
            out[name + "_2"] = value
    return out


def reference(
    x, ffn1_norm, ffn1_w_gate, ffn1_w_up, ffn1_w_down, mix_norm, w_in, conv_w, conv_b, dt_bias,
    a_log, d_skip, ssd_norm, rel_bias, w_out, ffn2_norm, ffn2_w_gate, ffn2_w_up, ffn2_w_down,
    final_norm, p_2, ln_mix_2, ln_ffn_2, ln_ple_2, gdn_w_in_2, gdn_conv_2, gdn_a_log_2,
    gdn_dt_bias_2, gdn_norm_2, gdn_w_out_2, kv_norm_2, w_kv_2, k_norm_2, sb_w_q_2, sb_q_norm_2,
    sb_w_out_2, ffn_w_in_2, ffn_w_out_2, ple_w_proj_2, ple_w_gate_2,
):
    x = first_block(
        x, ffn1_norm, ffn1_w_gate, ffn1_w_up, ffn1_w_down, mix_norm, w_in, conv_w, conv_b,
        dt_bias, a_log, d_skip, ssd_norm, rel_bias, w_out, ffn2_norm, ffn2_w_gate, ffn2_w_up,
        ffn2_w_down, final_norm,
    )
    return second_block(
        x, p_2, ln_mix_2, ln_ffn_2, ln_ple_2, gdn_w_in_2, gdn_conv_2, gdn_a_log_2,
        gdn_dt_bias_2, gdn_norm_2, gdn_w_out_2, kv_norm_2, w_kv_2, k_norm_2, sb_w_q_2,
        sb_q_norm_2, sb_w_out_2, ffn_w_in_2, ffn_w_out_2, ple_w_proj_2, ple_w_gate_2,
    )


_drawn_inputs = setup_inputs


def setup_inputs(seed=0):
    import zlib

    import numpy as np

    out = dict(_drawn_inputs(seed))
    spreads = {}
    factors = {'ffn1_norm': 3.893,
     'ssd_norm': 3.308,
     'rel_bias': 8.0,
     'ffn2_norm': 6.852,
     'ln_mix_2': 3.123,
     'ln_ffn_2': 3.433,
     'ln_ple_2': 8.0,
     'gdn_norm_2': 5.903,
     'kv_norm_2': 5.655,
     'k_norm_2': 8.0,
     'sb_q_norm_2': 8.0}
    for name, (base, spread) in spreads.items():
        noise = np.random.default_rng([zlib.crc32(name.encode()), seed]).standard_normal(out[name].shape)
        drawn = base * np.exp(spread * noise) if base else spread * noise
        out[name] = __import__('jax').numpy.asarray(drawn.astype(out[name].dtype))
    for name, factor in factors.items():
        out[name] = (out[name] * factor).astype(out[name].dtype)
    return out
```

```python
from contextlib import ExitStack, contextmanager

import numpy as np
import concourse.bass as bass
from concourse import mybir

F32, F32R = mybir.dt.float32, mybir.dt.float32r
ALU, ACT, AX = mybir.AluOpType, mybir.ActivationFunctionType, mybir.AxisListType

P = 128
T = 512
NB = T // P
D = 1024
DK = D // P
D_FF = 2816
HALVES = (12, 10)
CONV = 4
SSD_HEADS, SSD_DIM = 16, 64
ATT_HEADS, ATT_DIM = 8, 64
REL = 256
GDN_HEADS = 8
EPS_1, EPS_2 = 1e-5, 1e-6
UNIT = 8 * P
W_SLOTS, RAW_SLOTS = 4, 2
AHEAD = 3
MASKED = -3.0e38


def column_plan():
    plan, at = {}, 0
    for name, n in (("ffn1_norm", 8), ("mix_norm", 8), ("ffn2_norm", 8), ("final_norm", 8), ("ssd_norm", 8),
                    ("conv_w", 12 * CONV), ("conv_b", 12), ("dt_bias", 1), ("a_log", 1), ("d_skip", 8),
                    ("ln_mix0", 8), ("ln_mix1", 8), ("ln_ffn0", 8), ("ln_ffn1", 8), ("ln_ple0", 8), ("ln_ple1", 8),
                    ("gdn_conv", 24 * CONV), ("gdn_a_log", 1), ("gdn_dt_bias", 1), ("gdn_norm", 1),
                    ("kv_norm", 8), ("k_norm", 1), ("sb_q_norm", 1)):
        plan[name] = (at, n)
        at += n
    return plan, at


COL, N_COL = column_plan()
LEVELS = (1, 2, 4, 8, 16, 32, 64)
MASKS = ["ident", "ones", "upper", "strict", "neg_tri", "neg_ones"] + [f"merge{b}" for b in LEVELS]


def constant_tiles():
    s, r = np.meshgrid(np.arange(P), np.arange(P), indexing="ij")
    tiles = [s == r, s >= 0, r >= s, r > s, -(s >= r).astype(np.float32), -np.ones((P, P))]
    for b in LEVELS:
        tiles.append((s // (2 * b) == r // (2 * b)) & (s % (2 * b) < b) & (r % (2 * b) >= b))
    return np.stack([np.asarray(t, np.float32) for t in tiles], axis=1)


class Walk:

    def __init__(self):
        self.unit = 0
        self.bank = 0
        self.group = 0
        self.prev_bank = 0
        self.squares = 0
        self.tiles = 0
        self.sums = 0
        self.norms = 0
        self.mids = 0
        self.gated = 0
        self.hups = 0
        self.plo = 0
        self.tile_norms = 0

    def column_layer(self, count):
        at = (self.unit, self.bank, self.group)
        self.prev_bank = self.bank
        self.unit += count
        self.bank += count
        self.group ^= 1
        return at

    def square_layer(self, units):
        at = (self.unit, self.bank, self.group, self.prev_bank, self.squares)
        self.prev_bank = self.bank
        self.unit += units
        self.bank += 4
        self.group ^= 1
        self.squares += 1
        return at


def each(eng, count, body, first=0, begin=0):
    at, end = begin + first, begin + count
    for u in range(begin, at):
        body(0, u)
    laps = (end - at) // 4
    if laps >= 2:
        with eng.Fori(0, laps) as i:
            for j in range(at, at + 4):
                body(i, j)
        at += laps * 4
    for u in range(at, end):
        body(0, u)


def tile_at(t, u):
    if isinstance(u, int):
        return t[:, u, :]
    return t[:, bass.ds(u, 1), :].rearrange("p a t -> p (a t)")


def col_at(t, u, n=1):
    return t[:, u:u + n] if isinstance(u, int) else t[:, bass.ds(u, n)]


class Chain:

    def __init__(self, eng, sem):
        self.eng, self.sem, self.n, self.turn = eng, sem, 0, 0

    def step(self, ins):
        ins.then_inc(self.sem, 1)
        self.n += 1

    def wait(self):
        self.eng.wait_ge(self.sem, self.turn + self.n)

    def link(self, ins):
        self.step(ins)
        self.wait()

    @contextmanager
    def loop(self, count, per):
        start = self.n
        with self.eng.Fori(0, count) as i:
            self.turn = i * per
            yield i
        assert self.n - start == per, (self.n - start, per)
        self.turn, self.n = 0, start + count * per


def build(nc, units, x_t, p_t, vectors, constants, rel_table, out_t):
    base = (nc.sbuf_base + 31) // 32 * 32
    limit = nc.sbuf_usable_end
    KB = 1024

    def place(name, at, shape, dtype=F32):
        size = int(np.prod(shape[1:])) * 4
        assert base + at + size <= limit, (name, base + at + size, limit)
        return nc.alloc_sbuf_tensor_at(name, shape, dtype, offset=base + at)

    with ExitStack() as ctx:
        def sem(name):
            return ctx.enter_context(nc.semaphore(name))

        raw = place("raw", 0, [P, RAW_SLOTS, UNIT])
        w_hi = place("w_hi", 8 * KB, [P, W_SLOTS, UNIT], F32R)
        w_lo = place("w_lo", 24 * KB, [P, W_SLOTS, UNIT], F32R)
        h = place("h", 40 * KB, [P, DK, T])
        x_hi = place("x_hi", 56 * KB, [P, DK, T], F32R)
        x_lo = place("x_lo", 72 * KB, [P, DK, T], F32R)
        mid_hi = place("mid_hi", 88 * KB, [P, 12, T], F32R)
        mid_lo = place("mid_lo", 112 * KB, [P, 12, T], F32R)
        rstd = place("rstd", 136 * KB, [P, T])
        sum_sq = place("sum_sq", 138 * KB, [P, T])
        sq = place("sq", 140 * KB, [P, 2, T])
        vec = place("vec", 144 * KB, [P, N_COL])
        assert N_COL <= 320
        const = place("const", 144 * KB + 1280, [P, len(MASKS), P])
        XG, MID_HI, MID_LO = 56 * KB, 88 * KB, 112 * KB
        M = 152 * KB
        mask = {name: const[:, i, :] for i, name in enumerate(MASKS)}
        ident, ones = mask["ident"], mask["ones"]

        ff_gate = place("ff_gate", M, [P, 2, T])
        ff_up = place("ff_up", M + 4 * KB, [P, 2, T])
        p_f = place("p_f", M + 8 * KB, [P, 2, T])
        p_part = place("p_part", M + 16 * KB, [P, DK, T])
        qk = place("qk", M, [P, 8, T])
        v_tok = place("v_tok", M + 16 * KB, [P, NB, T])
        toep = place("toep", M + 24 * KB, [P, ATT_HEADS, T])
        bc = place("bc", M + 40 * KB, [P, 4, T])
        cs_row = place("cs_row", M + 48 * KB, [SSD_HEADS, T])
        cols1 = place("cols1", M + 50 * KB, [P, NB, 2, SSD_HEADS])
        pad1 = place("pad1", M + 24 * KB, [P, 2, T + 4])
        cv1 = place("cv1", M + 24 * KB + 4160, [P, 2, T])
        z_tmp = place("z_tmp", M + 24 * KB + 8256, [P, 2, T])
        xs = place("xs", MID_HI, [P, 8, T])
        zs = place("zs", MID_LO, [P, 8, T])
        dt_raw = place("dt_raw", MID_HI + 16 * KB, [SSD_HEADS, T])
        dt_abs = place("dt_abs", MID_HI + 18 * KB, [SSD_HEADS, T])
        dt_row = place("dt_row", M + 52 * KB, [SSD_HEADS, T])
        da_row = place("da_row", MID_HI + 22 * KB, [SSD_HEADS, T])
        a_neg = place("a_neg", M + 50 * KB + 512, [SSD_HEADS, 1])
        at_q = place("at_q", XG, [P, T])
        at_v = place("at_v", XG + 2 * KB, [P, NB, P])
        at_s = place("at_s", XG + 4 * KB, [P, 2, 10, P])
        at_k = place("at_k", XG + 14 * KB, [P, T])
        at_pt = place("at_pt", XG + 16 * KB, [P, 2, 10, P])
        at_stat = place("at_stat", XG + 30 * KB, [P, 2, 3, NB])
        x_tok = place("x_tok", XG, [P, NB, D])
        cb = place("cb", XG + 16 * KB, [P, 2, 10, P])
        xdt = place("xdt", M + 24 * KB, [P, 2, NB, SSD_DIM])
        decay = place("decay", M + 26 * KB, [P, 2, 10, P])
        bias_c = place("bias_c", M + 50 * KB + 544, [P, 10, SSD_HEADS])
        total_c = place("total_c", M + 50 * KB + 1184, [P, NB, SSD_HEADS])
        sel1 = place("sel1", M + 42 * KB, [SSD_HEADS, 2, P])
        y_tmp = place("y_tmp", M, [P, 2, T])
        qk2 = place("qk2", M, [P, 16, T])
        gate2 = place("gate2", M + 32 * KB, [P, 8, T])
        g_row = place("g_row", M + 48 * KB, [40, T])
        cols2 = place("cols2", M + 50 * KB, [P, NB, 40])
        v2 = place("v2", MID_LO, [P, 8, T])
        pad2 = place("pad2", MID_HI, [P, 2, T + 4])
        cv2 = place("cv2", MID_HI + 4160, [P, 2, T])
        ga = place("ga", MID_HI + 9 * KB, [40, 4, T])
        a_neg2 = place("a_neg2", M + 50 * KB + 640, [8, 1])
        g_names = ["k_st", "em", "eg", "at", "tt", "tm", "ao", "u_", "kb", "vb", "wt", "uu", "qkt", "qd"]
        gw = {}
        spots = [XG + 2 * KB * i for i in range(16)] + [MID_HI + 2 * KB * i for i in range(12)] + [MID_LO + 16 * KB + 2 * KB * i for i in range(4)]
        for n_, name in enumerate(g_names):
            gw[name] = [place(f"{name}{j}", spots[2 * n_ + j], [P, NB, P]) for j in range(2)]
        gw["kd"] = [place(f"kd{j}", spots[28 + j], [P, NB, P]) for j in range(2)]
        gw["st"] = [place(f"st{j}", spots[30] + j * 512, [P, P]) for j in range(2)]
        gw["vn"] = [place(f"vn{j}", spots[30] + 1024 + j * 512, [P, P]) for j in range(2)]
        gw["sel"] = [place(f"sel{j}", spots[31] + j * 1024, [40, 2, P]) for j in range(2)]
        g_dec = place("g_dec", M + 50 * KB + 800, [P, NB, 8])
        g_exp = place("g_exp", M + 50 * KB + 928, [P, NB, 8])
        g_tmp = place("g_tmp", MID_HI + 17 * KB, [P, 2, T])
        nrm = place("nrm", XG, [P, 2, 2, T])
        k3 = place("k3", M, [P, 8, T])
        v3 = place("v3", M + 16 * KB, [P, NB, D])
        q3 = place("q3", M + 32 * KB, [P, 8, T])
        sb_l = place("sb_l", XG, [P, 2, 10, P])
        sb_sp = place("sb_sp", XG + 10 * KB, [P, 2, 10, P])
        sb_k = place("sb_k", XG + 20 * KB, [P, 2, T])
        sb_v = place("sb_v", XG + 24 * KB, [P, 2, NB, P])

        ps = ctx.enter_context(nc.psum_tensor("ps", [P, 8, T], F32))

        s_const = sem("constants_loaded")
        s_x = sem("x_loaded")
        s_w = [sem(f"unit_loaded_{i}") for i in range(RAW_SLOTS)]
        s_whi = sem("w_hi_ready")
        s_wlo = sem("w_lo_ready")
        s_used = sem("units_used")
        s_bank = sem("square_result_ready")
        s_free = sem("banks_free")
        s_xhi = sem("x_hi_ready")
        s_sq = sem("square_ready")
        s_sum = sem("squares_summed")
        s_xlo = sem("x_lo_ready")
        s_msum = sem("sum_over_features_ready")
        s_lnv = sem("log_variance_ready")
        s_rstd = sem("rstd_ready")
        s_act1 = sem("gate_activated")
        s_prod = sem("gated_ready")
        s_mhi = sem("mid_hi_ready")
        s_mlo = sem("mid_lo_ready")
        s_dve = sem("vector_steps")
        s_act = sem("scalar_steps")
        s_hup = sem("h_updated")
        s_p = sem("p_loaded")
        s_phi = sem("p_hi_ready")
        s_plo = sem("p_lo_ready")
        s_out = sem("out_written")
        s_tick = {e: sem(f"tick_{e}") for e in ("sp", "pool")}
        N_UNITS = units.shape[0]
        NREAL = N_UNITS - 4

        def pe_norm_sum(pe, w, bank):
            pe.wait_ge(s_sum, 8 * (w.norms + 1))
            nc.tensor.matmul(ps[:, bank, :], ones, sum_sq[:, :], start=True, stop=True).then_inc(s_msum, 1)

        def pe_column_layer(pe, w, count, after_first=None):
            n0, b0, g = w.column_layer(count)

            def body(i, j):
                u, slot = i * 4 + j, (n0 + j) % W_SLOTS
                pe.wait_ge(s_wlo, n0 + u + 1)
                pe.wait_ge(s_free, b0 + u + 1)
                for k in range(DK):
                    if j == 0:
                        pe.wait_ge(s_xlo, w.tiles - DK + k + 1)
                    hi, lo = w_hi[:, slot, k * P:(k + 1) * P], w_lo[:, slot, k * P:(k + 1) * P]
                    out = ps[:, 4 * g + j % 4, :]
                    nc.tensor.matmul(out, hi, x_hi[:, k, :], start=(k == 0), stop=False)
                    nc.tensor.matmul(out, hi, x_lo[:, k, :], start=False, stop=False)
                    last = nc.tensor.matmul(out, lo, x_hi[:, k, :], start=False, stop=(k == DK - 1))
                last.then_inc(s_used, 1)
                if j == 0 and after_first is not None:
                    after_first(4 * (g ^ 1))

            each(pe, count, body, first=1)

        def pe_square_half(pe, w, tiles, rhs, ready):
            n0, b0, g, prev, _ = w.square_layer(tiles // 2)
            for kp in range(tiles // 2):
                slot = (n0 + kp) % W_SLOTS
                pe.wait_ge(s_wlo, n0 + kp + 1)
                if kp == 0:
                    pe.wait_ge(s_free, prev + 4)
                for k2 in range(2):
                    k = 2 * kp + k2
                    ready(k)
                    r_hi, r_lo = rhs(k)
                    for m in range(4):
                        at = k2 * T + m * P
                        hi, lo = w_hi[:, slot, at:at + P], w_lo[:, slot, at:at + P]
                        out = ps[:, 4 * g + m, :]
                        nc.tensor.matmul(out, hi, r_hi, start=(k == 0), stop=False)
                        nc.tensor.matmul(out, hi, r_lo, start=False, stop=False)
                        last = nc.tensor.matmul(out, lo, r_hi, start=False, stop=(k == tiles - 1))
                        if k == tiles - 1 and m < 3:
                            last.then_inc(s_bank, 1)
                last.then_inc(s_used, 1)

        def pe_square_tokens(pe, w):
            n0, b0, g, prev, _ = w.square_layer(4)
            for kp in range(4):
                slot = (n0 + kp) % W_SLOTS
                pe.wait_ge(s_wlo, n0 + kp + 1)
                if kp == 0:
                    pe.wait_ge(s_free, prev + 4)
                for k2 in range(2):
                    k = 2 * kp + k2
                    hi, lo = w_hi[:, slot, k2 * T:(k2 + 1) * T], w_lo[:, slot, k2 * T:(k2 + 1) * T]
                    for m in range(4):
                        t_hi, t_lo = x_hi[:, k, m * P:(m + 1) * P], x_lo[:, k, m * P:(m + 1) * P]
                        out = ps[:, 4 * g + m, :]
                        nc.tensor.matmul(out, t_hi, hi, start=(k == 0), stop=False)
                        nc.tensor.matmul(out, t_lo, hi, start=False, stop=False)
                        last = nc.tensor.matmul(out, t_hi, lo, start=False, stop=(k == DK - 1))
                        if k == DK - 1 and m < 3:
                            last.then_inc(s_bank, 1)
                last.then_inc(s_used, 1)

        def wait_square(eng, layer, units_, m):
            n0, _, _, _, squares = layer
            if m < 3:
                eng.wait_ge(s_bank, 3 * squares + m + 1)
            else:
                eng.wait_ge(s_used, n0 + units_)

        def act_round(act, i, n):
            act.wait_ge(s_w[n % RAW_SLOTS], i * 32 + 16 * (n // RAW_SLOTS + 1))
            if n >= W_SLOTS:
                act.wait_ge(s_used, i * 4 + (n + 1 - W_SLOTS))
            nc.scalar.activation(w_hi[:, n % W_SLOTS, :], raw[:, n % RAW_SLOTS, :], ACT.Copy).then_inc(s_whi, 1)

        def act_ahead(act, n0, i, j):
            act_round(act, i, n0 + j + AHEAD)

        def act_prep(act, w, tiles, gain, ready, squares=True):
            c = COL[gain][0] if gain else None
            for m in tiles:
                ready(m)
                if gain:
                    nc.scalar.activation(x_hi[:, m, :], h[:, m, :], ACT.Copy, scale=vec[:, c + m:c + m + 1]).then_inc(s_xhi, 1)
                    w.tiles += 1
                if squares:
                    if w.sums >= 2:
                        act.wait_ge(s_sum, w.sums - 1)
                    nc.scalar.activation(sq[:, m % 2, :], h[:, m, :], ACT.Square).then_inc(s_sq, 1)
                    w.sums += 1

        def dve_prep(dve, w, tiles, gain, squares=True):
            for m in tiles:
                if gain:
                    c = COL[gain][0] + m
                    dve.wait_ge(s_xhi, w.tiles + 1)
                    nc.vector.scalar_tensor_tensor(out=x_lo[:, m, :], in0=h[:, m, :], scalar=vec[:, c:c + 1],
                                                   in1=x_hi[:, m, :].bitcast(F32), op0=ALU.mult, op1=ALU.subtract).then_inc(s_xlo, 1)
                    w.tiles += 1
                if squares:
                    dve.wait_ge(s_sq, w.sums + 1)
                    if m == 0:
                        nc.vector.tensor_copy(sum_sq[:, :], sq[:, 0, :]).then_inc(s_sum, 1)
                    else:
                        dve.wait_ge(s_sum, w.sums)
                        nc.vector.tensor_tensor(sum_sq[:, :], sum_sq[:, :], sq[:, m % 2, :], ALU.add).then_inc(s_sum, 1)
                    w.sums += 1

        def act_rstd(act, w, bank, eps):
            act.wait_ge(s_msum, w.norms + 1)
            nc.scalar.activation(rstd[:, :], ps[:, bank, :], ACT.Ln, bias=eps, scale=1.0 / D).then_inc(s_lnv, 1)
            act.wait_ge(s_lnv, w.norms + 1)
            nc.scalar.activation(rstd[:, :], rstd[:, :], ACT.Exp, scale=-0.5).then_inc(s_rstd, 1)
            w.norms += 1

        def pe_ffn(pe, w):
            for half, tiles in enumerate(HALVES):
                if half == 0:
                    w.tiles += DK
                    pe_column_layer(pe, w, 2 * tiles, lambda bank: pe_norm_sum(pe, w, bank))
                    w.norms += 1
                else:
                    pe_column_layer(pe, w, 2 * tiles)
                mids = w.mids
                for side in range(2):
                    pe_square_half(pe, w, tiles, lambda k: (mid_hi[:, k, :], mid_lo[:, k, :]),
                                   lambda k: pe.wait_ge(s_mlo, mids + k + 1))
                w.mids += tiles

        def act_ffn(act, w, eps, gain, load_p=None):
            for half, tiles in enumerate(HALVES):
                n0, b0, g = w.column_layer(2 * tiles)
                if half == 0:
                    act_rstd(act, w, 4 * (g ^ 1), eps)
                    if load_p is not None:
                        act.dma_start(p_f[:, :, :], p_t[load_p].rearrange("(k p) t -> p k t", p=P)).then_inc(s_p, 16)
                mids, gated = w.mids, w.gated

                def body(i, j):
                    act_ahead(act, n0, i, j)
                    pair, done = j // 2 % 2, i * 2 + j // 2
                    if j % 2 == 0:
                        act.wait_ge(s_free, i * 4 + (b0 + j + 5))
                        nc.scalar.activation(ff_gate[:, pair, :], ff_gate[:, pair, :], ACT.Silu).then_inc(s_act1, 1)
                    else:
                        act.wait_ge(s_prod, gated + done + 1)
                        nc.scalar.activation(tile_at(mid_hi, done), ff_up[:, pair, :], ACT.Copy).then_inc(s_mhi, 1)

                each(act, 2 * tiles, body, first=1)
                w.mids += tiles
                w.gated += tiles
                for side in range(2):
                    layer = w.square_layer(tiles // 2)
                    for kp in range(tiles // 2):
                        act_ahead(act, layer[0], 0, kp)
                    if half == 1:
                        act_prep(act, w, range(4 * side, 4 * side + 4), gain,
                                 lambda m: act.wait_ge(s_free, layer[1] + m % 4 + 5))

        def dve_ffn(dve, w, scale, gain):
            for half, tiles in enumerate(HALVES):
                n0, b0, g = w.column_layer(2 * tiles)
                if half == 0:
                    dve.wait_ge(s_rstd, w.norms + 1)
                    w.norms += 1
                mids, gated = w.mids, w.gated

                def body(i, j):
                    u, pair, done = i * 4 + j, j // 2 % 2, i * 2 + j // 2
                    dve.wait_ge(s_used, n0 + u + 1)
                    if j % 2 == 0:
                        nc.vector.tensor_tensor(ff_gate[:, pair, :], ps[:, 4 * g + j % 4, :], rstd[:, :], ALU.mult).then_inc(s_free, 1)
                    else:
                        nc.vector.tensor_tensor(ff_up[:, pair, :], ps[:, 4 * g + j % 4, :], rstd[:, :], ALU.mult).then_inc(s_free, 1)
                        dve.wait_ge(s_act1, gated + done + 1)
                        dve.wait_ge(s_free, b0 + u + 5)
                        nc.vector.tensor_tensor(ff_up[:, pair, :], ff_up[:, pair, :], ff_gate[:, pair, :], ALU.mult).then_inc(s_prod, 1)
                        dve.wait_ge(s_mhi, mids + done + 1)
                        nc.vector.tensor_tensor(tile_at(mid_lo, done), ff_up[:, pair, :], tile_at(mid_hi, done).bitcast(F32),
                                                ALU.subtract).then_inc(s_mlo, 1)

                each(dve, 2 * tiles, body)
                w.mids += tiles
                w.gated += tiles
                for side in range(2):
                    dve_add_to_h(dve, w, tiles // 2, side, scale, gain, half == 1)

        def dve_add_to_h(dve, w, units_, side, scale, gain, prep=True):
            layer = w.square_layer(units_)
            for m in range(4):
                wait_square(dve, layer, units_, m)
                t = 4 * side + m
                nc.vector.scalar_tensor_tensor(out=h[:, t, :], in0=ps[:, 4 * layer[2] + m, :], scalar=scale, in1=h[:, t, :],
                                               op0=ALU.mult, op1=ALU.add).then_inc(s_free, 1)
                if prep and m:
                    dve_prep(dve, w, [t - 1], gain)
            if prep:
                dve_prep(dve, w, [4 * side + 3], gain)


        U_DT, U_XBC, U_Z, U_END = 8, 9, 21, 29
        s_conv = sem("conv_ready")
        s_convact = sem("conv_activated")
        s_zact = sem("z_activated")
        s_rcolp = sem("rstd_columns_in_psum")
        s_rcol = sem("rstd_columns")
        s_toep = sem("bias_table_loaded")
        s_toepm = sem("bias_table_masked")
        s_stage = sem("staged")
        s_scores = sem("scores_ready")
        s_sfree = sem("scores_taken")
        s_max = sem("max_ready")
        s_exp = sem("exp_ready")
        s_pn = sem("probs_ready")
        s_ptp = sem("probs_transposed")
        s_pt = sem("probs_t_ready")
        s_o = sem("att_out_ready")
        s_dt = sem("dt_steps")
        s_cbp = sem("cb_in_psum")
        s_cb = sem("cb_diag_ready")
        s_cb2 = sem("cb_rest_ready")
        s_xtp = sem("x_transposed")
        s_xt = sem("x_tok_ready")
        s_colp = sem("columns_in_psum")
        s_col = sem("columns_ready")
        s_totp = sem("totals_in_psum")
        s_bias = sem("decay_biases_ready")
        s_sel = sem("selector_ready")
        s_csb = sem("cumsum_broadcast")
        s_dec = sem("decay_ready")
        s_m = sem("decayed_cb_ready")
        s_y = sem("y_ready")
        s_yg = sem("y_gated")
        s_ysq = sem("y_square_ready")
        s_ysum = sem("y_squares_summed")
        s_ymsum = sem("y_sum_in_psum")
        s_yrstd = sem("y_rstd_ready")
        s_yn = sem("y_normed")
        rcol = place("rcol", 144 * KB + 1248, [P, NB])

        OFF = {0: 4, 1: 8, 2: 7}

        def pairs():
            return [(0, 0), (0, 1), (0, 2), (0, 3), (1, 1), (1, 2), (1, 3), (3, 3), (2, 2), (2, 3)]

        PAIR = {p_: n_ for n_, p_ in enumerate(pairs())}

        def score_row(j, ib):
            at = ib * (ib + 1) // 2
            return at_s[:, j, at:at + ib + 1, :].rearrange("p a t -> p (a t)")

        def pe_rstd_columns(pe, w):
            bank = 4 * w.group + 3
            pe.wait_ge(s_rstd, w.norms)
            pe.wait_ge(s_free, w.prev_bank + 4)
            for m in range(NB):
                last = nc.tensor.matmul(ps[:, bank, m:m + 1], rstd[:, m * P:(m + 1) * P], ident[:, 0:1], start=True, stop=True)
            last.then_inc(s_rcolp, 1)

        def dve_rstd_columns(dve, w, n_):
            dve.wait_ge(s_rcolp, n_)
            nc.vector.tensor_copy(rcol[:, :], ps[:, 4 * w.group + 3, 0:NB]).then_inc(s_rcol, 1)

        def dve_tokens_out(dve, w, dest):
            layer = w.square_layer(4)
            for m in range(NB):
                wait_square(dve, layer, 4, m)
                nc.vector.tensor_scalar(dest[:, m, :], ps[:, 4 * layer[2] + m, :], rcol[:, m:m + 1], None, ALU.mult).then_inc(s_free, 1)

        def dve_conv(dve, ch, at, count, pad, cv, w_name, b_name, first_unit, convs):
            n0, b0, g = at
            wc = COL[w_name][0]
            with ch.loop(count // 4, 12) as i:
                for j in range(first_unit, first_unit + 4):
                    slot = (j - first_unit) % 2
                    t = j - first_unit
                    dve.wait_ge(s_used, i * 4 + (n0 + j + 1))
                    nc.vector.tensor_tensor(pad[:, slot, 3:3 + T], ps[:, 4 * g + j % 4, :], rstd[:, :], ALU.mult).then_inc(s_free, 1)
                    dve.wait_ge(s_free, i * 4 + (b0 + j + 5))
                    dve.wait_ge(s_convact, i * 4 + (convs + max(t, 1)))
                    tap = lambda q: col_at(vec, i * 16 + (wc + 4 * t + q))
                    if b_name:
                        ch.link(nc.vector.tensor_scalar(cv[:, slot, :], pad[:, slot, 3:3 + T], tap(3), col_at(vec, i * 4 + (COL[b_name][0] + t)), ALU.mult, ALU.add))
                    else:
                        ch.link(nc.vector.tensor_scalar(cv[:, slot, :], pad[:, slot, 3:3 + T], tap(3), None, ALU.mult))
                    for q in (2, 1, 0):
                        last = nc.vector.scalar_tensor_tensor(out=cv[:, slot, :], in0=pad[:, slot, q:q + T], scalar=tap(q), in1=cv[:, slot, :],
                                                              op0=ALU.mult, op1=ALU.add)
                        if q:
                            ch.link(last)
                    last.then_inc(s_conv, 1)

        def pe_mixer1(pe, w):
            w.tiles += DK
            pe_column_layer(pe, w, U_END, lambda bank: pe_norm_sum(pe, w, bank))
            w.norms += 1
            pe_rstd_columns(pe, w)
            pe.wait_ge(s_rcol, 1)
            pe_square_tokens(pe, w)
            pe.wait_ge(s_free, w.bank + 4)
            with pe.Fori(0, 4) as i:
                pe.wait_ge(s_stage, i * 3 + 3)
                for j in range(2):
                    rows = slice(64 * j, 64 * j + 64)
                    if j == 0:
                        pe.wait_ge(s_sfree, i * 2 + 1)
                    else:
                        pe.wait_ge(s_sfree, i * 2 + 2)
                    for ib in range(NB):
                        last = nc.tensor.matmul(ps[:, ib, 0:(ib + 1) * P], at_q[rows, ib * P:(ib + 1) * P], at_k[rows, 0:(ib + 1) * P], start=True, stop=True)
                    last.then_inc(s_scores, 1)
                for j in range(2):
                    pe.wait_ge(s_pn, i * 2 + (j + 1))
                    pe.wait_ge(s_pt, i * 2 + (j + 1))
                    for n_, (a, ib) in enumerate(pairs()):
                        last = nc.tensor.transpose(ps[:, 4 + n_ // 4, n_ % 4 * P:(n_ % 4 + 1) * P], at_s[:, j, ib * (ib + 1) // 2 + a, :], ident)
                    last.then_inc(s_ptp, 1)
                    pe.wait_ge(s_pt, i * 2 + (j + 2))
                    if j == 0:
                        pe.wait_ge(s_mlo, i + w.mids)
                    for a in range(NB):
                        first = PAIR[a, a]
                        last = nc.tensor.matmul(ps[64 * j:64 * j + 64, 7, a * P:T], at_v[:, a, 64 * j:64 * j + 64],
                                                at_pt[:, j, first:first + NB - a, :], start=(a == 0), stop=(a == NB - 1))
                    last.then_inc(s_o, 1)
            w.mids += 4
            pe.wait_ge(s_dt, 1)
            pe.wait_ge(s_pt, 9)
            for m in range(NB):
                nc.tensor.transpose(ps[:, 4, m * 32:m * 32 + 16], cs_row[:, m * P:(m + 1) * P], ident[0:16, 0:16])
                last = nc.tensor.transpose(ps[:, 4, m * 32 + 16:m * 32 + 32], dt_row[:, m * P:(m + 1) * P], ident[0:16, 0:16])
            last.then_inc(s_colp, 1)
            for g in range(2):
                if g:
                    pe.wait_ge(s_cb, 1)
                    pe.wait_ge(s_cb2, 1)
                for m in range(NB):
                    b_block = bc[:, g, m * P:(m + 1) * P]
                    last = nc.tensor.matmul(ps[:, 0, m * P:(m + 1) * P], b_block, bc[:, 2 + g, m * P:(m + 1) * P], start=True, stop=True)
                    if m < NB - 1:
                        bk, at = divmod(OFF[m] * P, T)
                        last = nc.tensor.matmul(ps[:, bk, at:at + (NB - 1 - m) * P], b_block, bc[:, 2 + g, (m + 1) * P:T], start=True, stop=True)
                last.then_inc(s_cbp, 1)
            pe.wait_ge(s_col, 1)
            nc.tensor.matmul(ps[:, 4, 256:256 + NB * 16], ident[:, P - 1:P].to_broadcast([P, P]), cols1[:, :, 0, :], start=True, stop=True).then_inc(s_totp, 1)
            for n_ in range(8):
                m, half = n_ // 2, n_ % 2
                if n_ >= 2:
                    pe.wait_ge(s_xt, n_ - 1)
                for t in range(4):
                    last = nc.tensor.transpose(ps[:, 5 + n_ % 2, t * P:(t + 1) * P], xs[:, 4 * half + t, m * P:(m + 1) * P], ident)
                last.then_inc(s_xtp, 1)

            def broadcast(i, t):
                pe.wait_ge(s_sel, i * 2 + (t + 1))
                if t >= 2:
                    pe.wait_ge(s_dec, i * 2 + (t - 1))
                nc.tensor.matmul(ps[:, t % 2, :], sel1[:, t % 2, :], cs_row[:, :], start=True, stop=True).then_inc(s_csb, 1)

            def y_head(i, t):
                j = t % 2
                pe.wait_ge(s_m, i * 2 + (t + 1))
                if j == 0:
                    pe.wait_ge(s_yg, i + 1)
                for a in range(NB):
                    last = nc.tensor.matmul(ps[64 * j:64 * j + 64, 2, a * P:(a + 1) * P], xdt[:, j, a, :], decay[:, j, a, :],
                                            start=(a == 0), stop=(a == NB - 1), skip_group_check=True)
                    if a < NB - 1:
                        nc.tensor.matmul(ps[64 * j:64 * j + 64, 2, (a + 1) * P:T], xdt[:, j, a, :], decay[:, j, OFF[a]:OFF[a] + NB - 1 - a, :],
                                         start=False, stop=False, skip_group_check=True)
                last.then_inc(s_y, 1)

            pe.wait_ge(s_cb, 2)
            pe.wait_ge(s_cb2, 2)
            broadcast(0, 0)
            broadcast(0, 1)
            with pe.Fori(0, 7) as i:
                y_head(i, 0)
                broadcast(i, 2)
                y_head(i, 1)
                broadcast(i, 3)
            y_head(7, 0)
            y_head(7, 1)
            pe.wait_ge(s_ysum, 8)
            nc.tensor.matmul(ps[:, 4 * (w.group ^ 1) + 3, :], ones, sum_sq[:, :], start=True, stop=True).then_inc(s_ymsum, 1)
            mids = w.mids - 4
            for side in range(2):
                pe_square_half(pe, w, 12, lambda k: (mid_hi[:, (k + 8) % 12, :], mid_lo[:, (k + 8) % 12, :]),
                               lambda k: pe.wait_ge(s_mlo, mids + k + 1))
            w.mids += 8

        def act_mixer1(act, w, gain):
            n0, b0, g = w.column_layer(U_END)
            act_ahead(act, n0, 0, 0)
            act_rstd(act, w, 4 * (g ^ 1), EPS_1)
            each(act, U_XBC - 1, lambda i, j: act_ahead(act, n0, i, j), begin=1)

            def conv_tile(dest, t0):
                def body(i, j):
                    act_ahead(act, n0, i, j)
                    act.wait_ge(s_conv, i * 4 + (j - U_XBC + 1))
                    nc.scalar.activation(tile_at(dest, i * 4 + (j - U_XBC - t0)), cv1[:, (j - U_XBC) % 2, :], ACT.Silu).then_inc(s_convact, 1)
                return body

            each(act, 8, conv_tile(xs, 0), begin=U_XBC)
            each(act, 4, conv_tile(bc, 8), begin=U_XBC + 8)

            def z_tile(i, j):
                act_ahead(act, n0, i, j)
                act.wait_ge(s_free, i * 4 + (b0 + j + 5))
                nc.scalar.activation(tile_at(zs, i * 4 + (j - U_Z)), z_tmp[:, (j - U_Z) % 2, :], ACT.Silu).then_inc(s_zact, 1)

            each(act, 8, z_tile, begin=U_Z)
            act.wait_ge(s_zact, 9)
            act.dma_start(toep[:, :, :], rel_table[:, :, :]).then_inc(s_toep, 16)
            layer = w.square_layer(4)
            for kp in range(4):
                act_ahead(act, layer[0], 0, kp)
            ch = Chain(act, s_act)
            w.act_steps = ch
            act.wait_ge(s_dtb, 1)
            ch.link(nc.scalar.activation(dt_abs[:, :], dt_raw[:, :], ACT.Abs))
            ch.link(nc.scalar.activation(dt_abs[:, :], dt_abs[:, :], ACT.Exp, scale=-1.0))
            ch.step(nc.scalar.activation(dt_abs[:, :], dt_abs[:, :], ACT.Ln, bias=1.0))
            ch.step(nc.scalar.activation(a_neg[:, :], vec[0:SSD_HEADS, COL["a_log"][0]:COL["a_log"][0] + 1], ACT.Exp))
            mids = w.mids
            with act.Fori(0, 4) as i:
                for j in range(2):
                    act.wait_ge(s_max, i * 2 + (j + 1))
                    for ib in range(NB):
                        last = nc.scalar.activation(score_row(j, ib), score_row(j, ib), ACT.Exp,
                                                    bias=at_stat[:, j, 0, ib:ib + 1], accum_out=at_stat[:, j, 1, ib:ib + 1])
                    last.then_inc(s_exp, 1)
                for j in range(2):
                    act.wait_ge(s_ptp, i * 2 + (j + 2))
                    for n_, width in ((0, 4), (1, 4), (2, 2)):
                        last = nc.scalar.activation(at_pt[:, j, 4 * n_:4 * n_ + width, :].rearrange("p a t -> p (a t)"),
                                                    ps[:, 4 + n_, 0:width * P], ACT.Copy)
                    last.then_inc(s_pt, 1)
                act.wait_ge(s_o, i * 2 + 3)
                nc.scalar.activation(tile_at(mid_hi, i + 8), ps[:, 7, :], ACT.Copy).then_inc(s_mhi, 1)
            w.mids += 4
            for g in range(2):
                act.wait_ge(s_cbp, g + 1)
                nc.scalar.activation(cb[:, g, NB:10, :].rearrange("p a t -> p (a t)"),
                                     ps[:, 1:3, :].rearrange("p a t -> p (a t)")[:, 0:6 * P], ACT.Copy).then_inc(s_cb2, 1)
            for n_ in range(8):
                act.wait_ge(s_xtp, n_ + 1)
                nc.scalar.activation(x_tok[:, n_ // 2, n_ % 2 * T:(n_ % 2 + 1) * T], ps[:, 5 + n_ % 2, :], ACT.Copy).then_inc(s_xt, 1)
            act.wait_ge(s_bias, 1)

            def decays(i, t):
                act.wait_ge(s_csb, i * 2 + (t + 1))
                if t >= 2:
                    act.wait_ge(s_y, i * 2 + t)
                head = slice(t, t + 1) if isinstance(i, int) else bass.ds(i * 2 + t, 1)
                j = t % 2
                for a in range(NB):
                    last = nc.scalar.activation(decay[:, j, a, :], ps[:, j, a * P:(a + 1) * P], ACT.Relu, bias=cols1[:, a, 0, head], scale=-1.0)
                ch.step(last)
                for a in range(NB - 1):
                    for ib in range(a + 1, NB):
                        last = nc.scalar.activation(decay[:, j, OFF[a] + ib - a - 1, :], ps[:, j, ib * P:(ib + 1) * P], ACT.Exp,
                                                    bias=bias_c[:, PAIR[a, ib], head])
                ch.wait()
                diag = decay[:, j, 0:NB, :].rearrange("p a t -> p (a t)")
                last = nc.scalar.activation(diag, diag, ACT.Exp, scale=-1.0)
                last.then_inc(s_dec, 1)

            decays(0, 0)
            decays(0, 1)
            with ch.loop(7, 2) as i:
                decays(i, 2)
                decays(i, 3)
            for m in range(8):
                act.wait_ge(s_yg, m + 2)
                if m >= 2:
                    act.wait_ge(s_ysum, m - 1)
                nc.scalar.activation(sq[:, m % 2, :], zs[:, m, :], ACT.Square).then_inc(s_ysq, 1)
            act.wait_ge(s_ymsum, 1)
            ch.link(nc.scalar.activation(rstd[:, :], ps[:, 4 * (w.group ^ 1) + 3, :], ACT.Ln, bias=EPS_1, scale=1.0 / D))
            nc.scalar.activation(rstd[:, :], rstd[:, :], ACT.Exp, scale=-0.5).then_inc(s_yrstd, 1)
            for m in range(8):
                act.wait_ge(s_yn, m + 1)
                nc.scalar.activation(mid_hi[:, m, :], zs[:, m, :], ACT.Copy).then_inc(s_mhi, 1)
            w.mids += 8
            for side in range(2):
                layer = w.square_layer(6)
                for kp in range(6):
                    act_ahead(act, layer[0], 0, kp)
                act_prep(act, w, range(4 * side, 4 * side + 4), gain, lambda m: act.wait_ge(s_free, layer[1] + m % 4 + 5))

        s_dtb = sem("dt_biased")

        def dve_mixer1(dve, w, ch, gain):
            n0, b0, g = w.column_layer(U_END)
            dve.wait_ge(s_rstd, w.norms + 1)
            w.norms += 1
            ch.step(nc.vector.memset(pad1[:, :, 0:3], 0.0))

            def qk_tile(i, j):
                dve.wait_ge(s_used, i * 4 + (n0 + j + 1))
                nc.vector.tensor_tensor(tile_at(qk, i * 4 + j), ps[:, 4 * g + j % 4, :], rstd[:, :], ALU.mult).then_inc(s_free, 1)

            each(dve, 8, qk_tile)
            dve.wait_ge(s_used, n0 + U_DT + 1)
            nc.vector.tensor_tensor(dt_raw[:, :], ps[0:SSD_HEADS, 4 * g, :], rstd[0:SSD_HEADS, :], ALU.mult).then_inc(s_free, 1)
            dve.wait_ge(s_free, b0 + U_DT + 5)
            nc.vector.tensor_scalar(dt_raw[:, :], dt_raw[:, :], vec[0:SSD_HEADS, COL["dt_bias"][0]:COL["dt_bias"][0] + 1], None, ALU.add).then_inc(s_dtb, 1)
            dve.wait_ge(s_dtb, 1)

            dve_conv(dve, ch, (n0, b0, g), 12, pad1, cv1, "conv_w", "conv_b", U_XBC, 0)

            def z_tile(i, j):
                dve.wait_ge(s_used, i * 4 + (n0 + j + 1))
                if j - U_Z >= 2:
                    dve.wait_ge(s_zact, i * 4 + (j - U_Z))
                else:
                    dve.wait_ge(s_zact, i * 4 + 1)
                nc.vector.tensor_tensor(z_tmp[:, (j - U_Z) % 2, :], ps[:, 4 * g + j % 4, :], rstd[:, :], ALU.mult).then_inc(s_free, 1)

            each(dve, 8, z_tile, begin=U_Z)
            dve_rstd_columns(dve, w, 1)
            dve.wait_ge(s_rcol, 1)
            dve_tokens_out(dve, w, v_tok)
            dve.wait_ge(s_act, 4)
            ch.link(nc.vector.scalar_tensor_tensor(out=dt_row[:, :], in0=dt_raw[:, :], scalar=0.0, in1=dt_abs[:, :], op0=ALU.max, op1=ALU.add))
            ch.link(nc.vector.tensor_scalar(da_row[:, :], dt_row[:, :], a_neg[:, 0:1], -1.0, ALU.mult, ALU.mult))
            for m in range(NB):
                cols = slice(m * P, (m + 1) * P)
                last = nc.vector.tensor_tensor_scan(cs_row[:, cols], ones[0:SSD_HEADS, :], da_row[:, cols], 0.0, ALU.mult, ALU.add)
            last.then_inc(s_dt, 1)
            dve.wait_ge(s_toepm, 1)
            mids = w.mids
            with ch.loop(4, 4) as i:
                for j in range(2):
                    dve.wait_ge(s_scores, i * 2 + (j + 1))
                    dve.wait_ge(s_ptp, i * 2 + 1)
                    for ib in range(NB):
                        width = (ib + 1) * P
                        table = toep[:, bass.ds(i * 2 + j, 1), T - width:T].rearrange("p a t -> p (a t)")
                        last = nc.vector.scalar_tensor_tensor(out=score_row(j, ib), in0=ps[:, ib, 0:width], scalar=ATT_DIM ** -0.5,
                                                              in1=table, op0=ALU.mult, op1=ALU.add)
                    last.then_inc(s_sfree, 1)
                    dve.wait_ge(s_sfree, i * 2 + (j + 2))
                    for ib in range(NB):
                        last = nc.vector.tensor_reduce(at_stat[:, j, 1, ib:ib + 1], score_row(j, ib), AX.X, ALU.max)
                    ch.link(last)
                    nc.vector.tensor_scalar(at_stat[:, j, 0, :], at_stat[:, j, 1, :], -1.0, None, ALU.mult).then_inc(s_max, 1)
                for j in range(2):
                    dve.wait_ge(s_exp, i * 2 + (j + 1))
                    ch.link(nc.vector.reciprocal(at_stat[:, j, 2, :], at_stat[:, j, 1, :]))
                    for ib in range(NB):
                        last = nc.vector.tensor_scalar(score_row(j, ib), score_row(j, ib), at_stat[:, j, 2, ib:ib + 1], None, ALU.mult)
                    last.then_inc(s_pn, 1)
                dve.wait_ge(s_mhi, i + (mids + 1))
                nc.vector.tensor_tensor(tile_at(mid_lo, i + 8), ps[:, 7, :], tile_at(mid_hi, i + 8).bitcast(F32), ALU.subtract).then_inc(s_mlo, 1)
            w.mids += 4
            dve.wait_ge(s_colp, 1)
            nc.vector.tensor_copy(cols1[:, :, :, :].rearrange("p a b c -> p (a b c)"), ps[:, 4, 0:NB * 32]).then_inc(s_col, 1)
            for g_ in range(2):
                dve.wait_ge(s_cbp, g_ + 1)
                nc.vector.tensor_tensor(cb[:, g_, 0:NB, :], ps[:, 0, :].rearrange("p (a t) -> p a t", a=NB),
                                        mask["upper"].rearrange("p (a t) -> p a t", a=1).to_broadcast([P, NB, P]), ALU.mult).then_inc(s_cb, 1)
            dve.wait_ge(s_totp, 1)
            ch.link(nc.vector.tensor_copy(total_c[:, :, :].rearrange("p a c -> p (a c)"), ps[:, 4, 256:256 + NB * 16]))
            for a in range(NB):
                last = nc.vector.tensor_scalar(bias_c[:, PAIR[a, a], :], cols1[:, a, 0, :], -1.0, None, ALU.mult)
                if a < NB - 1:
                    ch.link(last)
                for ib in range(a + 1, NB):
                    ch.link(nc.vector.tensor_tensor(bias_c[:, PAIR[a, ib], :], bias_c[:, PAIR[a, ib - 1], :], total_c[:, ib - 1, :], ALU.add))
            last.then_inc(s_bias, 1)
            dve.wait_ge(s_xt, 8)
            dve.wait_ge(s_cb2, 2)

            def select(i, t):
                if t >= 2:
                    dve.wait_ge(s_csb, i * 2 + (t - 1))
                src = ident[0:16, 2 * i + t:2 * i + t + 1] if isinstance(i, int) else const[0:16, 0, bass.ds(i * 2 + t, 1)]
                nc.vector.tensor_copy(sel1[:, t % 2, :], src.to_broadcast([16, P])).then_inc(s_sel, 1)

            def head(i, t, g_, hd, tt):
                j = t % 2
                if tt >= 2:
                    dve.wait_ge(s_y, i * 2 + tt)
                else:
                    dve.wait_ge(s_y, i * 2 + 1)
                ch.step(nc.vector.tensor_tensor(xdt[:, j, :, :], x_tok[:, :, bass.ds(hd * 64, 64)],
                                                cols1[:, :, 1, bass.ds(hd, 1)].to_broadcast([P, NB, SSD_DIM]), ALU.mult))
                dve.wait_ge(s_dec, i * 2 + (tt + 1))
                last = nc.vector.tensor_tensor(decay[:, j, :, :], decay[:, j, :, :], cb[:, g_, :, :], ALU.mult)
                last.then_inc(s_m, 1)

            select(0, 0)
            select(0, 1)
            skip = COL["d_skip"][0]
            for g_ in range(2):
                with ch.loop(4, 3) as i:
                    for j in range(2):
                        tt = 8 * g_ + j
                        head(i, j, g_, i * 2 + tt, tt)
                        dve.wait_ge(s_csb, i * 2 + (tt + 1))
                        nc.vector.tensor_copy(sel1[:, j, :], const[0:16, 0, bass.ds(i * 2 + (tt + 2), 1)].to_broadcast([16, P])).then_inc(s_sel, 1)
                    m = i + 4 * g_
                    dve.wait_ge(s_y, i * 2 + (8 * g_ + 3))
                    ch.link(nc.vector.scalar_tensor_tensor(out=y_tmp[:, 0, :], in0=tile_at(xs, m), scalar=col_at(vec, m + skip), in1=ps[:, 2, :],
                                                           op0=ALU.mult, op1=ALU.add))
                    nc.vector.tensor_tensor(tile_at(zs, m), y_tmp[:, 0, :], tile_at(zs, m), ALU.mult).then_inc(s_yg, 1)
            for m in range(8):
                dve.wait_ge(s_ysq, m + 1)
                if m == 0:
                    nc.vector.tensor_copy(sum_sq[:, :], sq[:, 0, :]).then_inc(s_ysum, 1)
                else:
                    dve.wait_ge(s_ysum, m)
                    nc.vector.tensor_tensor(sum_sq[:, :], sum_sq[:, :], sq[:, m % 2, :], ALU.add).then_inc(s_ysum, 1)
            dve.wait_ge(s_yrstd, 1)
            c = COL["ssd_norm"][0]
            for m in range(8):
                nc.vector.scalar_tensor_tensor(out=zs[:, m, :], in0=zs[:, m, :], scalar=vec[:, c + m:c + m + 1], in1=rstd[:, :],
                                               op0=ALU.mult, op1=ALU.mult).then_inc(s_yn, 1)
                if m:
                    dve_lo_y(dve, w, m - 1, zs)
            dve_lo_y(dve, w, 7, zs)
            for side in range(2):
                dve_add_to_h(dve, w, 6, side, 1.0, gain)

        def dve_lo_y(dve, w, m, src):
            dve.wait_ge(s_mhi, w.mids + 1)
            nc.vector.tensor_tensor(mid_lo[:, m, :], src[:, m, :], mid_hi[:, m, :].bitcast(F32), ALU.subtract).then_inc(s_mlo, 1)
            w.mids += 1

        def pool_mixer1(pool, w):
            pool.wait_ge(s_toep, 16)
            nc.gpsimd.memset(toep[0:64, :, T - 64:T], MASKED).then_inc(s_toepm, 1)
            pool.wait_ge(s_free, w.bank + 4)
            with pool.Fori(0, 4) as i:
                pool.wait_ge(s_o, i * 2 + 1)
                pool.sem_inc(s_tick["pool"], 1)
                nc.gpsimd.tensor_copy(at_q[:, :], tile_at(qk, i)).then_inc(s_stage, 1)
                nc.gpsimd.tensor_copy(at_k[:, :], tile_at(qk, i + 4)).then_inc(s_stage, 1)
                nc.gpsimd.tensor_copy(at_v[:, :, :], v_tok[:, :, bass.ds(i * 128, 128)]).then_inc(s_stage, 1)

        s_tsq = sem("tile_squares")
        s_tsum = sem("tile_sums")
        s_tln = sem("tile_log_variances")
        s_trs = sem("tile_rstds")
        s_tn = sem("tiles_normed")

        def pe_tile_norm(pe, w, count):
            c = w.tile_norms
            with pe.Fori(0, count // 2) as i:
                for s in range(2):
                    pe.wait_ge(s_tsq, i * 2 + (c + s + 1))
                    pe.wait_ge(s_tln, i * 2 + max(c + s, 1))
                    nc.tensor.matmul(ps[:, s, :], ones, nrm[:, 0, s, :], start=True, stop=True).then_inc(s_tsum, 1)
            w.tile_norms += count

        def act_tile_norm(act, w, src, t0, count, scale, bias):
            c = w.tile_norms
            with act.Fori(0, count // 2) as i:
                for s in range(2):
                    act.wait_ge(s_tsum, i * 2 + (c + 1))
                    nc.scalar.activation(nrm[:, 0, s, :], tile_at(src, i * 2 + (t0 + s)), ACT.Square).then_inc(s_tsq, 1)
                for s in range(2):
                    act.wait_ge(s_tsum, i * 2 + (c + s + 2))
                    act.wait_ge(s_tn, i * 2 + (c + 1))
                    nc.scalar.activation(nrm[:, 1, s, :], ps[:, s, :], ACT.Ln, bias=bias, scale=scale).then_inc(s_tln, 1)
                for s in range(2):
                    act.wait_ge(s_tln, i * 2 + (c + s + 2))
                    nc.scalar.activation(nrm[:, 1, s, :], nrm[:, 1, s, :], ACT.Exp, scale=-0.5).then_inc(s_trs, 1)
            w.tile_norms += count

        def dve_tile_norm(dve, w, ch, src, t0, count, gain=None, factor=None):
            c = w.tile_norms
            with ch.loop(count // 2, 2 if factor is not None else 0) as i:
                for s in range(2):
                    tile = tile_at(src, i * 2 + (t0 + s))
                    dve.wait_ge(s_trs, i * 2 + (c + s + 1))
                    if gain is None:
                        last = nc.vector.tensor_tensor(tile, tile, nrm[:, 1, s, :], ALU.mult)
                    else:
                        last = nc.vector.scalar_tensor_tensor(out=tile, in0=tile, scalar=vec[:, COL[gain][0]:COL[gain][0] + 1],
                                                              in1=nrm[:, 1, s, :], op0=ALU.mult, op1=ALU.mult)
                    if factor is not None:
                        ch.link(last)
                        last = nc.vector.tensor_tensor(tile, tile, tile_at(factor, i * 2 + (t0 + s)), ALU.mult)
                    last.then_inc(s_tn, 1)
            w.tile_norms += count

        U_AB, U_GATE, U_END2 = 24, 25, 33
        s_ga = sem("decay_inputs_biased")
        s_ga2 = sem("decay_and_beta_rows")
        s_gateact = sem("gate2_activated")
        s_gcolp = sem("gdn_columns_in_psum")
        s_gcol = sem("gdn_columns")
        s_gtot = sem("gdn_totals_in_psum")
        s_gcd = sem("gdn_log_columns")
        s_gce = sem("gdn_exp_columns")
        s_gcb = sem("gdn_all_columns")
        s_gst = sem("gdn_staged")
        s_gsel = sem("gdn_selectors")
        s_gbc = sem("gdn_broadcasts")
        s_gem = sem("gdn_decays")
        s_gkb = sem("gdn_beta_k")
        s_gmm = sem("gdn_products")
        s_gin = sem("gdn_inputs_ready")
        s_gtt = sem("gdn_first_inverse_t")
        s_gtmp = sem("gdn_first_inverse_in_psum")
        s_gtm = sem("gdn_first_inverse")
        s_gao = sem("gdn_off_blocks")
        s_gup = sem("gdn_u_in_psum")
        s_gu = sem("gdn_u")
        s_gdp = sem("gdn_update_in_psum")
        s_gd = sem("gdn_inverse_updated")
        s_guw = sem("gdn_uw_in_psum")
        s_guwc = sem("gdn_uw")
        s_gva = sem("gdn_w_state")
        s_gvn = sem("gdn_v_new")
        s_gop = sem("gdn_state_update_in_psum")
        s_gs = sem("gdn_state")
        s_gop2 = sem("gdn_out_in_psum")
        s_go = sem("gdn_out")

        def pe_mixer2(pe, w):
            w.tiles += DK
            pe_column_layer(pe, w, U_END2, lambda bank: pe_norm_sum(pe, w, bank))
            w.norms += 1
            pe.wait_ge(s_free, w.bank + 4)
            pe_tile_norm(pe, w, 16)
            pe.wait_ge(s_ga2, 2)
            pe.wait_ge(s_tln, w.tile_norms + 1)
            for m in range(NB):
                last = nc.tensor.transpose(ps[:, 0, m * 64:m * 64 + 40], g_row[:, m * P:(m + 1) * P], ident[0:40, 0:40])
            last.then_inc(s_gcolp, 1)
            pe.wait_ge(s_gcol, 1)
            nc.tensor.matmul(ps[:, 1, 0:32], ident[:, P - 1:P].to_broadcast([P, P]), cols2[:, :, 0:8], start=True, stop=True).then_inc(s_gtot, 1)
            pe.wait_ge(s_gcb, 1)
            with pe.Fori(0, 4) as i:
                for j in range(2):
                    b = 4 * j
                    pe.wait_ge(s_gsel, i * 2 + (j + 1))
                    pe.wait_ge(s_go, i * 2 + 1)
                    nc.tensor.matmul(ps[:, b, :], gw["sel"][j][:, 0, :], g_row[:, :], start=True, stop=True)
                    nc.tensor.matmul(ps[:, b + 1, :], gw["sel"][j][:, 1, :], g_row[:, :], start=True, stop=True).then_inc(s_gbc, 1)
                for j in range(2):
                    b = 4 * j
                    pe.wait_ge(s_gst, i * 4 + (2 * j + 2))
                    for c in range(NB):
                        ks = gw["k_st"][j][:, c, :]
                        nc.tensor.matmul(ps[:, b + 2, c * P:(c + 1) * P], ks, qk2[:, bass.ds(i * 2 + j, 1), c * P:(c + 1) * P].rearrange("p a t -> p (a t)"), start=True, stop=True)
                        nc.tensor.transpose(ps[:, b + 3, c * P:(c + 1) * P], ks, ident)
                    pe.wait_ge(s_gem, i * 2 + (j + 1))
                    for c in range(NB):
                        nc.tensor.transpose(ps[:, b, c * P:(c + 1) * P], gw["uu"][j][:, c, :], ident)
                    pe.wait_ge(s_gkb, i * 2 + (j + 1))
                    for c in range(NB):
                        last = nc.tensor.matmul(ps[:, b + 1, c * P:(c + 1) * P], gw["k_st"][j][:, c, :], gw["ao"][j][:, c, :], start=True, stop=True)
                    last.then_inc(s_gmm, 1)
                for j in range(2):
                    pe.wait_ge(s_gtt, i * 2 + (j + 1))
                    for c in range(NB):
                        last = nc.tensor.transpose(ps[:, 4 * j, c * P:(c + 1) * P], gw["tt"][j][:, c, :], ident)
                    last.then_inc(s_gtmp, 1)
                for n_ in range(6):
                    for j in range(2):
                        b = 4 * j
                        pe.wait_ge(s_gao, i * 12 + (2 * n_ + j + 1))
                        if n_ == 0:
                            pe.wait_ge(s_gtm, i * 2 + (j + 1))
                        else:
                            pe.wait_ge(s_gd, i * 12 + (2 * n_ - 2 + j + 1))
                        for c in range(NB):
                            last = nc.tensor.matmul(ps[:, b + 1, c * P:(c + 1) * P], gw["ao"][j][:, c, :], gw["tm"][j][:, c, :], start=True, stop=True)
                        last.then_inc(s_gup, 1)
                    for j in range(2):
                        b = 4 * j
                        pe.wait_ge(s_gu, i * 12 + (2 * n_ + j + 1))
                        for c in range(NB):
                            cols = slice(c * P, (c + 1) * P)
                            if n_ < 5:
                                nc.tensor.matmul(ps[:, b + 2, cols], gw["tt"][j][:, c, :], gw["u_"][j][:, c, :], start=True, stop=True)
                            last = nc.tensor.matmul(ps[:, b + 3, cols], gw["u_"][j][:, c, :], gw["tt"][j][:, c, :], start=True, stop=True)
                        last.then_inc(s_gdp, 1)
                for j in range(2):
                    b = 4 * j
                    pe.wait_ge(s_gd, i * 12 + (10 + j + 1))
                    for c in range(NB):
                        cols = slice(c * P, (c + 1) * P)
                        nc.tensor.matmul(ps[:, b, cols], gw["tt"][j][:, c, :], gw["vb"][j][:, c, :], start=True, stop=True)
                        last = nc.tensor.matmul(ps[:, b + 1, cols], gw["kb"][j][:, c, :], gw["tt"][j][:, c, :], start=True, stop=True)
                    last.then_inc(s_guw, 1)
                for c in range(NB):
                    cols = slice(c * P, (c + 1) * P)
                    for j in range(2):
                        b = 4 * j
                        if c == 0:
                            pe.wait_ge(s_guwc, i * 2 + (j + 1))
                        else:
                            pe.wait_ge(s_gs, i * 6 + (2 * (c - 1) + j + 1))
                            nc.tensor.matmul(ps[:, b + 2, 0:P], gw["wt"][j][:, c, :], gw["st"][j][:, :], start=True, stop=True).then_inc(s_gva, 1)
                    for j in range(2):
                        b = 4 * j
                        vn = gw["vn"][j][:, :]
                        if c == 0:
                            vn = gw["uu"][j][:, 0, :]
                            last = nc.tensor.matmul(ps[:, b + 3, cols], vn, gw["qkt"][j][:, c, :], start=True, stop=True)
                        else:
                            nc.tensor.matmul(ps[:, b + 3, cols], gw["st"][j][:, :], gw["qd"][j][:, c, :], start=True, stop=False)
                            pe.wait_ge(s_gvn, i * 6 + (2 * (c - 1) + j + 1))
                            last = nc.tensor.matmul(ps[:, b + 3, cols], vn, gw["qkt"][j][:, c, :], start=False, stop=True)
                        if c < NB - 1:
                            nc.tensor.matmul(ps[:, b + 2, P:2 * P], gw["kd"][j][:, c, :], vn, start=True, stop=True).then_inc(s_gop, 1)
                        else:
                            last.then_inc(s_gop2, 1)
            pe.wait_ge(s_go, 9)
            pe_tile_norm(pe, w, 8)
            mids = w.mids
            for side in range(2):
                pe_square_half(pe, w, 8, lambda k: (mid_hi[:, k, :], mid_lo[:, k, :]), lambda k: pe.wait_ge(s_mlo, mids + k + 1))
            w.mids += 8

        def act_mixer2(act, w, gain):
            n0, b0, g = w.column_layer(U_END2)
            act_ahead(act, n0, 0, 0)
            act_rstd(act, w, 4 * (g ^ 1), EPS_2)

            def conv_tile(dest, t0):
                def body(i, j):
                    if j > 0:
                        act_ahead(act, n0, i, j)
                    act.wait_ge(s_conv, i * 4 + (12 + j + 1))
                    nc.scalar.activation(tile_at(dest, i * 4 + (j - t0)), cv2[:, j % 2, :], ACT.Silu).then_inc(s_convact, 1)
                return body

            each(act, 16, conv_tile(qk2, 0), first=4)
            each(act, 8, conv_tile(v2, 16), begin=16)
            act_ahead(act, n0, 0, U_AB)

            def gate_tile(i, j):
                act_ahead(act, n0, i, j)
                act.wait_ge(s_free, i * 4 + (b0 + j + 5))
                nc.scalar.activation(tile_at(gate2, i * 4 + (j - U_GATE)), g_tmp[:, (j - U_GATE) % 2, :], ACT.Silu).then_inc(s_gateact, 1)

            each(act, 8, gate_tile, begin=U_GATE)
            ch = w.act_steps
            act.wait_ge(s_ga, 1)
            ch.link(nc.scalar.activation(ga[0:8, 1, :], ga[0:8, 0, :], ACT.Abs))
            ch.link(nc.scalar.activation(ga[0:8, 1, :], ga[0:8, 1, :], ACT.Exp, scale=-1.0))
            ch.step(nc.scalar.activation(ga[0:8, 1, :], ga[0:8, 1, :], ACT.Ln, bias=1.0))
            ch.step(nc.scalar.activation(a_neg2[:, :], vec[0:8, COL["gdn_a_log"][0]:COL["gdn_a_log"][0] + 1], ACT.Exp))
            w.softplus2 = ch.n
            nc.scalar.activation(g_row[32:40, :], ga[32:40, 0, :], ACT.Sigmoid).then_inc(s_ga2, 1)
            act_tile_norm(act, w, qk2, 0, 8, 128.0, 128.0 * EPS_2)
            act_tile_norm(act, w, qk2, 8, 8, 1.0, EPS_2)
            act.wait_ge(s_gcd, 1)
            nc.scalar.activation(g_dec[:, :, :], g_dec[:, :, :], ACT.Exp).then_inc(s_gce, 1)
            nc.scalar.activation(g_exp[:, :, :], cols2[:, :, 0:8], ACT.Exp).then_inc(s_gce, 1)
            with ch.loop(4, 2) as i:
                for j in range(2):
                    act.wait_ge(s_gbc, i * 2 + (j + 1))
                    nc.scalar.activation(gw["eg"][j][:, :, :].rearrange("p a t -> p (a t)"), ps[:, 4 * j, :], ACT.Exp)
                    for c in range(NB):
                        last = nc.scalar.activation(gw["em"][j][:, c, :], ps[:, 4 * j, c * P:(c + 1) * P], ACT.Relu,
                                                    bias=cols2[:, c, bass.ds(i * 2 + j, 1)], scale=-1.0)
                    ch.link(last)
                    em = gw["em"][j][:, :, :].rearrange("p a t -> p (a t)")
                    nc.scalar.activation(em, em, ACT.Exp, scale=-1.0).then_inc(s_gem, 1)
                for j in range(2):
                    act.wait_ge(s_gtmp, i * 2 + (j + 1))
                    nc.scalar.activation(gw["tm"][j][:, :, :].rearrange("p a t -> p (a t)"), ps[:, 4 * j, :], ACT.Copy).then_inc(s_gtm, 1)
                for n_ in range(6):
                    for j in range(2):
                        act.wait_ge(s_gup, i * 12 + (2 * n_ + j + 1))
                        nc.scalar.activation(gw["u_"][j][:, :, :].rearrange("p a t -> p (a t)"), ps[:, 4 * j + 1, :], ACT.Copy).then_inc(s_gu, 1)
                for j in range(2):
                    act.wait_ge(s_guw, i * 2 + (j + 1))
                    nc.scalar.activation(gw["uu"][j][:, :, :].rearrange("p a t -> p (a t)"), ps[:, 4 * j, :], ACT.Copy)
                    nc.scalar.activation(gw["wt"][j][:, :, :].rearrange("p a t -> p (a t)"), ps[:, 4 * j + 1, :], ACT.Copy).then_inc(s_guwc, 1)
                for j in range(2):
                    act.wait_ge(s_gop2, i * 2 + (j + 1))
                    nc.scalar.activation(tile_at(v2, i * 2 + j), ps[:, 4 * j + 3, :], ACT.Copy).then_inc(s_go, 1)
            act.wait_ge(s_go, 9)
            act_tile_norm(act, w, v2, 0, 8, 1.0 / P, EPS_2)
            for m in range(8):
                act.wait_ge(s_tn, w.tile_norms - 8 + m + 2)
                nc.scalar.activation(mid_hi[:, m, :], v2[:, m, :], ACT.Copy).then_inc(s_mhi, 1)
            w.mids += 8
            for side in range(2):
                layer = w.square_layer(4)
                for kp in range(4):
                    act_ahead(act, layer[0], 0, kp)
                act_prep(act, w, range(4 * side, 4 * side + 4), gain, lambda m: act.wait_ge(s_free, layer[1] + m % 4 + 5))

        def dve_mixer2(dve, w, ch, gain):
            n0, b0, g = w.column_layer(U_END2)
            dve.wait_ge(s_rstd, w.norms + 1)
            w.norms += 1
            ch.step(nc.vector.memset(pad2[:, :, 0:3], 0.0))
            ch.step(nc.vector.memset(g_row[:, :], 0.0))
            dve_conv(dve, ch, (n0, b0, g), 24, pad2, cv2, "gdn_conv", None, 0, 12)
            dve.wait_ge(s_used, n0 + U_AB + 1)
            nc.vector.tensor_tensor(ga[:, 0, :], ps[0:40, 4 * g + U_AB % 4, :], rstd[0:40, :], ALU.mult).then_inc(s_free, 1)
            dve.wait_ge(s_free, b0 + U_AB + 5)
            nc.vector.tensor_scalar(ga[0:8, 0, :], ga[0:8, 0, :], vec[0:8, COL["gdn_dt_bias"][0]:COL["gdn_dt_bias"][0] + 1], None, ALU.add).then_inc(s_ga, 1)
            dve.wait_ge(s_ga, 1)

            def gate_tile(i, j):
                dve.wait_ge(s_used, i * 4 + (n0 + j + 1))
                dve.wait_ge(s_gateact, i * 4 + max(j - U_GATE, 1))
                nc.vector.tensor_tensor(g_tmp[:, (j - U_GATE) % 2, :], ps[:, 4 * g + j % 4, :], rstd[:, :], ALU.mult).then_inc(s_free, 1)

            each(dve, 8, gate_tile, begin=U_GATE)
            dve.wait_ge(s_act, 25)
            ch.link(nc.vector.scalar_tensor_tensor(out=ga[0:8, 2, :], in0=ga[0:8, 0, :], scalar=0.0, in1=ga[0:8, 1, :], op0=ALU.max, op1=ALU.add))
            ch.link(nc.vector.tensor_scalar(ga[0:8, 2, :], ga[0:8, 2, :], a_neg2[:, 0:1], -1.0, ALU.mult, ALU.mult))
            for m in range(NB):
                cols = slice(m * P, (m + 1) * P)
                last = nc.vector.tensor_tensor_scan(g_row[0:8, cols], ones[0:8, :], ga[0:8, 2, cols], 0.0, ALU.mult, ALU.add)
            last.then_inc(s_ga2, 1)
            dve_tile_norm(dve, w, ch, qk2, 0, 8)
            dve_tile_norm(dve, w, ch, qk2, 8, 8)
            dve.wait_ge(s_gcolp, 1)
            nc.vector.tensor_copy(cols2[:, :, :], ps[:, 0, 0:256].rearrange("p (a c) -> p a c", a=NB)[:, :, 0:40]).then_inc(s_gcol, 1)
            dve.wait_ge(s_gcol, 1)
            dve.wait_ge(s_gtot, 1)
            nc.vector.tensor_tensor(g_dec[:, :, :], ps[:, 1, 0:32].rearrange("p (a c) -> p a c", a=NB), cols2[:, :, 0:8], ALU.subtract).then_inc(s_gcd, 1)
            dve.wait_ge(s_gce, 2)
            nc.vector.tensor_tensor(g_exp[:, :, :], g_exp[:, :, :], cols2[:, :, 32:40], ALU.mult).then_inc(s_gcb, 1)
            dve.wait_ge(s_gcb, 1)
            wide = [P, NB, P]
            upper = mask["upper"].rearrange("p (a t) -> p a t", a=1).to_broadcast(wide)
            merge1 = mask["merge1"].rearrange("p (a t) -> p a t", a=1).to_broadcast(wide)
            eye = ident.rearrange("p (a t) -> p a t", a=1).to_broadcast(wide)

            def bank(b):
                return ps[:, b, :].rearrange("p (a t) -> p a t", a=NB)

            with ch.loop(4, 6) as i:
                for j in range(2):
                    dve.wait_ge(s_go, i * 2 + 1)
                    nc.vector.tensor_copy(gw["sel"][j][:, 0, :], const[0:40, 0, bass.ds(i * 2 + j, 1)].to_broadcast([40, P]))
                    nc.vector.tensor_copy(gw["sel"][j][:, 1, :], const[0:40, 0, bass.ds(i * 2 + (32 + j), 1)].to_broadcast([40, P])).then_inc(s_gsel, 1)
                for j in range(2):
                    head = bass.ds(i * 2 + j, 1)
                    dve.wait_ge(s_gbc, i * 2 + (j + 1))
                    nc.vector.tensor_tensor(gw["ao"][j][:, :, :].rearrange("p a t -> p (a t)"), ps[:, 4 * j + 1, :], tile_at(qk2, i * 2 + (8 + j)), ALU.mult).then_inc(s_gkb, 1)
                    dve.wait_ge(s_gem, i * 2 + (j + 1))
                    ch.step(nc.vector.tensor_tensor(gw["em"][j][:, :, :], gw["em"][j][:, :, :], upper, ALU.mult))
                    nc.vector.tensor_tensor(gw["qd"][j][:, :, :].rearrange("p a t -> p (a t)"), gw["eg"][j][:, :, :].rearrange("p a t -> p (a t)"), tile_at(qk2, i * 2 + j), ALU.mult)
                for j in range(2):
                    b, head = 4 * j, bass.ds(i * 2 + j, 1)
                    dve.wait_ge(s_gmm, i * 2 + (j + 1))
                    ch.wait()
                    nc.vector.tensor_tensor(gw["at"][j][:, :, :], bank(b + 1), gw["em"][j][:, :, :], ALU.mult).then_inc(s_gin, 1)
                    nc.vector.tensor_tensor(gw["qkt"][j][:, :, :], bank(b + 2), gw["em"][j][:, :, :], ALU.mult)
                    dve.wait_ge(s_gin, i * 2 + (j + 1))
                    ch.link(nc.vector.tensor_tensor(gw["tm"][j][:, :, :], gw["at"][j][:, :, :], merge1, ALU.mult))
                    ch.step(nc.vector.tensor_tensor(gw["tt"][j][:, :, :], eye, gw["tm"][j][:, :, :], ALU.subtract))
                    nc.vector.tensor_tensor(gw["kb"][j][:, :, :], bank(b + 3), g_exp[:, :, head].to_broadcast(wide), ALU.mult)
                    nc.vector.tensor_tensor(gw["kd"][j][:, :, :], bank(b + 3), g_dec[:, :, head].to_broadcast(wide), ALU.mult)
                    nc.vector.tensor_tensor(gw["vb"][j][:, :, :], bank(b), cols2[:, :, bass.ds(i * 2 + (32 + j), 1)].to_broadcast(wide), ALU.mult).then_inc(s_gtt, 1)
                for n_ in range(6):
                    for j in range(2):
                        dve.wait_ge(s_gdp, i * 12 + (2 * n_ + j + 1))
                        if n_ == 0:
                            dve.wait_ge(s_gtt, i * 2 + (j + 1))
                            dve.wait_ge(s_gtm, i * 2 + (j + 1))
                        else:
                            dve.wait_ge(s_gd, i * 12 + (2 * n_ - 2 + j + 1))
                        if n_ < 5:
                            nc.vector.tensor_tensor(gw["tm"][j][:, :, :], gw["tm"][j][:, :, :], bank(4 * j + 2), ALU.subtract)
                        nc.vector.tensor_tensor(gw["tt"][j][:, :, :], gw["tt"][j][:, :, :], bank(4 * j + 3), ALU.subtract).then_inc(s_gd, 1)
                for c in range(NB):
                    for j in range(2):
                        b = 4 * j
                        if c:
                            dve.wait_ge(s_gva, i * 6 + (2 * (c - 1) + j + 1))
                            nc.vector.tensor_tensor(gw["vn"][j][:, :], gw["uu"][j][:, c, :], ps[:, b + 2, 0:P], ALU.subtract).then_inc(s_gvn, 1)
                    for j in range(2):
                        b = 4 * j
                        if c < NB - 1:
                            dve.wait_ge(s_gop, i * 6 + (2 * c + j + 1))
                            if c == 0:
                                nc.vector.tensor_copy(gw["st"][j][:, :], ps[:, b + 2, P:2 * P]).then_inc(s_gs, 1)
                            else:
                                dve.wait_ge(s_gs, i * 6 + (2 * (c - 1) + j + 1))
                                nc.vector.scalar_tensor_tensor(out=gw["st"][j][:, :], in0=gw["st"][j][:, :], scalar=gw["eg"][j][:, c, P - 1:P],
                                                               in1=ps[:, b + 2, P:2 * P], op0=ALU.mult, op1=ALU.add).then_inc(s_gs, 1)
            dve_tile_norm(dve, w, ch, v2, 0, 8, "gdn_norm", gate2)
            for m in range(8):
                if m == 0:
                    dve.wait_ge(s_tn, w.tile_norms + 1)
                dve_lo_y(dve, w, m, v2)
            for side in range(2):
                dve_add_to_h(dve, w, 4, side, 1.0, gain)

        def pool_mixer2(pool):
            with pool.Fori(0, 4) as i:
                pool.wait_ge(s_tn, 17)
                pool.wait_ge(s_gcb, 1)
                pool.wait_ge(s_go, i * 2 + 1)
                pool.sem_inc(s_tick["pool"], 1)
                for j in range(2):
                    nc.gpsimd.tensor_copy(gw["k_st"][j][:, :, :].rearrange("p a t -> p (a t)"), tile_at(qk2, i * 2 + (8 + j))).then_inc(s_gst, 1)
                    nc.gpsimd.tensor_copy(gw["uu"][j][:, :, :].rearrange("p a t -> p (a t)"), tile_at(v2, i * 2 + j)).then_inc(s_gst, 1)
                for n_ in range(6):
                    level = mask[f"merge{2 << n_}"].rearrange("p (a t) -> p a t", a=1).to_broadcast([P, NB, P])
                    for j in range(2):
                        if n_ == 0:
                            pool.wait_ge(s_gtt, i * 2 + (j + 1))
                        else:
                            pool.wait_ge(s_gup, i * 12 + (2 * n_ - 2 + j + 1))
                        nc.gpsimd.tensor_tensor(gw["ao"][j][:, :, :], gw["at"][j][:, :, :], level, ALU.mult).then_inc(s_gao, 1)

        s_gact = sem("embedding_gate_activated")

        def pe_embed(pe, w):
            for side in range(2):
                plo = w.plo
                pe_square_half(pe, w, 2, lambda k: (mid_hi[:, 10 + k, :], mid_lo[:, 10 + k, :]), lambda k: pe.wait_ge(s_plo, plo + k + 1))
            w.plo += 2
            w.tiles += DK
            pe_column_layer(pe, w, 8, lambda bank: pe_norm_sum(pe, w, bank))
            w.norms += 1

        def act_embed(act, w, gain):
            act.wait_ge(s_p, 16 * (w.plo // 2 + 1))
            for k in range(2):
                nc.scalar.activation(mid_hi[:, 10 + k, :], p_f[:, k, :], ACT.Copy).then_inc(s_phi, 1)
            w.plo += 2
            for side in range(2):
                layer = w.square_layer(1)
                act_ahead(act, layer[0], 0, 0)
            n0, b0, g = w.column_layer(8)
            act_ahead(act, n0, 0, 0)
            act_rstd(act, w, 4 * (g ^ 1), EPS_2)
            for u in range(8):
                if u:
                    act_ahead(act, n0, 0, u)
                act.wait_ge(s_free, b0 + u + 5)
                nc.scalar.activation(ff_gate[:, u % 2, :], ff_gate[:, u % 2, :], ACT.Sigmoid).then_inc(s_gact, 1)
            if gain is not None:
                act.wait_ge(s_used, n0 + 8)
                act_prep(act, w, range(8), gain, lambda m: act.wait_ge(s_hup, w.hups + m + 1))
            w.hups += 8

        def dve_embed(dve, w, ch, gain):
            dve.wait_ge(s_phi, w.plo + 2)
            for k in range(2):
                nc.vector.tensor_tensor(mid_lo[:, 10 + k, :], p_f[:, k, :], mid_hi[:, 10 + k, :].bitcast(F32), ALU.subtract).then_inc(s_plo, 1)
            w.plo += 2
            for side in range(2):
                layer = w.square_layer(1)
                for m in range(4):
                    wait_square(dve, layer, 1, m)
                    nc.vector.tensor_copy(p_part[:, 4 * side + m, :], ps[:, 4 * layer[2] + m, :]).then_inc(s_free, 1)
            n0, b0, g = w.column_layer(8)
            dve.wait_ge(s_rstd, w.norms + 1)
            w.norms += 1
            for u in range(8):
                dve.wait_ge(s_used, n0 + u + 1)
                nc.vector.tensor_tensor(ff_gate[:, u % 2, :], ps[:, 4 * g + u % 4, :], rstd[:, :], ALU.mult).then_inc(s_free, 1)
                dve.wait_ge(s_gact, (w.plo // 2 - 1) * 8 + u + 1)
                ch.link(nc.vector.tensor_tensor(ff_gate[:, u % 2, :], ff_gate[:, u % 2, :], p_part[:, u, :], ALU.mult))
                nc.vector.tensor_tensor(h[:, u, :], h[:, u, :], ff_gate[:, u % 2, :], ALU.add).then_inc(s_hup, 1)
            if gain is not None:
                dve_prep(dve, w, range(8), gain)
            w.hups += 8

        s_sst = sem("sb_staged")
        s_sz = sem("sb_scores")
        s_ssp = sem("sb_softplus")
        s_sln = sem("sb_steps")
        s_slw = sem("sb_log_weights")
        s_sw = sem("sb_weights")
        s_swc = sem("sb_diagonal_clamped")
        s_swm = sem("sb_weights_masked")
        s_so = sem("sb_out")

        def pe_mixer3(pe, w):
            w.tiles += DK
            pe_column_layer(pe, w, 8, lambda bank: pe_norm_sum(pe, w, bank))
            w.norms += 1
            pe_rstd_columns(pe, w)
            pe.wait_ge(s_rcol, 2)
            pe_square_tokens(pe, w)
            pe_square_tokens(pe, w)
            w.tiles += DK
            pe_column_layer(pe, w, 8)
            pe.wait_ge(s_free, w.bank + 4)
            pe_tile_norm(pe, w, 16)
            pe.wait_ge(s_tln, w.tile_norms + 1)
            with pe.Fori(0, 4) as i:
                for j in range(2):
                    b = 3 * j
                    q_ = lambda lo_, hi_: q3[:, bass.ds(i * 2 + j, 1), lo_ * P:hi_ * P].rearrange("p a t -> p (a t)")
                    pe.wait_ge(s_sst, i * 4 + (2 * j + 2))
                    pe.wait_ge(s_sw, i * 2 + 1)
                    for a in range(NB - 1):
                        bk, at = divmod(b * T + OFF[a] * P, T)
                        nc.tensor.matmul(ps[:, bk, at:at + (NB - 1 - a) * P], sb_k[:, j, a * P:(a + 1) * P], q_(a + 1, NB),
                                         start=(a != 2), stop=False, skip_group_check=True)
                    for a in range(NB):
                        last = nc.tensor.matmul(ps[:, b, a * P:(a + 1) * P], sb_k[:, j, a * P:(a + 1) * P], q_(a, a + 1),
                                                start=(a == 0), stop=False, skip_group_check=True)
                    last.then_inc(s_sz, 1)
                for j in range(2):
                    pe.wait_ge(s_ssp, i * 2 + (j + 1))
                    for name, src, dst, n_ in sb_pairs():
                        bk, at = divmod(3 * j * T + dst * P, T)
                        last = nc.tensor.matmul(ps[:, bk, at:at + n_ * P], mask[name], sb_sp[:, j, src:src + n_, :],
                                                start=False, stop=True, skip_group_check=True)
                    last.then_inc(s_slw, 1)
                for j in range(2):
                    pe.wait_ge(s_swm, i * 2 + (j + 1))
                    if j == 0:
                        pe.wait_ge(s_mlo, i * 2 + w.mids)
                    for a in range(NB):
                        nc.tensor.matmul(ps[:, 6 + j, a * P:(a + 1) * P], sb_v[:, j, a, :], sb_l[:, j, a, :],
                                         start=(a == 0), stop=(a == NB - 1), skip_group_check=True) if a < NB - 1 else None
                        if a < NB - 1:
                            nc.tensor.matmul(ps[:, 6 + j, (a + 1) * P:T], sb_v[:, j, a, :], sb_l[:, j, OFF[a]:OFF[a] + NB - 1 - a, :],
                                             start=False, stop=False, skip_group_check=True)
                    nc.tensor.matmul(ps[:, 6 + j, (NB - 1) * P:T], sb_v[:, j, NB - 1, :], sb_l[:, j, NB - 1, :],
                                     start=False, stop=True, skip_group_check=True).then_inc(s_so, 1)
            mids = w.mids
            for side in range(2):
                pe_square_half(pe, w, 8, lambda k: (mid_hi[:, k, :], mid_lo[:, k, :]), lambda k: pe.wait_ge(s_mlo, mids + k + 1))
            w.mids += 8

        def sb_pairs():
            terms = []
            for a in range(NB):
                terms.append(("neg_tri", a, a, 1))
                if a < NB - 1:
                    terms.append(("neg_tri", OFF[a], OFF[a], NB - 1 - a))
                for c in range(a + 1, NB):
                    terms.append(("neg_ones", c, OFF[a] + c - a - 1, 1))
                    if c < NB - 1:
                        terms.append(("neg_ones", OFF[c], OFF[a] + c - a, NB - 1 - c))
            return terms

        def act_mixer3(act, w, gain):
            n0, b0, g = w.column_layer(8)
            act_ahead(act, n0, 0, 0)
            act_rstd(act, w, 4 * (g ^ 1), EPS_2)
            for u in range(1, 8):
                act_ahead(act, n0, 0, u)
            for side in range(2):
                layer = w.square_layer(4)
                for kp in range(4):
                    act_ahead(act, layer[0], 0, kp)
            act.wait_ge(s_used, layer[0] + 4)
            act_prep(act, w, range(8), "ln_mix1", lambda m: None, squares=False)
            n0, b0, g = w.column_layer(8)
            for u in range(8):
                act_ahead(act, n0, 0, u)
            act.wait_ge(s_free, w.bank + 4)
            act_tile_norm(act, w, k3, 0, 8, 1.0 / P, EPS_2)
            act_tile_norm(act, w, q3, 0, 8, 1.0, P * EPS_2)
            act.wait_ge(s_tn, w.tile_norms + 1)
            ch = w.act_steps
            with ch.loop(4, 4) as i:
                for j in range(2):
                    act.wait_ge(s_sz, i * 2 + (j + 1))
                    act.wait_ge(s_so, i * 2 + 1)
                    l_ = sb_l[:, j, :, :].rearrange("p a t -> p (a t)")
                    z_ = ps[:, 3 * j:3 * j + 3, :].rearrange("p a t -> p (a t)")[:, 0:10 * P]
                    ch.link(nc.scalar.activation(l_, z_, ACT.Abs))
                    ch.link(nc.scalar.activation(l_, l_, ACT.Exp, scale=-1.0))
                    nc.scalar.activation(l_, l_, ACT.Ln, bias=1.0).then_inc(s_sln, 1)
                for j in range(2):
                    act.wait_ge(s_slw, i * 2 + (j + 1))
                    l_ = sb_l[:, j, :, :].rearrange("p a t -> p (a t)")
                    z_ = ps[:, 3 * j + 1:3 * j + 3, :].rearrange("p a t -> p (a t)")[:, 0:6 * P]
                    nc.scalar.activation(l_[:, 4 * P:10 * P], z_, ACT.Exp)
                    act.wait_ge(s_swc, i * 2 + (j + 1))
                    nc.scalar.activation(l_[:, 0:4 * P], l_[:, 0:4 * P], ACT.Exp).then_inc(s_sw, 1)
                for j in range(2):
                    act.wait_ge(s_so, i * 2 + (j + 2))
                    nc.scalar.activation(tile_at(mid_hi, i * 2 + j), ps[:, 6 + j, :], ACT.Copy).then_inc(s_mhi, 1)
            w.mids += 8
            for side in range(2):
                layer = w.square_layer(4)
                for kp in range(4):
                    act_ahead(act, layer[0], 0, kp)
                act_prep(act, w, range(4 * side, 4 * side + 4), gain, lambda m: act.wait_ge(s_free, layer[1] + m % 4 + 5))

        def dve_mixer3(dve, w, ch, gain):
            def take(dest):
                n0, b0, g = w.column_layer(8)
                def body(i, j):
                    dve.wait_ge(s_used, i * 4 + (n0 + j + 1))
                    nc.vector.tensor_tensor(tile_at(dest, i * 4 + j), ps[:, 4 * g + j % 4, :], rstd[:, :], ALU.mult).then_inc(s_free, 1)
                each(dve, 8, body)

            dve.wait_ge(s_rstd, w.norms + 1)
            w.norms += 1
            take(k3)
            dve_rstd_columns(dve, w, 2)
            dve.wait_ge(s_rcol, 2)
            for half in range(2):
                dve_tokens_out(dve, w, v3[:, :, half * T:(half + 1) * T])
            dve_prep(dve, w, range(8), "ln_mix1", squares=False)
            take(q3)
            dve.wait_ge(s_free, w.bank + 4)
            dve_tile_norm(dve, w, ch, k3, 0, 8, "k_norm")
            dve_tile_norm(dve, w, ch, q3, 0, 8, "sb_q_norm")
            strict = mask["strict"].rearrange("p (a t) -> p a t", a=1).to_broadcast([P, NB, P])
            mids = w.mids
            with ch.loop(4, 2) as i:
                for j in range(2):
                    z_ = ps[:, 3 * j:3 * j + 3, :].rearrange("p a t -> p (a t)")[:, 0:10 * P]
                    dve.wait_ge(s_sln, i * 2 + (j + 1))
                    ch.link(nc.vector.scalar_tensor_tensor(out=sb_sp[:, j, :, :].rearrange("p a t -> p (a t)"), in0=z_, scalar=0.0,
                                                           in1=sb_l[:, j, :, :].rearrange("p a t -> p (a t)"), op0=ALU.max, op1=ALU.add))
                    nc.vector.tensor_tensor(sb_sp[:, j, 0:NB, :], sb_sp[:, j, 0:NB, :], strict, ALU.mult).then_inc(s_ssp, 1)
                for j in range(2):
                    dve.wait_ge(s_slw, i * 2 + (j + 1))
                    nc.vector.tensor_scalar(sb_l[:, j, 0:NB, :].rearrange("p a t -> p (a t)"), ps[:, 3 * j, :], 0.0, None, ALU.min).then_inc(s_swc, 1)
                for j in range(2):
                    dve.wait_ge(s_sw, i * 2 + (j + 2))
                    nc.vector.tensor_tensor(sb_l[:, j, 0:NB, :], sb_l[:, j, 0:NB, :], strict, ALU.mult).then_inc(s_swm, 1)
                for j in range(2):
                    dve.wait_ge(s_mhi, i * 2 + (mids + j + 1))
                    nc.vector.tensor_tensor(tile_at(mid_lo, i * 2 + j), ps[:, 6 + j, :], tile_at(mid_hi, i * 2 + j).bitcast(F32), ALU.subtract).then_inc(s_mlo, 1)
            w.mids += 8
            for side in range(2):
                dve_add_to_h(dve, w, 4, side, 1.0, gain)

        def pool_mixer3(pool, tn):
            with pool.Fori(0, 4) as i:
                pool.wait_ge(s_so, i * 2 + 1)
                pool.sem_inc(s_tick["pool"], 1)
                pool.wait_ge(s_tn, tn + 1)
                for j in range(2):
                    nc.gpsimd.tensor_copy(sb_k[:, j, :], tile_at(k3, i * 2 + j)).then_inc(s_sst, 1)
                    nc.gpsimd.tensor_copy(sb_v[:, j, :, :], v3[:, :, bass.ds((i * 2 + j) * P, P)]).then_inc(s_sst, 1)

        def pe_final_norm(pe, w):
            pe_norm_sum(pe, w, 4 * w.group)
            w.norms += 1

        def act_final_norm(act, w):
            act_rstd(act, w, 4 * w.group, EPS_1)
            act_prep(act, w, range(8), "ln_mix0", lambda m: act.wait_ge(s_hup, w.hups + m + 1))
            w.hups += 8

        def dve_final_norm(dve, w):
            dve.wait_ge(s_rstd, w.norms + 1)
            w.norms += 1
            c = COL["final_norm"][0]
            for m in range(8):
                nc.vector.scalar_tensor_tensor(out=h[:, m, :], in0=h[:, m, :], scalar=vec[:, c + m:c + m + 1], in1=rstd[:, :],
                                               op0=ALU.mult, op1=ALU.mult).then_inc(s_hup, 1)
            dve_prep(dve, w, range(8), "ln_mix0")
            w.hups += 8

        from_one = [s_o, s_sfree, s_ptp, s_pt, s_yg, s_y, s_zact, s_convact, s_tsum, s_tn, s_tln, s_gateact, s_go, s_so, s_sw]
        block = ctx.enter_context(nc.Block())

        @block.sync
        def _(sp):
            def load(i, n):
                unit = units[n] if isinstance(i, int) else units[bass.ds(i * 2 + n, 1), :, :].rearrange("a p n -> (a p) n")
                sp.dma_start(raw[:, n % 2, :], unit).then_inc(s_w[n % 2], 16)

            sp.dma_start(vec[:, :], vectors[:, :]).then_inc(s_const, 16)
            sp.dma_start(h[:, :, :], x_t.rearrange("(k p) t -> p k t", p=P)).then_inc(s_x, 16)
            sp.dma_start(const[:, :, :], constants[:, :, :]).then_inc(s_const, 16)
            load(0, 0)
            load(0, 1)
            with sp.Fori(0, N_UNITS // 2 - 1) as i:
                for n in (2, 3):
                    sp.wait_ge(s_wlo, i * 2 + (n - 1))
                    load(i, n)
            sp.wait_ge(s_hup, 24)
            sp.dma_start(out_t.rearrange("(k p) t -> p k t", p=P), h[:, :, :]).then_inc(s_out, 16)
            sp.wait_ge(s_out, 16)

        @block.gpsimd
        def _(pool):
            w = Walk()
            for one in from_one:
                pool.sem_inc(one, 1)
            pool_at = [0]

            def split_to(end):
                n0 = pool_at[0]

                def body(i, j):
                    n = n0 + j
                    pool.wait_ge(s_whi, i * 4 + (n + 1))
                    nc.gpsimd.tensor_tensor(w_lo[:, n % W_SLOTS, :], raw[:, n % RAW_SLOTS, :], w_hi[:, n % W_SLOTS, :].bitcast(F32), ALU.subtract).then_inc(s_wlo, 1)

                each(pool, end - n0, body)
                pool_at[0] = end

            def ffn_walk():
                for tiles in HALVES:
                    w.column_layer(2 * tiles)
                    w.square_layer(tiles // 2)
                    w.square_layer(tiles // 2)

            ffn_walk()
            w.column_layer(U_END)
            w.square_layer(4)
            split_to(w.unit + AHEAD)
            pool_mixer1(pool, w)
            w.square_layer(6)
            w.square_layer(6)
            ffn_walk()
            w.column_layer(U_END2)
            split_to(w.unit + AHEAD)
            pool_mixer2(pool)
            w.square_layer(4)
            w.square_layer(4)
            ffn_walk()
            for units_ in (1, 1):
                w.square_layer(units_)
            w.column_layer(8)
            w.column_layer(8)
            w.square_layer(4)
            w.square_layer(4)
            w.column_layer(8)
            split_to(w.unit + AHEAD)
            pool_mixer3(pool, 40)
            split_to(NREAL + AHEAD)

        @block.tensor
        def _(pe):
            w = Walk()
            pe.wait_ge(s_const, 32)
            pe_ffn(pe, w)
            pe_mixer1(pe, w)
            pe_ffn(pe, w)
            pe_final_norm(pe, w)
            pe_mixer2(pe, w)
            pe_ffn(pe, w)
            pe_embed(pe, w)
            pe_mixer3(pe, w)
            pe_ffn(pe, w)
            pe_embed(pe, w)
            assert w.unit == NREAL, (w.unit, NREAL)

        @block.scalar
        def _(act):
            w = Walk()
            for n in range(AHEAD):
                act_round(act, 0, n)
            act.wait_ge(s_const, 32)
            act_prep(act, w, range(8), "ffn1_norm", lambda m: act.wait_ge(s_x, 16))
            act_ffn(act, w, EPS_1, "mix_norm")
            act_mixer1(act, w, "ffn2_norm")
            act_ffn(act, w, EPS_1, None)
            act_final_norm(act, w)
            act_mixer2(act, w, "ln_ffn0")
            act_ffn(act, w, EPS_2, "ln_ple0", 0)
            act_embed(act, w, "kv_norm")
            act_mixer3(act, w, "ln_ffn1")
            act_ffn(act, w, EPS_2, "ln_ple1", 1)
            act_embed(act, w, None)

        @block.vector
        def _(dve):
            w = Walk()
            ch = Chain(dve, s_dve)
            for b in range(4):
                nc.vector.memset(rcol[:, b:b + 1], 0.0).then_inc(s_free, 1)
            dve.wait_ge(s_const, 32)
            dve_prep(dve, w, range(8), "ffn1_norm")
            dve_ffn(dve, w, 0.5, "mix_norm")
            dve_mixer1(dve, w, ch, "ffn2_norm")
            dve_ffn(dve, w, 0.5, None)
            dve_final_norm(dve, w)
            dve_mixer2(dve, w, ch, "ln_ffn0")
            dve_ffn(dve, w, 1.0, "ln_ple0")
            dve_embed(dve, w, ch, "kv_norm")
            dve_mixer3(dve, w, ch, "ln_ffn1")
            dve_ffn(dve, w, 1.0, "ln_ple1")
            dve_embed(dve, w, ch, None)


def kernel(**inputs):
    import concourse.bacc as _bacc
    from concourse import mybir as _mybir
    from concourse.bass_utils import run_bass_kernel_spmd as _run

    a = {k: np.asarray(v) for k, v in inputs.items()}

    def column_units(wt):
        n = -(-wt.shape[1] // P)
        full = np.zeros((D, n * P), np.float32)
        full[:, :wt.shape[1]] = wt
        return full.reshape(DK, P, n, P).transpose(2, 1, 0, 3).reshape(n, P, UNIT)

    def square_units(wt):
        k, n = wt.shape
        return wt.reshape(k // 256, 2, P, n // T, T).transpose(3, 0, 2, 1, 4).reshape(-1, P, UNIT)

    def ffn_units(gate, up, down):
        parts, at = [], 0
        for tiles in HALVES:
            cols = slice(at * P, (at + tiles) * P)
            g, u = column_units(gate[:, cols]), column_units(up[:, cols])
            parts.append(np.stack([g, u], axis=1).reshape(2 * tiles, P, UNIT))
            parts.append(square_units(down[cols]))
            at += tiles
        return parts

    def ffn2(i):
        wt = a["ffn_w_in_2"][i]
        return ffn_units(wt[:, :D_FF], wt[:, D_FF:], a["ffn_w_out_2"][i])

    w1, g2 = a["w_in"][0], a["gdn_w_in_2"][0]
    ab = np.zeros((D, P), np.float32)
    ab[:, 0:8], ab[:, 32:40] = g2[:, 4096:4104], g2[:, 4104:4112]
    w_out = a["w_out"][0]
    units = np.concatenate(
        ffn_units(a["ffn1_w_gate"][0], a["ffn1_w_up"][0], a["ffn1_w_down"][0])
        + [column_units(w1[:, 2576:3600]), column_units(w1[:, 2560:2576]), column_units(w1[:, 1024:2560]),
           column_units(w1[:, 0:1024]), square_units(w1[:, 3600:4112]),
           square_units(np.concatenate([w_out[1024:], w_out[:1024]]))]
        + ffn_units(a["ffn2_w_gate"][0], a["ffn2_w_up"][0], a["ffn2_w_down"][0])
        + [column_units(g2[:, 0:3072]), column_units(ab), column_units(g2[:, 3072:4096]), square_units(a["gdn_w_out_2"][0])]
        + ffn2(0) + [square_units(a["ple_w_proj_2"][0]), column_units(a["ple_w_gate_2"][0])]
        + [column_units(a["w_kv_2"][:, 0:1024]), square_units(a["w_kv_2"][:, 1024:2048]), column_units(a["sb_w_q_2"][0]),
           square_units(a["sb_w_out_2"][0])]
        + ffn2(1) + [square_units(a["ple_w_proj_2"][1]), column_units(a["ple_w_gate_2"][1])]
        + [np.zeros((4, P, UNIT), np.float32)])

    vec = np.zeros((P, N_COL), np.float32)

    def put(name, block):
        at, n = COL[name]
        vec[:block.shape[0], at:at + n] = block

    def tiles_of(v):
        return v.reshape(-1, P).T

    for name, v in (("ffn1_norm", a["ffn1_norm"][0]), ("mix_norm", a["mix_norm"][0]), ("ffn2_norm", a["ffn2_norm"][0]),
                    ("final_norm", a["final_norm"]), ("ssd_norm", a["ssd_norm"][0]), ("conv_b", a["conv_b"][0]),
                    ("ln_mix0", a["ln_mix_2"][0]), ("ln_mix1", a["ln_mix_2"][1]), ("ln_ffn0", a["ln_ffn_2"][0]),
                    ("ln_ffn1", a["ln_ffn_2"][1]), ("ln_ple0", a["ln_ple_2"][0]), ("ln_ple1", a["ln_ple_2"][1]),
                    ("gdn_norm", a["gdn_norm_2"][0]), ("kv_norm", a["kv_norm_2"]), ("k_norm", a["k_norm_2"]),
                    ("sb_q_norm", a["sb_q_norm_2"][0]), ("d_skip", np.repeat(a["d_skip"][0], SSD_DIM))):
        put(name, tiles_of(v))
    for name, v in (("conv_w", a["conv_w"][0]), ("gdn_conv", a["gdn_conv_2"][0])):
        put(name, v.reshape(CONV, -1, P).transpose(2, 1, 0).reshape(P, -1))
    for name, v in (("dt_bias", a["dt_bias"][0]), ("a_log", a["a_log"][0]), ("gdn_a_log", a["gdn_a_log_2"][0]),
                    ("gdn_dt_bias", a["gdn_dt_bias_2"][0])):
        put(name, v.reshape(-1, 1))

    distance = np.arange(P)[:, None] - np.arange(T)[None, :] + (T - P)
    rel = a["rel_bias"][0][:, np.clip(distance, -REL, REL) + REL].transpose(1, 0, 2)

    arrays = {
        "units": units, "x_t": a["x"][0].T, "p_t": a["p_2"][:, 0].transpose(0, 2, 1), "vectors": vec,
        "constants": constant_tiles(), "rel_table": rel,
    }
    arrays = {f"in_{k}_dram": np.ascontiguousarray(v) for k, v in arrays.items()}
    nc = _bacc.Bacc("TRN2", target_bir_lowering=False, num_devices=1)
    args = [nc.dram_tensor(k, v.shape, _mybir.dt.from_np(v.dtype), kind="ExternalInput").ap() for k, v in arrays.items()]
    out = nc.dram_tensor("out_0_dram", (D, T), F32, kind="ExternalOutput").ap()
    build(nc, *args, out)
    r = _run(nc, [arrays], core_ids=[0])
    return np.ascontiguousarray(r.results[0]["out_0_dram"].T)[None]
```

```python
from contextlib import ExitStack, contextmanager

import numpy as np
import concourse.bass as bass
from concourse import mybir

F32, F32R = mybir.dt.float32, mybir.dt.float32r
ALU, ACT, AX = mybir.AluOpType, mybir.ActivationFunctionType, mybir.AxisListType

P = 128
T = 512
NB = T // P
D = 1024
DK = D // P
D_FF = 2816
HALVES = (12, 10)
CONV = 4
SSD_HEADS, SSD_DIM = 16, 64
ATT_HEADS, ATT_DIM = 8, 64
REL = 256
GDN_HEADS = 8
EPS_1, EPS_2 = 1e-5, 1e-6
UNIT = 8 * P
W_SLOTS, RAW_SLOTS = 4, 2
AHEAD = 3
MASKED = -3.0e38
SOFTPLUS_2 = 9
Y0, YG0 = 4, 2


def column_plan():
    plan, at = {}, 0
    for name, n in (("ffn1_norm", 8), ("mix_norm", 8), ("ffn2_norm", 8), ("final_norm", 8), ("ssd_norm", 8),
                    ("conv_w", 12 * CONV), ("conv_b", 12), ("dt_bias", 1), ("a_log", 1), ("d_skip", 8),
                    ("ln_mix0", 8), ("ln_mix1", 8), ("ln_ffn0", 8), ("ln_ffn1", 8), ("ln_ple0", 8), ("ln_ple1", 8),
                    ("gdn_conv", 24 * CONV), ("gdn_a_log", 1), ("gdn_dt_bias", 1), ("gdn_norm", 1),
                    ("kv_norm", 8), ("k_norm", 1), ("sb_q_norm", 1)):
        plan[name] = (at, n)
        at += n
    return plan, at


COL, N_COL = column_plan()
LEVELS = (1, 2, 4, 8, 16, 32, 64)
MASKS = ["ident", "ones", "upper", "strict", "neg_tri", "neg_ones"] + [f"merge{b}" for b in LEVELS]


def constant_tiles():
    s, r = np.meshgrid(np.arange(P), np.arange(P), indexing="ij")
    tiles = [s == r, s >= 0, r >= s, r > s, -(s >= r).astype(np.float32), -np.ones((P, P))]
    for b in LEVELS:
        tiles.append((s // (2 * b) == r // (2 * b)) & (s % (2 * b) < b) & (r % (2 * b) >= b))
    return np.stack([np.asarray(t, np.float32) for t in tiles], axis=1)


class Walk:

    def __init__(self):
        self.unit = 0
        self.bank = 0
        self.group = 0
        self.prev_bank = 0
        self.squares = 0
        self.tiles = 0
        self.sums = 0
        self.norms = 0
        self.mids = 0
        self.gated = 0
        self.hups = 0
        self.plo = 0
        self.batches = 0
        self.squared = 0

    def column_layer(self, count):
        at = (self.unit, self.bank, self.group)
        self.prev_bank = self.bank
        self.unit += count
        self.bank += count
        self.group ^= 1
        return at

    def square_layer(self, units):
        at = (self.unit, self.bank, self.group, self.prev_bank, self.squares)
        self.prev_bank = self.bank
        self.unit += units
        self.bank += 4
        self.group ^= 1
        self.squares += 1
        return at


def each(eng, count, body, first=0, begin=0):
    at, end = begin + first, begin + count
    for u in range(begin, at):
        body(0, u)
    laps = (end - at) // 4
    if laps >= 2:
        with eng.Fori(0, laps) as i:
            for j in range(at, at + 4):
                body(i, j)
        at += laps * 4
    for u in range(at, end):
        body(0, u)


def tile_at(t, u):
    if isinstance(u, int):
        return t[:, u, :]
    return t[:, bass.ds(u, 1), :].rearrange("p a t -> p (a t)")


def col_at(t, u, n=1):
    return t[:, u:u + n] if isinstance(u, int) else t[:, bass.ds(u, n)]


class Chain:

    def __init__(self, eng, sem):
        self.eng, self.sem, self.n, self.turn = eng, sem, 0, 0

    def step(self, ins):
        ins.then_inc(self.sem, 1)
        self.n += 1

    def wait(self):
        self.eng.wait_ge(self.sem, self.turn + self.n)

    def link(self, ins):
        self.step(ins)
        self.wait()

    @contextmanager
    def loop(self, count, per):
        start = self.n
        with self.eng.Fori(0, count) as i:
            self.turn = i * per
            yield i
        assert self.n - start == per, (self.n - start, per)
        self.turn, self.n = 0, start + count * per


def build(nc, units, x_t, p_t, vectors, constants, rel_table, out_t):
    base = (nc.sbuf_base + 31) // 32 * 32
    limit = nc.sbuf_usable_end
    KB = 1024

    def place(name, at, shape, dtype=F32):
        size = int(np.prod(shape[1:])) * 4
        assert base + at + size <= limit, (name, base + at + size, limit)
        return nc.alloc_sbuf_tensor_at(name, shape, dtype, offset=base + at)

    with ExitStack() as ctx:
        def sem(name):
            return ctx.enter_context(nc.semaphore(name))

        raw = place("raw", 0, [P, RAW_SLOTS, UNIT])
        w_hi = place("w_hi", 8 * KB, [P, W_SLOTS, UNIT], F32R)
        w_lo = place("w_lo", 24 * KB, [P, W_SLOTS, UNIT], F32R)
        h = place("h", 40 * KB, [P, DK, T])
        x_hi = place("x_hi", 56 * KB, [P, DK, T], F32R)
        x_lo = place("x_lo", 72 * KB, [P, DK, T], F32R)
        mid_hi = place("mid_hi", 88 * KB, [P, 12, T], F32R)
        mid_lo = place("mid_lo", 112 * KB, [P, 12, T], F32R)
        rstd = place("rstd", 136 * KB, [P, T])
        sum_sq = place("sum_sq", 138 * KB, [P, T])
        sq = place("sq", 140 * KB, [P, 2, T])
        vec = place("vec", 144 * KB, [P, N_COL])
        assert N_COL <= 320
        const = place("const", 144 * KB + 1280, [P, len(MASKS), P])
        XG, MID_HI, MID_LO = 56 * KB, 88 * KB, 112 * KB
        M = 152 * KB
        mask = {name: const[:, i, :] for i, name in enumerate(MASKS)}
        ident, ones = mask["ident"], mask["ones"]

        ff_gate = place("ff_gate", M, [P, 2, T])
        ff_up = place("ff_up", M + 4 * KB, [P, 2, T])
        p_f = place("p_f", M + 8 * KB, [P, 2, T])
        p_part = place("p_part", M + 16 * KB, [P, DK, T])
        qk = place("qk", M, [P, 8, T])
        v_tok = place("v_tok", M + 16 * KB, [P, NB, T])
        toep = place("toep", M + 24 * KB, [P, ATT_HEADS, T])
        bc = place("bc", M + 40 * KB, [P, 4, T])
        cs_row = place("cs_row", M + 48 * KB, [SSD_HEADS, T])
        cols1 = place("cols1", M + 50 * KB, [P, NB, 2, SSD_HEADS])
        pad1 = place("pad1", M + 24 * KB, [P, 2, T + 4])
        cv1 = place("cv1", M + 24 * KB + 4160, [P, 2, T])
        z_tmp = place("z_tmp", M + 24 * KB + 8256, [P, 2, T])
        xs = place("xs", MID_HI, [P, 8, T])
        zs = place("zs", MID_LO, [P, 8, T])
        dt_raw = place("dt_raw", MID_HI + 16 * KB, [SSD_HEADS, T])
        dt_abs = place("dt_abs", MID_HI + 18 * KB, [SSD_HEADS, T])
        dt_row = place("dt_row", M + 52 * KB, [SSD_HEADS, T])
        da_row = place("da_row", MID_HI + 22 * KB, [SSD_HEADS, T])
        a_neg = place("a_neg", M + 50 * KB + 512, [SSD_HEADS, 1])
        at_q = place("at_q", XG, [P, T])
        at_v = place("at_v", XG + 2 * KB, [P, NB, P])
        at_s = place("at_s", XG + 4 * KB, [P, 2, 10, P])
        at_k = place("at_k", XG + 14 * KB, [P, T])
        at_pt = place("at_pt", XG + 16 * KB, [P, 2, 10, P])
        at_stat = place("at_stat", XG + 30 * KB, [P, 2, 3, NB])
        x_tok = place("x_tok", XG, [P, NB, D])
        cb = place("cb", XG + 16 * KB, [P, 2, 10, P])
        xdt = place("xdt", M + 24 * KB, [P, 4, NB, SSD_DIM])
        decay = place("decay", M + 4 * KB, [P, 4, 10, P])
        bias_c = place("bias_c", M + 50 * KB + 544, [P, 10, SSD_HEADS])
        total_c = place("total_c", M + 50 * KB + 1184, [P, NB, SSD_HEADS])
        sel1 = place("sel1", M + 42 * KB, [SSD_HEADS, 2, P])
        y_tmp = place("y_tmp", M, [P, 2, T])
        qk2 = place("qk2", M, [P, 16, T])
        gate2 = place("gate2", M + 32 * KB, [P, 8, T])
        g_row = place("g_row", M + 48 * KB, [40, T])
        cols2 = place("cols2", M + 50 * KB, [P, NB, 40])
        v2 = place("v2", MID_LO, [P, 8, T])
        pad2 = place("pad2", MID_HI, [P, 2, T + 4])
        cv2 = place("cv2", MID_HI + 4160, [P, 2, T])
        ga = place("ga", MID_HI + 9 * KB, [40, 4, T])
        a_neg2 = place("a_neg2", M + 50 * KB + 640, [8, 1])
        g_names = ["k_st", "em", "eg", "at", "tt", "tm", "ao", "u_", "kb", "vb", "wt", "uu", "qkt", "qd"]
        gw = {}
        spots = [XG + 2 * KB * i for i in range(16)] + [MID_HI + 2 * KB * i for i in range(12)] + [MID_LO + 16 * KB + 2 * KB * i for i in range(4)]
        for n_, name in enumerate(g_names):
            gw[name] = [place(f"{name}{j}", spots[2 * n_ + j], [P, NB, P]) for j in range(2)]
        gw["kd"] = [place(f"kd{j}", spots[28 + j], [P, NB, P]) for j in range(2)]
        gw["st"] = [place(f"st{j}", spots[30] + j * 512, [P, P]) for j in range(2)]
        gw["vn"] = [place(f"vn{j}", spots[30] + 1024 + j * 512, [P, P]) for j in range(2)]
        gw["sel"] = [place(f"sel{j}", spots[31] + j * 1024, [40, 2, P]) for j in range(2)]
        g_dec = place("g_dec", M + 50 * KB + 800, [P, NB, 8])
        g_exp = place("g_exp", M + 50 * KB + 928, [P, NB, 8])
        g_tmp = place("g_tmp", MID_HI + 17 * KB, [P, 2, T])
        nrm_sq = place("nrm_sq", XG, [P, 2, 4, T])
        nrm = place("nrm", XG + 16 * KB, [P, 2, 4, T])
        v_st = place("v_st", 140 * KB, [P, 2, T])
        k3 = place("k3", M, [P, 8, T])
        v3 = place("v3", M + 16 * KB, [P, NB, D])
        q3 = place("q3", M + 32 * KB, [P, 8, T])
        sb_l = place("sb_l", XG, [P, 2, 10, P])
        sb_sp = place("sb_sp", XG + 10 * KB, [P, 2, 10, P])
        sb_k = place("sb_k", XG + 20 * KB, [P, 2, T])
        sb_v = place("sb_v", XG + 24 * KB, [P, 2, NB, P])

        ps = ctx.enter_context(nc.psum_tensor("ps", [P, 8, T], F32))

        s_const = sem("constants_loaded")
        s_const2 = sem("masks_loaded")
        s_x = [sem(f"x_loaded_{i}") for i in range(4)]
        s_w = [sem(f"unit_loaded_{i}") for i in range(RAW_SLOTS)]
        s_whi = sem("w_hi_ready")
        s_wlo = sem("w_lo_ready")
        s_used = sem("units_used")
        s_bank = sem("square_result_ready")
        s_free = sem("banks_free")
        s_xhi = sem("x_hi_ready")
        s_sq = sem("square_ready")
        s_sum = sem("squares_summed")
        s_xlo = sem("x_lo_ready")
        s_msum = sem("sum_over_features_ready")
        s_lnv = sem("log_variance_ready")
        s_rstd = sem("rstd_ready")
        s_act1 = sem("gate_activated")
        s_prod = sem("gated_ready")
        s_mhi = sem("mid_hi_ready")
        s_mlo = sem("mid_lo_ready")
        s_dve = sem("vector_steps")
        s_act = sem("scalar_steps")
        s_hup = sem("h_updated")
        s_p = sem("p_loaded")
        s_phi = sem("p_hi_ready")
        s_plo = sem("p_lo_ready")
        s_out = sem("out_written")
        s_tick = {"pool": sem("tick_pool")}
        N_UNITS = units.shape[0]
        NREAL = N_UNITS - 4

        def pe_norm_sum(pe, w, bank):
            pe.wait_ge(s_sum, 8 * (w.norms + 1))
            nc.tensor.matmul(ps[:, bank, :], ones, sum_sq[:, :], start=True, stop=True).then_inc(s_msum, 1)

        def pe_column_layer(pe, w, count, after_first=None):
            n0, b0, g = w.column_layer(count)

            def body(i, j):
                u, slot = i * 4 + j, (n0 + j) % W_SLOTS
                pe.wait_ge(s_wlo, n0 + u + 1)
                pe.wait_ge(s_free, b0 + u + 1)
                for k in range(DK):
                    if j == 0:
                        pe.wait_ge(s_xlo, w.tiles - DK + k + 1)
                    hi, lo = w_hi[:, slot, k * P:(k + 1) * P], w_lo[:, slot, k * P:(k + 1) * P]
                    out = ps[:, 4 * g + j % 4, :]
                    nc.tensor.matmul(out, hi, x_hi[:, k, :], start=(k == 0), stop=False)
                    nc.tensor.matmul(out, hi, x_lo[:, k, :], start=False, stop=False)
                    last = nc.tensor.matmul(out, lo, x_hi[:, k, :], start=False, stop=(k == DK - 1))
                last.then_inc(s_used, 1)
                if j == 0 and after_first is not None:
                    after_first(4 * (g ^ 1))

            each(pe, count, body, first=1)

        def pe_square_half(pe, w, tiles, rhs, ready):
            n0, b0, g, prev, _ = w.square_layer(tiles // 2)
            for kp in range(tiles // 2):
                slot = (n0 + kp) % W_SLOTS
                pe.wait_ge(s_wlo, n0 + kp + 1)
                if kp == 0:
                    pe.wait_ge(s_free, prev + 4)
                for k2 in range(2):
                    k = 2 * kp + k2
                    ready(k)
                    r_hi, r_lo = rhs(k)
                    for m in range(4):
                        at = k2 * T + m * P
                        hi, lo = w_hi[:, slot, at:at + P], w_lo[:, slot, at:at + P]
                        out = ps[:, 4 * g + m, :]
                        nc.tensor.matmul(out, hi, r_hi, start=(k == 0), stop=False)
                        nc.tensor.matmul(out, hi, r_lo, start=False, stop=False)
                        last = nc.tensor.matmul(out, lo, r_hi, start=False, stop=(k == tiles - 1))
                        if k == tiles - 1 and m < 3:
                            last.then_inc(s_bank, 1)
                last.then_inc(s_used, 1)

        def pe_square_tokens(pe, w):
            n0, b0, g, prev, _ = w.square_layer(4)
            for kp in range(4):
                slot = (n0 + kp) % W_SLOTS
                pe.wait_ge(s_wlo, n0 + kp + 1)
                if kp == 0:
                    pe.wait_ge(s_free, prev + 4)
                for k2 in range(2):
                    k = 2 * kp + k2
                    hi, lo = w_hi[:, slot, k2 * T:(k2 + 1) * T], w_lo[:, slot, k2 * T:(k2 + 1) * T]
                    for m in range(4):
                        t_hi, t_lo = x_hi[:, k, m * P:(m + 1) * P], x_lo[:, k, m * P:(m + 1) * P]
                        out = ps[:, 4 * g + m, :]
                        nc.tensor.matmul(out, t_hi, hi, start=(k == 0), stop=False)
                        nc.tensor.matmul(out, t_lo, hi, start=False, stop=False)
                        last = nc.tensor.matmul(out, t_hi, lo, start=False, stop=(k == DK - 1))
                        if k == DK - 1 and m < 3:
                            last.then_inc(s_bank, 1)
                last.then_inc(s_used, 1)

        def wait_square(eng, layer, units_, m):
            n0, _, _, _, squares = layer
            if m < 3:
                eng.wait_ge(s_bank, 3 * squares + m + 1)
            else:
                eng.wait_ge(s_used, n0 + units_)

        def act_round(act, i, n):
            act.wait_ge(s_w[n % RAW_SLOTS], i * 32 + 16 * (n // RAW_SLOTS + 1))
            if n >= W_SLOTS:
                act.wait_ge(s_used, i * 4 + (n + 1 - W_SLOTS))
            nc.scalar.activation(w_hi[:, n % W_SLOTS, :], raw[:, n % RAW_SLOTS, :], ACT.Copy).then_inc(s_whi, 1)

        def act_ahead(act, n0, i, j):
            act_round(act, i, n0 + j + AHEAD)

        def act_prep(act, w, tiles, gain, ready, squares=True):
            c = COL[gain][0] if gain else None
            for m in tiles:
                ready(m)
                if gain:
                    nc.scalar.activation(x_hi[:, m, :], h[:, m, :], ACT.Copy, scale=vec[:, c + m:c + m + 1]).then_inc(s_xhi, 1)
                    w.tiles += 1
                if squares:
                    if w.sums >= 2:
                        act.wait_ge(s_sum, w.sums - 1)
                    nc.scalar.activation(sq[:, m % 2, :], h[:, m, :], ACT.Square).then_inc(s_sq, 1)
                    w.sums += 1

        def dve_prep(dve, w, tiles, gain, squares=True):
            for m in tiles:
                if gain:
                    c = COL[gain][0] + m
                    dve.wait_ge(s_xhi, w.tiles + 1)
                    nc.vector.scalar_tensor_tensor(out=x_lo[:, m, :], in0=h[:, m, :], scalar=vec[:, c:c + 1],
                                                   in1=x_hi[:, m, :].bitcast(F32), op0=ALU.mult, op1=ALU.subtract).then_inc(s_xlo, 1)
                    w.tiles += 1
                if squares:
                    dve.wait_ge(s_sq, w.sums + 1)
                    if m == 0:
                        nc.vector.tensor_copy(sum_sq[:, :], sq[:, 0, :]).then_inc(s_sum, 1)
                    else:
                        dve.wait_ge(s_sum, w.sums)
                        nc.vector.tensor_tensor(sum_sq[:, :], sum_sq[:, :], sq[:, m % 2, :], ALU.add).then_inc(s_sum, 1)
                    w.sums += 1

        def act_rstd(act, w, bank, eps):
            act.wait_ge(s_msum, w.norms + 1)
            nc.scalar.activation(rstd[:, :], ps[:, bank, :], ACT.Ln, bias=eps, scale=1.0 / D).then_inc(s_lnv, 1)
            act.wait_ge(s_lnv, w.norms + 1)
            nc.scalar.activation(rstd[:, :], rstd[:, :], ACT.Exp, scale=-0.5).then_inc(s_rstd, 1)
            w.norms += 1

        def pe_ffn(pe, w):
            for half, tiles in enumerate(HALVES):
                if half == 0:
                    w.tiles += DK
                    pe_column_layer(pe, w, 2 * tiles, lambda bank: pe_norm_sum(pe, w, bank))
                    w.norms += 1
                else:
                    pe_column_layer(pe, w, 2 * tiles)
                mids = w.mids
                for side in range(2):
                    pe_square_half(pe, w, tiles, lambda k: (mid_hi[:, k, :], mid_lo[:, k, :]),
                                   lambda k: pe.wait_ge(s_mlo, mids + k + 1))
                w.mids += tiles

        def act_ffn(act, w, eps, gain, load_p=None):
            for half, tiles in enumerate(HALVES):
                n0, b0, g = w.column_layer(2 * tiles)
                if half == 0:
                    act_rstd(act, w, 4 * (g ^ 1), eps)
                    if load_p is not None:
                        act.dma_start(p_f[:, :, :], p_t[load_p].rearrange("(k p) t -> p k t", p=P)).then_inc(s_p, 16)
                mids, gated = w.mids, w.gated

                def body(i, j):
                    act_ahead(act, n0, i, j)
                    pair, done = j // 2 % 2, i * 2 + j // 2
                    if j % 2 == 0:
                        act.wait_ge(s_free, i * 4 + (b0 + j + 5))
                        nc.scalar.activation(ff_gate[:, pair, :], ff_gate[:, pair, :], ACT.Silu).then_inc(s_act1, 1)
                    else:
                        act.wait_ge(s_prod, gated + done + 1)
                        nc.scalar.activation(tile_at(mid_hi, done), ff_up[:, pair, :], ACT.Copy).then_inc(s_mhi, 1)

                each(act, 2 * tiles, body, first=1)
                w.mids += tiles
                w.gated += tiles
                for side in range(2):
                    layer = w.square_layer(tiles // 2)
                    for kp in range(tiles // 2):
                        act_ahead(act, layer[0], 0, kp)
                    if half == 1:
                        act_prep(act, w, range(4 * side, 4 * side + 4), gain,
                                 lambda m: act.wait_ge(s_free, layer[1] + m % 4 + 5))

        def dve_ffn(dve, w, scale, gain):
            for half, tiles in enumerate(HALVES):
                n0, b0, g = w.column_layer(2 * tiles)
                if half == 0:
                    dve.wait_ge(s_rstd, w.norms + 1)
                    w.norms += 1
                mids, gated = w.mids, w.gated

                def body(i, j):
                    u, pair, done = i * 4 + j, j // 2 % 2, i * 2 + j // 2
                    dve.wait_ge(s_used, n0 + u + 1)
                    if j % 2 == 0:
                        nc.vector.tensor_tensor(ff_gate[:, pair, :], ps[:, 4 * g + j % 4, :], rstd[:, :], ALU.mult).then_inc(s_free, 1)
                    else:
                        nc.vector.tensor_tensor(ff_up[:, pair, :], ps[:, 4 * g + j % 4, :], rstd[:, :], ALU.mult).then_inc(s_free, 1)
                        dve.wait_ge(s_act1, gated + done + 1)
                        dve.wait_ge(s_free, b0 + u + 5)
                        nc.vector.tensor_tensor(ff_up[:, pair, :], ff_up[:, pair, :], ff_gate[:, pair, :], ALU.mult).then_inc(s_prod, 1)
                        dve.wait_ge(s_mhi, mids + done + 1)
                        nc.vector.tensor_tensor(tile_at(mid_lo, done), ff_up[:, pair, :], tile_at(mid_hi, done).bitcast(F32),
                                                ALU.subtract).then_inc(s_mlo, 1)

                each(dve, 2 * tiles, body)
                w.mids += tiles
                w.gated += tiles
                for side in range(2):
                    dve_add_to_h(dve, w, tiles // 2, side, scale, gain, half == 1)

        def dve_add_to_h(dve, w, units_, side, scale, gain, prep=True):
            layer = w.square_layer(units_)
            for m in range(4):
                wait_square(dve, layer, units_, m)
                t = 4 * side + m
                nc.vector.scalar_tensor_tensor(out=h[:, t, :], in0=ps[:, 4 * layer[2] + m, :], scalar=scale, in1=h[:, t, :],
                                               op0=ALU.mult, op1=ALU.add).then_inc(s_free, 1)
                if prep and m:
                    dve_prep(dve, w, [t - 1], gain)
            if prep:
                dve_prep(dve, w, [4 * side + 3], gain)


        U_DT, U_XBC, U_Z, U_END = 8, 9, 21, 29
        s_conv = sem("conv_ready")
        s_convact = sem("conv_activated")
        s_zact = sem("z_activated")
        s_rcolp = sem("rstd_columns_in_psum")
        s_rcol = sem("rstd_columns")
        s_toep = sem("bias_table_loaded")
        s_toepm = sem("bias_table_masked")
        s_stage = sem("staged")
        s_scores = sem("scores_ready")
        s_sfree = sem("scores_taken")
        s_max = sem("max_ready")
        s_exp = sem("exp_ready")
        s_pn = sem("probs_ready")
        s_ptp = sem("probs_transposed")
        s_pt = sem("probs_t_ready")
        s_o = sem("att_out_ready")
        s_dt = sem("dt_steps")
        s_cbp = sem("cb_in_psum")
        s_cb = sem("cb_diag_ready")
        s_cb2 = sem("cb_rest_ready")
        s_xtp = sem("x_transposed")
        s_xt = sem("x_tok_ready")
        s_colp = sem("columns_in_psum")
        s_col = sem("columns_ready")
        s_totp = sem("totals_in_psum")
        s_bias = sem("decay_biases_ready")
        s_sel = sem("selector_ready")
        s_csb = sem("cumsum_broadcast")
        s_dec = sem("decay_ready")
        s_dmin = sem("diagonal_exponents_ready")
        s_m = sem("decayed_cb_ready")
        s_y = sem("y_ready")
        s_yg = sem("y_gated")
        s_ysq = sem("y_square_ready")
        s_ysum = sem("y_squares_summed")
        s_ymsum = sem("y_sum_in_psum")
        s_yrstd = sem("y_rstd_ready")
        s_yn = sem("y_normed")
        rcol = place("rcol", 144 * KB + 1248, [P, NB])

        OFF = {0: 4, 1: 8, 2: 7}

        def pairs():
            return [(0, 0), (0, 1), (0, 2), (0, 3), (1, 1), (1, 2), (1, 3), (3, 3), (2, 2), (2, 3)]

        PAIR = {p_: n_ for n_, p_ in enumerate(pairs())}

        def score_row(j, ib):
            at = ib * (ib + 1) // 2
            return at_s[:, j, at:at + ib + 1, :].rearrange("p a t -> p (a t)")

        def score_bank(ib):
            bank, at = ((1, 3 * P), (2, 0), (1, 0), (0, 0))[ib]
            return ps[:, bank, at:at + (ib + 1) * P]

        def pe_keep_warm(bank, count):
            for _ in range(count):
                nc.tensor.matmul(ps[:, bank, :], ones, const[:, 0:4, :], start=True, stop=True)

        def pe_rstd_columns(pe, w):
            bank = 4 * w.group + 3
            pe.wait_ge(s_rstd, w.norms)
            pe.wait_ge(s_free, w.prev_bank + 4)
            for m in range(NB):
                last = nc.tensor.matmul(ps[:, bank, m:m + 1], rstd[:, m * P:(m + 1) * P], ident[:, 0:1], start=True, stop=True)
            last.then_inc(s_rcolp, 1)

        def dve_rstd_columns(dve, w, n_):
            dve.wait_ge(s_rcolp, n_)
            nc.vector.tensor_copy(rcol[:, :], ps[:, 4 * w.group + 3, 0:NB]).then_inc(s_rcol, 1)

        def dve_tokens_out(dve, w, dest):
            layer = w.square_layer(4)
            for m in range(NB):
                wait_square(dve, layer, 4, m)
                nc.vector.tensor_scalar(dest[:, m, :], ps[:, 4 * layer[2] + m, :], rcol[:, m:m + 1], None, ALU.mult).then_inc(s_free, 1)

        def dve_conv(dve, ch, at, count, pad, cv, w_name, b_name, first_unit, convs):
            n0, b0, g = at
            wc = COL[w_name][0]
            with ch.loop(count // 4, 12) as i:
                for j in range(first_unit, first_unit + 4):
                    slot = (j - first_unit) % 2
                    t = j - first_unit
                    dve.wait_ge(s_used, i * 4 + (n0 + j + 1))
                    nc.vector.tensor_tensor(pad[:, slot, 3:3 + T], ps[:, 4 * g + j % 4, :], rstd[:, :], ALU.mult).then_inc(s_free, 1)
                    dve.wait_ge(s_free, i * 4 + (b0 + j + 5))
                    dve.wait_ge(s_convact, i * 4 + (convs + max(t, 1)))
                    tap = lambda q: col_at(vec, i * 16 + (wc + 4 * t + q))
                    if b_name:
                        ch.link(nc.vector.tensor_scalar(cv[:, slot, :], pad[:, slot, 3:3 + T], tap(3), col_at(vec, i * 4 + (COL[b_name][0] + t)), ALU.mult, ALU.add))
                    else:
                        ch.link(nc.vector.tensor_scalar(cv[:, slot, :], pad[:, slot, 3:3 + T], tap(3), None, ALU.mult))
                    for q in (2, 1, 0):
                        last = nc.vector.scalar_tensor_tensor(out=cv[:, slot, :], in0=pad[:, slot, q:q + T], scalar=tap(q), in1=cv[:, slot, :],
                                                              op0=ALU.mult, op1=ALU.add)
                        if q:
                            ch.link(last)
                    last.then_inc(s_conv, 1)

        def pe_mixer1(pe, w):
            w.tiles += DK
            pe_column_layer(pe, w, U_END, lambda bank: pe_norm_sum(pe, w, bank))
            w.norms += 1
            pe_rstd_columns(pe, w)
            pe.wait_ge(s_rcol, 1)
            pe_square_tokens(pe, w)
            pe.wait_ge(s_free, w.bank + 4)
            def scores(pair, j):
                rows = slice(64 * j, 64 * j + 64)
                if j == 0:
                    pe.wait_ge(s_stage, pair * 3 + 2)
                pe.wait_ge(s_sfree, pair * 2 + (j + 1))
                for ib in range(NB):
                    last = nc.tensor.matmul(score_bank(ib), at_q[rows, ib * P:(ib + 1) * P], at_k[rows, 0:(ib + 1) * P], start=True, stop=True)
                last.then_inc(s_scores, 1)

            def turn_probs(pair, j):
                pe.wait_ge(s_pn, pair * 2 + (j + 1))
                pe.wait_ge(s_pt, pair * 2 + (j + 1))
                for n_, (a, ib) in enumerate(pairs()):
                    last = nc.tensor.transpose(ps[:, 4 + n_ // 4, n_ % 4 * P:(n_ % 4 + 1) * P], at_s[:, j, ib * (ib + 1) // 2 + a, :], ident)
                last.then_inc(s_ptp, 1)

            mids = w.mids

            def values(pair, j):
                pe.wait_ge(s_pt, pair * 2 + (j + 2))
                if j == 0:
                    pe.wait_ge(s_stage, pair * 3 + 3)
                    pe.wait_ge(s_mlo, pair + mids)
                for a in range(NB):
                    first = PAIR[a, a]
                    last = nc.tensor.matmul(ps[64 * j:64 * j + 64, 7, a * P:T], at_v[:, a, 64 * j:64 * j + 64],
                                            at_pt[:, j, first:first + NB - a, :], start=(a == 0), stop=(a == NB - 1))
                last.then_inc(s_o, 1)

            def pair_of_heads(pair, more):
                turn_probs(pair, 0)
                if more:
                    scores(pair + 1, 0)
                values(pair, 0)
                turn_probs(pair, 1)
                pe_keep_warm(3, 1)
                values(pair, 1)
                if more:
                    scores(pair + 1, 1)

            scores(0, 0)
            scores(0, 1)
            pe_keep_warm(3, 3)
            with pe.Fori(0, 3) as i:
                pair_of_heads(i, True)
            pair_of_heads(3, False)
            w.mids += 4
            pe.wait_ge(s_dt, 1)
            pe.wait_ge(s_pt, 9)
            for m in range(NB):
                nc.tensor.transpose(ps[:, 4, m * 32:m * 32 + 16], cs_row[:, m * P:(m + 1) * P], ident[0:16, 0:16])
                last = nc.tensor.transpose(ps[:, 4, m * 32 + 16:m * 32 + 32], dt_row[:, m * P:(m + 1) * P], ident[0:16, 0:16])
            last.then_inc(s_colp, 1)
            for g in range(2):
                if g:
                    pe.wait_ge(s_cb, 1)
                    pe.wait_ge(s_cb2, 1)
                for m in range(NB):
                    b_block = bc[:, g, m * P:(m + 1) * P]
                    last = nc.tensor.matmul(ps[:, 0, m * P:(m + 1) * P], b_block, bc[:, 2 + g, m * P:(m + 1) * P], start=True, stop=True)
                    if m < NB - 1:
                        bk, at = divmod(OFF[m] * P, T)
                        last = nc.tensor.matmul(ps[:, bk, at:at + (NB - 1 - m) * P], b_block, bc[:, 2 + g, (m + 1) * P:T], start=True, stop=True)
                last.then_inc(s_cbp, 1)
            pe.wait_ge(s_col, 1)
            nc.tensor.matmul(ps[:, 4, 256:256 + NB * 16], ident[:, P - 1:P].to_broadcast([P, P]), cols1[:, :, 0, :], start=True, stop=True).then_inc(s_totp, 1)
            for n_ in range(8):
                m, half = n_ // 2, n_ % 2
                if n_ >= 2:
                    pe.wait_ge(s_xt, n_ - 1)
                for t in range(4):
                    last = nc.tensor.transpose(ps[:, 5 + n_ % 2, t * P:(t + 1) * P], xs[:, 4 * half + t, m * P:(m + 1) * P], ident)
                last.then_inc(s_xtp, 1)

            def broadcast(i, t):
                pe.wait_ge(s_sel, i * 4 + (t + 1))
                if t >= 2:
                    pe.wait_ge(s_dec, i * 4 + (t - 1))
                nc.tensor.matmul(ps[:, t % 2, :], sel1[:, t % 2, :], cs_row[:, :], start=True, stop=True).then_inc(s_csb, 1)

            def y_head(i, t):
                j, bank = t % 2, 2 + t // 2 % 2
                pe.wait_ge(s_m, i * 4 + (t + 1))
                if j == 0:
                    pe.wait_ge(s_yg, i * 2 + (t // 2 + 1))
                for a in range(NB):
                    last = nc.tensor.matmul(ps[64 * j:64 * j + 64, bank, a * P:(a + 1) * P], xdt[:, t, a, :], decay[:, t, a, :],
                                            start=(a == 0), stop=(a == NB - 1), skip_group_check=True)
                    if a < NB - 1:
                        nc.tensor.matmul(ps[64 * j:64 * j + 64, bank, (a + 1) * P:T], xdt[:, t, a, :], decay[:, t, OFF[a]:OFF[a] + NB - 1 - a, :],
                                         start=False, stop=False, skip_group_check=True)
                last.then_inc(s_y, 1)

            pe.wait_ge(s_cb, 2)
            pe.wait_ge(s_cb2, 2)
            broadcast(0, 0)
            broadcast(0, 1)
            with pe.Fori(0, 4) as i:
                for t in range(4):
                    broadcast(i, t + 2)
                    pe_keep_warm(5, 1)
                    y_head(i, t)
            pe.wait_ge(s_ysum, 8)
            nc.tensor.matmul(ps[:, 4 * (w.group ^ 1) + 3, :], ones, sum_sq[:, :], start=True, stop=True).then_inc(s_ymsum, 1)
            mids = w.mids - 4
            for side in range(2):
                pe_square_half(pe, w, 12, lambda k: (mid_hi[:, (k + 8) % 12, :], mid_lo[:, (k + 8) % 12, :]),
                               lambda k: pe.wait_ge(s_mlo, mids + k + 1))
            w.mids += 8

        def act_mixer1(act, w, gain):
            n0, b0, g = w.column_layer(U_END)
            act_ahead(act, n0, 0, 0)
            act_rstd(act, w, 4 * (g ^ 1), EPS_1)
            each(act, U_XBC - 1, lambda i, j: act_ahead(act, n0, i, j), begin=1)

            def conv_tile(dest, t0):
                def body(i, j):
                    act_ahead(act, n0, i, j)
                    act.wait_ge(s_conv, i * 4 + (j - U_XBC + 1))
                    nc.scalar.activation(tile_at(dest, i * 4 + (j - U_XBC - t0)), cv1[:, (j - U_XBC) % 2, :], ACT.Silu).then_inc(s_convact, 1)
                return body

            each(act, 8, conv_tile(xs, 0), begin=U_XBC)
            each(act, 4, conv_tile(bc, 8), begin=U_XBC + 8)

            def z_tile(i, j):
                act_ahead(act, n0, i, j)
                act.wait_ge(s_free, i * 4 + (b0 + j + 5))
                nc.scalar.activation(tile_at(zs, i * 4 + (j - U_Z)), z_tmp[:, (j - U_Z) % 2, :], ACT.Silu).then_inc(s_zact, 1)

            each(act, 8, z_tile, begin=U_Z)
            act.wait_ge(s_zact, 9)
            act.dma_start(toep[:, :, :], rel_table[:, :, :]).then_inc(s_toep, 16)
            layer = w.square_layer(4)
            for kp in range(4):
                act_ahead(act, layer[0], 0, kp)
            ch = Chain(act, s_act)
            w.act_steps = ch
            act.wait_ge(s_dtb, 1)
            ch.link(nc.scalar.activation(dt_abs[:, :], dt_raw[:, :], ACT.Abs))
            ch.link(nc.scalar.activation(dt_abs[:, :], dt_abs[:, :], ACT.Exp, scale=-1.0))
            ch.step(nc.scalar.activation(dt_abs[:, :], dt_abs[:, :], ACT.Ln, bias=1.0))
            ch.step(nc.scalar.activation(a_neg[:, :], vec[0:SSD_HEADS, COL["a_log"][0]:COL["a_log"][0] + 1], ACT.Exp))
            mids = w.mids
            def exps(pair, j):
                act.wait_ge(s_max, pair * 2 + (j + 1))
                for ib in range(NB):
                    last = nc.scalar.activation(score_row(j, ib), score_row(j, ib), ACT.Exp,
                                                bias=at_stat[:, j, 0, ib:ib + 1], accum_out=at_stat[:, j, 1, ib:ib + 1])
                last.then_inc(s_exp, 1)

            def pair_of_heads(pair, more):
                exps(pair, 1)
                for j in range(2):
                    act.wait_ge(s_ptp, pair * 2 + (j + 2))
                    for n_, width in ((0, 4), (1, 4), (2, 2)):
                        last = nc.scalar.activation(at_pt[:, j, 4 * n_:4 * n_ + width, :].rearrange("p a t -> p (a t)"),
                                                    ps[:, 4 + n_, 0:width * P], ACT.Copy)
                    last.then_inc(s_pt, 1)
                if more:
                    exps(pair + 1, 0)
                act.wait_ge(s_o, pair * 2 + 3)
                nc.scalar.activation(tile_at(mid_hi, pair + 8), ps[:, 7, :], ACT.Copy).then_inc(s_mhi, 1)

            exps(0, 0)
            with act.Fori(0, 3) as i:
                pair_of_heads(i, True)
            pair_of_heads(3, False)
            w.mids += 4
            for g in range(2):
                act.wait_ge(s_cbp, g + 1)
                nc.scalar.activation(cb[:, g, NB:10, :].rearrange("p a t -> p (a t)"),
                                     ps[:, 1:3, :].rearrange("p a t -> p (a t)")[:, 0:6 * P], ACT.Copy).then_inc(s_cb2, 1)
            for n_ in range(8):
                act.wait_ge(s_xtp, n_ + 1)
                nc.scalar.activation(x_tok[:, n_ // 2, n_ % 2 * T:(n_ % 2 + 1) * T], ps[:, 5 + n_ % 2, :], ACT.Copy).then_inc(s_xt, 1)
            act.wait_ge(s_bias, 1)

            def decays(i, t):
                act.wait_ge(s_csb, i * 4 + (t + 1))
                act.wait_ge(s_y, i * 4 + (t + 1))
                act.wait_ge(s_dmin, i * 4 + (t + 1))
                head = bass.ds(i * 4 + t, 1)
                for a in range(NB - 1):
                    for ib in range(a + 1, NB):
                        nc.scalar.activation(decay[:, t, OFF[a] + ib - a - 1, :], ps[:, t % 2, ib * P:(ib + 1) * P], ACT.Exp,
                                             bias=bias_c[:, PAIR[a, ib], head])
                diag = decay[:, t, 0:NB, :].rearrange("p a t -> p (a t)")
                nc.scalar.activation(diag, diag, ACT.Exp).then_inc(s_dec, 1)

            with act.Fori(0, 4) as i:
                for t in range(4):
                    decays(i, t)
            for m in range(8):
                act.wait_ge(s_yg, m + 3)
                if m >= 2:
                    act.wait_ge(s_ysum, m - 1)
                nc.scalar.activation(sq[:, m % 2, :], zs[:, m, :], ACT.Square).then_inc(s_ysq, 1)
            act.wait_ge(s_ymsum, 1)
            ch.link(nc.scalar.activation(rstd[:, :], ps[:, 4 * (w.group ^ 1) + 3, :], ACT.Ln, bias=EPS_1, scale=1.0 / D))
            nc.scalar.activation(rstd[:, :], rstd[:, :], ACT.Exp, scale=-0.5).then_inc(s_yrstd, 1)
            for m in range(8):
                act.wait_ge(s_yn, m + 1)
                nc.scalar.activation(mid_hi[:, m, :], zs[:, m, :], ACT.Copy).then_inc(s_mhi, 1)
            w.mids += 8
            for side in range(2):
                layer = w.square_layer(6)
                for kp in range(6):
                    act_ahead(act, layer[0], 0, kp)
                act_prep(act, w, range(4 * side, 4 * side + 4), gain, lambda m: act.wait_ge(s_free, layer[1] + m % 4 + 5))

        s_dtb = sem("dt_biased")

        def dve_mixer1(dve, w, ch, gain):
            n0, b0, g = w.column_layer(U_END)
            dve.wait_ge(s_rstd, w.norms + 1)
            w.norms += 1
            ch.step(nc.vector.memset(pad1[:, :, 0:3], 0.0))

            def qk_tile(i, j):
                dve.wait_ge(s_used, i * 4 + (n0 + j + 1))
                nc.vector.tensor_tensor(tile_at(qk, i * 4 + j), ps[:, 4 * g + j % 4, :], rstd[:, :], ALU.mult).then_inc(s_free, 1)

            each(dve, 8, qk_tile)
            dve.wait_ge(s_used, n0 + U_DT + 1)
            nc.vector.tensor_tensor(dt_raw[:, :], ps[0:SSD_HEADS, 4 * g, :], rstd[0:SSD_HEADS, :], ALU.mult).then_inc(s_free, 1)
            dve.wait_ge(s_free, b0 + U_DT + 5)
            nc.vector.tensor_scalar(dt_raw[:, :], dt_raw[:, :], vec[0:SSD_HEADS, COL["dt_bias"][0]:COL["dt_bias"][0] + 1], None, ALU.add).then_inc(s_dtb, 1)
            dve.wait_ge(s_dtb, 1)

            dve_conv(dve, ch, (n0, b0, g), 12, pad1, cv1, "conv_w", "conv_b", U_XBC, 0)

            def z_tile(i, j):
                dve.wait_ge(s_used, i * 4 + (n0 + j + 1))
                if j - U_Z >= 2:
                    dve.wait_ge(s_zact, i * 4 + (j - U_Z))
                else:
                    dve.wait_ge(s_zact, i * 4 + 1)
                nc.vector.tensor_tensor(z_tmp[:, (j - U_Z) % 2, :], ps[:, 4 * g + j % 4, :], rstd[:, :], ALU.mult).then_inc(s_free, 1)

            each(dve, 8, z_tile, begin=U_Z)
            dve_rstd_columns(dve, w, 1)
            dve.wait_ge(s_rcol, 1)
            dve_tokens_out(dve, w, v_tok)
            dve.wait_ge(s_act, 4)
            ch.link(nc.vector.scalar_tensor_tensor(out=dt_row[:, :], in0=dt_raw[:, :], scalar=0.0, in1=dt_abs[:, :], op0=ALU.max, op1=ALU.add))
            ch.link(nc.vector.tensor_scalar(da_row[:, :], dt_row[:, :], a_neg[:, 0:1], -1.0, ALU.mult, ALU.mult))
            for m in range(NB):
                cols = slice(m * P, (m + 1) * P)
                last = nc.vector.tensor_tensor_scan(cs_row[:, cols], ones[0:SSD_HEADS, :], da_row[:, cols], 0.0, ALU.mult, ALU.add)
            last.then_inc(s_dt, 1)
            dve.wait_ge(s_toepm, 1)
            mids = w.mids
            def scale(pair, j):
                dve.wait_ge(s_scores, pair * 2 + (j + 1))
                if not isinstance(pair, int):
                    dve.wait_ge(s_ptp, pair * 2 + j)
                for ib in range(NB):
                    width = (ib + 1) * P
                    table = toep[:, bass.ds(pair * 2 + j, 1), T - width:T].rearrange("p a t -> p (a t)")
                    last = nc.vector.scalar_tensor_tensor(out=score_row(j, ib), in0=score_bank(ib), scalar=ATT_DIM ** -0.5,
                                                          in1=table, op0=ALU.mult, op1=ALU.add)
                last.then_inc(s_sfree, 1)
                dve.wait_ge(s_sfree, pair * 2 + (j + 2))
                for ib in range(NB):
                    last = nc.vector.tensor_reduce(at_stat[:, j, 1, ib:ib + 1], score_row(j, ib), AX.X, ALU.max)
                ch.link(last)
                nc.vector.tensor_scalar(at_stat[:, j, 0, :], at_stat[:, j, 1, :], -1.0, None, ALU.mult).then_inc(s_max, 1)

            def normalise(pair, j):
                dve.wait_ge(s_exp, pair * 2 + (j + 1))
                ch.link(nc.vector.reciprocal(at_stat[:, j, 2, :], at_stat[:, j, 1, :]))
                for ib in range(NB):
                    last = nc.vector.tensor_scalar(score_row(j, ib), score_row(j, ib), at_stat[:, j, 2, ib:ib + 1], None, ALU.mult)
                last.then_inc(s_pn, 1)

            def pair_of_heads(pair, more):
                normalise(pair, 1)
                if more:
                    scale(pair + 1, 0)
                    normalise(pair + 1, 0)
                dve.wait_ge(s_mhi, pair + (mids + 1))
                nc.vector.tensor_tensor(tile_at(mid_lo, pair + 8), ps[:, 7, :], tile_at(mid_hi, pair + 8).bitcast(F32), ALU.subtract).then_inc(s_mlo, 1)
                if more:
                    scale(pair + 1, 1)

            scale(0, 0)
            scale(0, 1)
            normalise(0, 0)
            with ch.loop(3, 4) as i:
                pair_of_heads(i, True)
            pair_of_heads(3, False)
            w.mids += 4
            dve.wait_ge(s_colp, 1)
            nc.vector.tensor_copy(cols1[:, :, :, :].rearrange("p a b c -> p (a b c)"), ps[:, 4, 0:NB * 32]).then_inc(s_col, 1)
            for g_ in range(2):
                dve.wait_ge(s_cbp, g_ + 1)
                nc.vector.tensor_tensor(cb[:, g_, 0:NB, :], ps[:, 0, :].rearrange("p (a t) -> p a t", a=NB),
                                        mask["upper"].rearrange("p (a t) -> p a t", a=1).to_broadcast([P, NB, P]), ALU.mult).then_inc(s_cb, 1)
            dve.wait_ge(s_totp, 1)
            ch.link(nc.vector.tensor_copy(total_c[:, :, :].rearrange("p a c -> p (a c)"), ps[:, 4, 256:256 + NB * 16]))
            for a in range(NB):
                last = nc.vector.tensor_scalar(bias_c[:, PAIR[a, a], :], cols1[:, a, 0, :], -1.0, None, ALU.mult)
                if a < NB - 1:
                    ch.link(last)
                for ib in range(a + 1, NB):
                    ch.link(nc.vector.tensor_tensor(bias_c[:, PAIR[a, ib], :], bias_c[:, PAIR[a, ib - 1], :], total_c[:, ib - 1, :], ALU.add))
            last.then_inc(s_bias, 1)
            dve.wait_ge(s_xt, 8)
            dve.wait_ge(s_cb2, 2)

            def select(t, column):
                nc.vector.tensor_copy(sel1[:, t % 2, :], column.to_broadcast([16, P])).then_inc(s_sel, 1)

            def exponents(i, t):
                head, slot = bass.ds(i * 4 + t, 1), t % 4
                dve.wait_ge(s_y, i * 4 + (t + 1))
                dve.wait_ge(s_csb, i * 4 + (t + 1))
                for a in range(NB):
                    last = nc.vector.tensor_scalar(decay[:, slot, a, :], ps[:, t % 2, a * P:(a + 1) * P], bias_c[:, PAIR[a, a], head], 0.0,
                                                   ALU.add, ALU.min)
                last.then_inc(s_dmin, 1)
                select(t, const[0:16, 0, bass.ds(i * 4 + (t + 2), 1)])
                ch.step(nc.vector.tensor_tensor(xdt[:, slot, :, :], x_tok[:, :, bass.ds((i * 4 + t) * SSD_DIM, SSD_DIM)],
                                                cols1[:, :, 1, head].to_broadcast([P, NB, SSD_DIM]), ALU.mult))

            def weights(i, t, g_):
                dve.wait_ge(s_dec, i * 4 + (t + 1))
                nc.vector.tensor_tensor(decay[:, t, :, :], decay[:, t, :, :],
                                        cb[:, bass.ds(g_, 1), :, :].rearrange("p g a t -> p (g a) t"), ALU.mult).then_inc(s_m, 1)

            def gate(m, done, slot):
                dve.wait_ge(s_y, done)
                ch.link(nc.vector.scalar_tensor_tensor(out=y_tmp[:, slot, :], in0=tile_at(xs, m), scalar=col_at(vec, m + COL["d_skip"][0]),
                                                       in1=ps[:, 2 + slot, :], op0=ALU.mult, op1=ALU.add))
                nc.vector.tensor_tensor(tile_at(zs, m), y_tmp[:, slot, :], tile_at(zs, m), ALU.mult).then_inc(s_yg, 1)

            def four_heads(i, g_, first=False, last=False):
                for t in range(4):
                    if not (last and t == 3):
                        exponents(i, t + 1)
                    if t == 1 and not first:
                        gate(i * 2 - 1, i * 4 + Y0, 1)
                    if t == 3:
                        gate(i * 2, i * 4 + (2 + Y0), 0)
                    weights(i, t, g_)

            select(0, ident[0:16, 0:1])
            select(1, ident[0:16, 1:2])
            exponents(0, 0)
            four_heads(0, 0, first=True)
            with ch.loop(2, 6) as i:
                four_heads(i + 1, i)
            four_heads(3, 1, last=True)
            gate(7, 16 + Y0, 1)
            for m in range(8):
                dve.wait_ge(s_ysq, m + 1)
                if m == 0:
                    nc.vector.tensor_copy(sum_sq[:, :], sq[:, 0, :]).then_inc(s_ysum, 1)
                else:
                    dve.wait_ge(s_ysum, m)
                    nc.vector.tensor_tensor(sum_sq[:, :], sum_sq[:, :], sq[:, m % 2, :], ALU.add).then_inc(s_ysum, 1)
            dve.wait_ge(s_yrstd, 1)
            c = COL["ssd_norm"][0]
            for m in range(8):
                nc.vector.scalar_tensor_tensor(out=zs[:, m, :], in0=zs[:, m, :], scalar=vec[:, c + m:c + m + 1], in1=rstd[:, :],
                                               op0=ALU.mult, op1=ALU.mult).then_inc(s_yn, 1)
                if m:
                    dve_lo_y(dve, w, m - 1, zs)
            dve_lo_y(dve, w, 7, zs)
            for side in range(2):
                dve_add_to_h(dve, w, 6, side, 1.0, gain)

        def dve_lo_y(dve, w, m, src):
            dve.wait_ge(s_mhi, w.mids + 1)
            nc.vector.tensor_tensor(mid_lo[:, m, :], src[:, m, :], mid_hi[:, m, :].bitcast(F32), ALU.subtract).then_inc(s_mlo, 1)
            w.mids += 1

        def pool_mixer1(pool, w):
            pool.wait_ge(s_toep, 16)
            nc.gpsimd.memset(toep[0:64, :, T - 64:T], MASKED).then_inc(s_toepm, 1)
            pool.wait_ge(s_free, w.bank + 4)
            def stage_qk(pair):
                nc.gpsimd.tensor_copy(at_q[:, :], tile_at(qk, pair)).then_inc(s_stage, 1)
                nc.gpsimd.tensor_copy(at_k[:, :], tile_at(qk, pair + 4)).then_inc(s_stage, 1)

            def stage_v(pair):
                cols = slice(pair * P, (pair + 1) * P) if isinstance(pair, int) else bass.ds(pair * P, P)
                nc.gpsimd.tensor_copy(at_v[:, :, :], v_tok[:, :, cols]).then_inc(s_stage, 1)

            stage_qk(0)
            stage_v(0)
            with pool.Fori(0, 3) as i:
                pool.wait_ge(s_scores, i * 2 + 2)
                pool.sem_inc(s_tick["pool"], 1)
                stage_qk(i + 1)
                pool.wait_ge(s_o, i * 2 + 3)
                pool.sem_inc(s_tick["pool"], 1)
                stage_v(i + 1)

        s_tsq = sem("tile_squares_by_pool")
        s_tsq2 = sem("tile_squares_by_vector")
        s_tsum = sem("tile_sums")
        s_tln = sem("tile_log_variances")
        s_trs = sem("tile_rstds")
        s_tn = sem("tiles_normed")

        def pool_tile_norm(pool, w, src):
            for n in (w.batches, w.batches + 1):
                if n >= 2:
                    pool.wait_ge(s_tsum, n - 1)
                for t in range(2):
                    tile = src[:, 4 * (n % 2) + t, :]
                    nc.gpsimd.tensor_tensor(nrm_sq[:, n % 2, t, :], tile, tile, ALU.mult).then_inc(s_tsq, 1)
            w.batches += 2

        def pe_tile_norm(pe, w):
            for n in (w.batches, w.batches + 1):
                for t in range(4):
                    if t < 2:
                        pe.wait_ge(s_tsq, 2 * n + t + 1)
                    else:
                        pe.wait_ge(s_tsq2, 2 * n + t - 1)
                    if t == 0 and n >= 2:
                        pe.wait_ge(s_tln, n - 1)
                    last = nc.tensor.matmul(ps[:, 4 * (n % 2) + t, :], ones, nrm_sq[:, n % 2, t, :], start=True, stop=True)
                last.then_inc(s_tsum, 1)
            w.batches += 2

        def act_tile_norm(act, w, scale, bias):
            both = (w.batches, w.batches + 1)
            for n in both:
                act.wait_ge(s_tsum, n + 1)
                if n >= 2:
                    act.wait_ge(s_tn, 4 * (n - 1))
                nc.scalar.activation(nrm[:, n % 2, :, :], ps[:, 4 * (n % 2):4 * (n % 2) + 4, :], ACT.Ln, bias=bias, scale=scale).then_inc(s_tln, 1)
            for n in both:
                act.wait_ge(s_tln, n + 1)
                nc.scalar.activation(nrm[:, n % 2, :, :], nrm[:, n % 2, :, :], ACT.Exp, scale=-0.5).then_inc(s_trs, 1)
            w.batches += 2

        def dve_tile_squares(dve, w, src):
            for n in (w.squared, w.squared + 1):
                if n >= 2:
                    dve.wait_ge(s_tsum, n - 1)
                for t in range(2, 4):
                    tile = src[:, 4 * (n % 2) + t, :]
                    nc.vector.tensor_tensor(nrm_sq[:, n % 2, t, :], tile, tile, ALU.mult).then_inc(s_tsq2, 1)
            w.squared += 2

        def dve_tile_norm(dve, w, ch, src, gain=None, factor=None):
            for n in (w.batches, w.batches + 1):
                dve.wait_ge(s_trs, n + 1)
                for t in range(4):
                    m = 4 * (n % 2) + t
                    if gain is None:
                        last = nc.vector.tensor_tensor(src[:, m, :], src[:, m, :], nrm[:, n % 2, t, :], ALU.mult)
                    else:
                        last = nc.vector.scalar_tensor_tensor(out=src[:, m, :], in0=src[:, m, :], scalar=vec[:, COL[gain][0]:COL[gain][0] + 1],
                                                              in1=nrm[:, n % 2, t, :], op0=ALU.mult, op1=ALU.mult)
                    if factor is not None:
                        ch.link(last)
                        last = nc.vector.tensor_tensor(src[:, m, :], src[:, m, :], factor[:, m, :], ALU.mult)
                    last.then_inc(s_tn, 1)
                    if factor is not None and m:
                        dve_lo_y(dve, w, m - 1, src)
            if factor is not None:
                dve_lo_y(dve, w, 7, src)
            w.batches += 2

        U_AB, U_GATE, U_END2 = 24, 25, 33
        s_ga = sem("decay_inputs_biased")
        s_ga2 = sem("decay_and_beta_rows")
        s_gateact = sem("gate2_activated")
        s_gcolp = sem("gdn_columns_in_psum")
        s_gcol = sem("gdn_columns")
        s_gtot = sem("gdn_totals_in_psum")
        s_gcd = sem("gdn_log_columns")
        s_gce = sem("gdn_exp_columns")
        s_gcb = sem("gdn_all_columns")
        s_gst = sem("gdn_staged")
        s_gsel = sem("gdn_selectors")
        s_gbc = sem("gdn_broadcasts")
        s_gem = sem("gdn_decays")
        s_gkb = sem("gdn_beta_k")
        s_gmm = sem("gdn_products")
        s_gin = sem("gdn_a_ready")
        s_gqk = sem("gdn_qk_ready")
        s_gkv = sem("gdn_k_and_v_by_token")
        s_gtt = sem("gdn_first_inverse_t")
        s_gtmp = sem("gdn_first_inverse_in_psum")
        s_gtm = sem("gdn_first_inverse")
        s_gao = sem("gdn_off_blocks")
        s_gup = sem("gdn_u_in_psum")
        s_gu = sem("gdn_u")
        s_gdp = sem("gdn_update_in_psum")
        s_gd = sem("gdn_inverse_updated")
        s_guw = sem("gdn_uw_in_psum")
        s_guwc = sem("gdn_uw")
        s_gva = sem("gdn_w_state")
        s_gvn = sem("gdn_v_new")
        s_gop = sem("gdn_state_update_in_psum")
        s_gs = sem("gdn_state")
        s_gop2 = sem("gdn_out_in_psum")
        s_go = sem("gdn_out")

        def pe_mixer2(pe, w):
            w.tiles += DK
            pe_column_layer(pe, w, U_END2, lambda bank: pe_norm_sum(pe, w, bank))
            w.norms += 1
            pe.wait_ge(s_free, w.bank + 4)
            pe_keep_warm(7, 3)
            pe_tile_norm(pe, w)
            pe_tile_norm(pe, w)
            pe.wait_ge(s_ga2, 2)
            pe.wait_ge(s_tln, w.batches)
            pe_keep_warm(7, 6)
            for m in range(NB):
                last = nc.tensor.transpose(ps[:, 0, m * 64:m * 64 + 40], g_row[:, m * P:(m + 1) * P], ident[0:40, 0:40])
            last.then_inc(s_gcolp, 1)
            pe.wait_ge(s_gcol, 1)
            nc.tensor.matmul(ps[:, 1, 0:32], ident[:, P - 1:P].to_broadcast([P, P]), cols2[:, :, 0:8], start=True, stop=True).then_inc(s_gtot, 1)
            pe.wait_ge(s_gcb, 1)
            with pe.Fori(0, 4) as i:
                for j in range(2):
                    b = 4 * j
                    pe.wait_ge(s_gsel, i * 2 + (j + 1))
                    pe.wait_ge(s_go, i * 2 + 1)
                    nc.tensor.matmul(ps[:, b, :], gw["sel"][j][:, 0, :], g_row[:, :], start=True, stop=True)
                    nc.tensor.matmul(ps[:, b + 1, :], gw["sel"][j][:, 1, :], g_row[:, :], start=True, stop=True).then_inc(s_gbc, 1)
                for j in range(2):
                    b = 4 * j
                    pe.wait_ge(s_gst, i * 4 + (2 * j + 2))
                    for c in range(NB):
                        ks = gw["k_st"][j][:, c, :]
                        nc.tensor.matmul(ps[:, b + 2, c * P:(c + 1) * P], ks, qk2[:, bass.ds(i * 2 + j, 1), c * P:(c + 1) * P].rearrange("p a t -> p (a t)"), start=True, stop=True)
                        nc.tensor.transpose(ps[:, b + 3, c * P:(c + 1) * P], ks, ident)
                    pe.wait_ge(s_gem, i * 2 + (j + 1))
                    for c in range(NB):
                        nc.tensor.transpose(ps[:, b, c * P:(c + 1) * P], v_st[:, j, c * P:(c + 1) * P], ident)
                    pe.wait_ge(s_gkb, i * 2 + (j + 1))
                    for c in range(NB):
                        last = nc.tensor.matmul(ps[:, b + 1, c * P:(c + 1) * P], gw["k_st"][j][:, c, :], gw["ao"][j][:, c, :], start=True, stop=True)
                    last.then_inc(s_gmm, 1)
                for n_ in range(6):
                    for j in range(2):
                        if n_ == 0:
                            pe.wait_ge(s_gtt, i * 2 + (j + 1))
                        else:
                            pe.wait_ge(s_gd, i * 12 + (2 * n_ - 2 + j + 1))
                        for c in range(NB):
                            last = nc.tensor.transpose(ps[:, 4 * j + 1, c * P:(c + 1) * P], gw["tt"][j][:, c, :], ident)
                        last.then_inc(s_gtmp, 1)
                    for j in range(2):
                        b = 4 * j
                        pe.wait_ge(s_gao, i * 12 + (2 * n_ + j + 1))
                        pe.wait_ge(s_gtm, i * 12 + (2 * n_ + j + 1))
                        for c in range(NB):
                            last = nc.tensor.matmul(ps[:, b + 1, c * P:(c + 1) * P], gw["ao"][j][:, c, :], gw["tm"][j][:, c, :], start=True, stop=True)
                        last.then_inc(s_gup, 1)
                    for j in range(2):
                        b = 4 * j
                        pe.wait_ge(s_gu, i * 12 + (2 * n_ + j + 1))
                        if n_ == 0:
                            pe.wait_ge(s_gkv, i * 2 + (j + 1))
                        for c in range(NB):
                            cols = slice(c * P, (c + 1) * P)
                            last = nc.tensor.matmul(ps[:, b + 3, cols], gw["u_"][j][:, c, :], gw["tt"][j][:, c, :], start=True, stop=True)
                        last.then_inc(s_gdp, 1)
                for j in range(2):
                    b = 4 * j
                    pe.wait_ge(s_gd, i * 12 + (10 + j + 1))
                    for c in range(NB):
                        cols = slice(c * P, (c + 1) * P)
                        nc.tensor.matmul(ps[:, b, cols], gw["tt"][j][:, c, :], gw["vb"][j][:, c, :], start=True, stop=True)
                        last = nc.tensor.matmul(ps[:, b + 1, cols], gw["kb"][j][:, c, :], gw["tt"][j][:, c, :], start=True, stop=True)
                    last.then_inc(s_guw, 1)
                for c in range(NB):
                    cols = slice(c * P, (c + 1) * P)
                    for j in range(2):
                        b = 4 * j
                        if c == 0 and j == 0:
                            pe.wait_ge(s_guwc, i * 2 + 2)
                            pe.wait_ge(s_gqk, i * 2 + 2)
                        if c:
                            pe.wait_ge(s_gs, i * 6 + (2 * (c - 1) + j + 1))
                            nc.tensor.matmul(ps[:, b + 2, 0:P], gw["wt"][j][:, c, :], gw["st"][j][:, :], start=True, stop=True).then_inc(s_gva, 1)
                    for j in range(2):
                        b = 4 * j
                        vn = gw["vn"][j][:, :]
                        if c == 0:
                            vn = gw["uu"][j][:, 0, :]
                            last = nc.tensor.matmul(ps[:, b + 3, cols], vn, gw["qkt"][j][:, c, :], start=True, stop=True)
                        else:
                            nc.tensor.matmul(ps[:, b + 3, cols], gw["st"][j][:, :], gw["qd"][j][:, c, :], start=True, stop=False)
                            pe.wait_ge(s_gvn, i * 6 + (2 * (c - 1) + j + 1))
                            last = nc.tensor.matmul(ps[:, b + 3, cols], vn, gw["qkt"][j][:, c, :], start=False, stop=True)
                        if c < NB - 1:
                            nc.tensor.matmul(ps[:, b + 2, P:2 * P], gw["kd"][j][:, c, :], vn, start=True, stop=True).then_inc(s_gop, 1)
                        else:
                            last.then_inc(s_gop2, 1)
            pe.wait_ge(s_go, 9)
            pe_keep_warm(7, 3)
            pe_tile_norm(pe, w)
            mids = w.mids
            for side in range(2):
                pe_square_half(pe, w, 8, lambda k: (mid_hi[:, k, :], mid_lo[:, k, :]), lambda k: pe.wait_ge(s_mlo, mids + k + 1))
            w.mids += 8

        def act_mixer2(act, w, gain):
            n0, b0, g = w.column_layer(U_END2)
            act_ahead(act, n0, 0, 0)
            act_rstd(act, w, 4 * (g ^ 1), EPS_2)

            def conv_tile(dest, t0):
                def body(i, j):
                    if j > 0:
                        act_ahead(act, n0, i, j)
                    act.wait_ge(s_conv, i * 4 + (12 + j + 1))
                    nc.scalar.activation(tile_at(dest, i * 4 + (j - t0)), cv2[:, j % 2, :], ACT.Silu).then_inc(s_convact, 1)
                return body

            each(act, 16, conv_tile(qk2, 0), first=4)
            each(act, 8, conv_tile(v2, 16), begin=16)
            act_ahead(act, n0, 0, U_AB)

            def gate_tile(i, j):
                act_ahead(act, n0, i, j)
                act.wait_ge(s_free, i * 4 + (b0 + j + 5))
                nc.scalar.activation(tile_at(gate2, i * 4 + (j - U_GATE)), g_tmp[:, (j - U_GATE) % 2, :], ACT.Silu).then_inc(s_gateact, 1)

            each(act, 8, gate_tile, begin=U_GATE)
            ch = w.act_steps
            act.wait_ge(s_ga, 1)
            ch.link(nc.scalar.activation(ga[0:8, 1, :], ga[0:8, 0, :], ACT.Abs))
            ch.link(nc.scalar.activation(ga[0:8, 1, :], ga[0:8, 1, :], ACT.Exp, scale=-1.0))
            ch.step(nc.scalar.activation(ga[0:8, 1, :], ga[0:8, 1, :], ACT.Ln, bias=1.0))
            ch.step(nc.scalar.activation(a_neg2[:, :], vec[0:8, COL["gdn_a_log"][0]:COL["gdn_a_log"][0] + 1], ACT.Exp))
            assert ch.n == SOFTPLUS_2
            nc.scalar.activation(g_row[32:40, :], ga[32:40, 0, :], ACT.Sigmoid).then_inc(s_ga2, 1)
            act_tile_norm(act, w, 128.0, 128.0 * EPS_2)
            act_tile_norm(act, w, 1.0, EPS_2)
            act.wait_ge(s_gcd, 1)
            nc.scalar.activation(g_dec[:, :, :], g_dec[:, :, :], ACT.Exp).then_inc(s_gce, 1)
            nc.scalar.activation(g_exp[:, :, :], cols2[:, :, 0:8], ACT.Exp).then_inc(s_gce, 1)

            def turn(i, n_, j):
                act.wait_ge(s_gtmp, i * 12 + (2 * n_ + j + 1))
                nc.scalar.activation(gw["tm"][j][:, :, :].rearrange("p a t -> p (a t)"), ps[:, 4 * j + 1, :], ACT.Copy).then_inc(s_gtm, 1)

            with ch.loop(4, 2) as i:
                for j in range(2):
                    act.wait_ge(s_gbc, i * 2 + (j + 1))
                    nc.scalar.activation(gw["eg"][j][:, :, :].rearrange("p a t -> p (a t)"), ps[:, 4 * j, :], ACT.Exp)
                    for c in range(NB):
                        last = nc.scalar.activation(gw["em"][j][:, c, :], ps[:, 4 * j, c * P:(c + 1) * P], ACT.Relu,
                                                    bias=cols2[:, c, bass.ds(i * 2 + j, 1)], scale=-1.0)
                    ch.link(last)
                    em = gw["em"][j][:, :, :].rearrange("p a t -> p (a t)")
                    nc.scalar.activation(em, em, ACT.Exp, scale=-1.0).then_inc(s_gem, 1)
                for j in range(2):
                    act.wait_ge(s_gmm, i * 2 + (j + 1))
                    head, beta = bass.ds(i * 2 + j, 1), bass.ds(i * 2 + (32 + j), 1)
                    for c in range(NB):
                        cols = slice(c * P, (c + 1) * P)
                        nc.scalar.activation(gw["kb"][j][:, c, :], ps[:, 4 * j + 3, cols], ACT.Copy, scale=g_exp[:, c, head])
                        nc.scalar.activation(gw["kd"][j][:, c, :], ps[:, 4 * j + 3, cols], ACT.Copy, scale=g_dec[:, c, head])
                        last = nc.scalar.activation(gw["vb"][j][:, c, :], ps[:, 4 * j, cols], ACT.Copy, scale=cols2[:, c, beta])
                    last.then_inc(s_gkv, 1)
                    turn(i, 0, j)
                for n_ in range(6):
                    for j in range(2):
                        if n_:
                            turn(i, n_, j)
                    for j in range(2):
                        act.wait_ge(s_gup, i * 12 + (2 * n_ + j + 1))
                        nc.scalar.activation(gw["u_"][j][:, :, :].rearrange("p a t -> p (a t)"), ps[:, 4 * j + 1, :], ACT.Copy).then_inc(s_gu, 1)
                for j in range(2):
                    act.wait_ge(s_guw, i * 2 + (j + 1))
                    nc.scalar.activation(gw["uu"][j][:, :, :].rearrange("p a t -> p (a t)"), ps[:, 4 * j, :], ACT.Copy)
                    nc.scalar.activation(gw["wt"][j][:, :, :].rearrange("p a t -> p (a t)"), ps[:, 4 * j + 1, :], ACT.Copy).then_inc(s_guwc, 1)
                for j in range(2):
                    act.wait_ge(s_gop2, i * 2 + (j + 1))
                    nc.scalar.activation(tile_at(v2, i * 2 + j), ps[:, 4 * j + 3, :], ACT.Copy).then_inc(s_go, 1)
            act.wait_ge(s_go, 9)
            act_tile_norm(act, w, 1.0 / P, EPS_2)
            for m in range(8):
                act.wait_ge(s_tn, 4 * w.batches - 8 + m + 1)
                nc.scalar.activation(mid_hi[:, m, :], v2[:, m, :], ACT.Copy).then_inc(s_mhi, 1)
            w.mids += 8
            for side in range(2):
                layer = w.square_layer(4)
                for kp in range(4):
                    act_ahead(act, layer[0], 0, kp)
                act_prep(act, w, range(4 * side, 4 * side + 4), gain, lambda m: act.wait_ge(s_free, layer[1] + m % 4 + 5))

        def dve_mixer2(dve, w, ch, gain):
            n0, b0, g = w.column_layer(U_END2)
            dve.wait_ge(s_rstd, w.norms + 1)
            w.norms += 1
            ch.step(nc.vector.memset(pad2[:, :, 0:3], 0.0))
            ch.step(nc.vector.memset(g_row[:, :], 0.0))
            dve_conv(dve, ch, (n0, b0, g), 24, pad2, cv2, "gdn_conv", None, 0, 12)
            dve.wait_ge(s_used, n0 + U_AB + 1)
            nc.vector.tensor_tensor(ga[:, 0, :], ps[0:40, 4 * g + U_AB % 4, :], rstd[0:40, :], ALU.mult).then_inc(s_free, 1)
            dve.wait_ge(s_free, b0 + U_AB + 5)
            nc.vector.tensor_scalar(ga[0:8, 0, :], ga[0:8, 0, :], vec[0:8, COL["gdn_dt_bias"][0]:COL["gdn_dt_bias"][0] + 1], None, ALU.add).then_inc(s_ga, 1)
            dve.wait_ge(s_ga, 1)

            def gate_tile(i, j):
                dve.wait_ge(s_used, i * 4 + (n0 + j + 1))
                dve.wait_ge(s_gateact, i * 4 + max(j - U_GATE, 1))
                nc.vector.tensor_tensor(g_tmp[:, (j - U_GATE) % 2, :], ps[:, 4 * g + j % 4, :], rstd[:, :], ALU.mult).then_inc(s_free, 1)

            each(dve, 8, gate_tile, begin=U_GATE)
            dve.wait_ge(s_act, SOFTPLUS_2)
            ch.link(nc.vector.scalar_tensor_tensor(out=ga[0:8, 2, :], in0=ga[0:8, 0, :], scalar=0.0, in1=ga[0:8, 1, :], op0=ALU.max, op1=ALU.add))
            ch.link(nc.vector.tensor_scalar(ga[0:8, 2, :], ga[0:8, 2, :], a_neg2[:, 0:1], -1.0, ALU.mult, ALU.mult))
            for m in range(NB):
                cols = slice(m * P, (m + 1) * P)
                last = nc.vector.tensor_tensor_scan(g_row[0:8, cols], ones[0:8, :], ga[0:8, 2, cols], 0.0, ALU.mult, ALU.add)
            last.then_inc(s_ga2, 1)
            dve.wait_ge(s_free, w.bank + 4)
            dve.wait_ge(s_convact, 37)
            dve_tile_squares(dve, w, qk2[:, 0:8, :])
            dve_tile_squares(dve, w, qk2[:, 8:16, :])
            dve_tile_norm(dve, w, ch, qk2[:, 0:8, :])
            dve_tile_norm(dve, w, ch, qk2[:, 8:16, :])
            dve.wait_ge(s_gcolp, 1)
            nc.vector.tensor_copy(cols2[:, :, :], ps[:, 0, 0:256].rearrange("p (a c) -> p a c", a=NB)[:, :, 0:40]).then_inc(s_gcol, 1)
            dve.wait_ge(s_gcol, 1)
            dve.wait_ge(s_gtot, 1)
            nc.vector.tensor_tensor(g_dec[:, :, :], ps[:, 1, 0:32].rearrange("p (a c) -> p a c", a=NB), cols2[:, :, 0:8], ALU.subtract).then_inc(s_gcd, 1)
            dve.wait_ge(s_gce, 2)
            nc.vector.tensor_tensor(g_exp[:, :, :], g_exp[:, :, :], cols2[:, :, 32:40], ALU.mult).then_inc(s_gcb, 1)
            dve.wait_ge(s_gcb, 1)
            wide = [P, NB, P]
            upper = mask["upper"].rearrange("p (a t) -> p a t", a=1).to_broadcast(wide)
            merge1 = mask["merge1"].rearrange("p (a t) -> p a t", a=1).to_broadcast(wide)
            eye = ident.rearrange("p (a t) -> p a t", a=1).to_broadcast(wide)

            def bank(b):
                return ps[:, b, :].rearrange("p (a t) -> p a t", a=NB)

            with ch.loop(4, 4) as i:
                for j in range(2):
                    dve.wait_ge(s_go, i * 2 + 1)
                    nc.vector.tensor_copy(gw["sel"][j][:, 0, :], const[0:40, 0, bass.ds(i * 2 + j, 1)].to_broadcast([40, P]))
                    nc.vector.tensor_copy(gw["sel"][j][:, 1, :], const[0:40, 0, bass.ds(i * 2 + (32 + j), 1)].to_broadcast([40, P])).then_inc(s_gsel, 1)
                for j in range(2):
                    dve.wait_ge(s_gbc, i * 2 + (j + 1))
                    nc.vector.tensor_tensor(gw["ao"][j][:, :, :].rearrange("p a t -> p (a t)"), ps[:, 4 * j + 1, :], tile_at(qk2, i * 2 + (8 + j)), ALU.mult).then_inc(s_gkb, 1)
                    dve.wait_ge(s_gem, i * 2 + (j + 1))
                    ch.step(nc.vector.tensor_tensor(gw["em"][j][:, :, :], gw["em"][j][:, :, :], upper, ALU.mult))
                    nc.vector.tensor_tensor(gw["qd"][j][:, :, :].rearrange("p a t -> p (a t)"), gw["eg"][j][:, :, :].rearrange("p a t -> p (a t)"), tile_at(qk2, i * 2 + j), ALU.mult)
                for j in range(2):
                    dve.wait_ge(s_gmm, i * 2 + (j + 1))
                    ch.wait()
                    nc.vector.tensor_tensor(gw["at"][j][:, :, :], bank(4 * j + 1), gw["em"][j][:, :, :], ALU.mult).then_inc(s_gin, 1)
                    dve.wait_ge(s_gin, i * 2 + (j + 1))
                    ch.link(nc.vector.tensor_tensor(gw["tm"][j][:, :, :], gw["at"][j][:, :, :], merge1, ALU.mult))
                    nc.vector.tensor_tensor(gw["tt"][j][:, :, :], eye, gw["tm"][j][:, :, :], ALU.subtract).then_inc(s_gtt, 1)
                for j in range(2):
                    nc.vector.tensor_tensor(gw["qkt"][j][:, :, :], bank(4 * j + 2), gw["em"][j][:, :, :], ALU.mult).then_inc(s_gqk, 1)
                for n_ in range(6):
                    for j in range(2):
                        dve.wait_ge(s_gdp, i * 12 + (2 * n_ + j + 1))
                        if n_ == 0:
                            dve.wait_ge(s_gtt, i * 2 + (j + 1))
                        else:
                            dve.wait_ge(s_gd, i * 12 + (2 * n_ - 2 + j + 1))
                        nc.vector.tensor_tensor(gw["tt"][j][:, :, :], gw["tt"][j][:, :, :], bank(4 * j + 3), ALU.subtract).then_inc(s_gd, 1)
                for c in range(NB):
                    for j in range(2):
                        b = 4 * j
                        if c:
                            dve.wait_ge(s_gva, i * 6 + (2 * (c - 1) + j + 1))
                            nc.vector.tensor_tensor(gw["vn"][j][:, :], gw["uu"][j][:, c, :], ps[:, b + 2, 0:P], ALU.subtract).then_inc(s_gvn, 1)
                    for j in range(2):
                        b = 4 * j
                        if c < NB - 1:
                            dve.wait_ge(s_gop, i * 6 + (2 * c + j + 1))
                            if c == 0:
                                nc.vector.tensor_copy(gw["st"][j][:, :], ps[:, b + 2, P:2 * P]).then_inc(s_gs, 1)
                            else:
                                dve.wait_ge(s_gs, i * 6 + (2 * (c - 1) + j + 1))
                                nc.vector.scalar_tensor_tensor(out=gw["st"][j][:, :], in0=gw["st"][j][:, :], scalar=gw["eg"][j][:, c, P - 1:P],
                                                               in1=ps[:, b + 2, P:2 * P], op0=ALU.mult, op1=ALU.add).then_inc(s_gs, 1)
            dve.wait_ge(s_go, 9)
            dve_tile_squares(dve, w, v2)
            dve_tile_norm(dve, w, ch, v2, "gdn_norm", gate2)
            for side in range(2):
                dve_add_to_h(dve, w, 4, side, 1.0, gain)

        def pool_mixer2(pool, w):
            pool.wait_ge(s_free, w.bank + 4)
            pool.wait_ge(s_convact, w.convs + 1)
            pool_tile_norm(pool, w, qk2[:, 0:8, :])
            pool_tile_norm(pool, w, qk2[:, 8:16, :])
            pool.wait_ge(s_tn, 4 * w.batches)

            def stage(pair):
                for j in range(2):
                    k_head, v_head = (qk2[:, 8 + 2 * pair + j, :], v2[:, 2 * pair + j, :]) if isinstance(pair, int) else \
                                     (tile_at(qk2, pair * 2 + (8 + j)), tile_at(v2, pair * 2 + j))
                    nc.gpsimd.tensor_copy(gw["k_st"][j][:, :, :].rearrange("p a t -> p (a t)"), k_head).then_inc(s_gst, 1)
                    nc.gpsimd.tensor_copy(v_st[:, j, :], v_head).then_inc(s_gst, 1)

            def levels(i):
                for n_ in range(6):
                    level = mask[f"merge{2 << n_}"].rearrange("p (a t) -> p a t", a=1).to_broadcast([P, NB, P])
                    for j in range(2):
                        if n_ == 0:
                            pool.wait_ge(s_gtt, i * 2 + (j + 1))
                        else:
                            pool.wait_ge(s_gup, i * 12 + (2 * n_ - 2 + j + 1))
                        nc.gpsimd.tensor_tensor(gw["ao"][j][:, :, :], gw["at"][j][:, :, :], level, ALU.mult).then_inc(s_gao, 1)

            stage(0)
            with pool.Fori(0, 3) as i:
                levels(i)
                stage(i + 1)
            levels(3)

        s_gact = sem("embedding_gate_activated")

        def pe_embed(pe, w):
            for side in range(2):
                plo = w.plo
                pe_square_half(pe, w, 2, lambda k: (mid_hi[:, 10 + k, :], mid_lo[:, 10 + k, :]), lambda k: pe.wait_ge(s_plo, plo + k + 1))
            w.plo += 2
            w.tiles += DK
            pe_column_layer(pe, w, 8, lambda bank: pe_norm_sum(pe, w, bank))
            w.norms += 1

        def act_embed(act, w, gain):
            act.wait_ge(s_p, 16 * (w.plo // 2 + 1))
            for k in range(2):
                nc.scalar.activation(mid_hi[:, 10 + k, :], p_f[:, k, :], ACT.Copy).then_inc(s_phi, 1)
            w.plo += 2
            for side in range(2):
                layer = w.square_layer(1)
                act_ahead(act, layer[0], 0, 0)
            n0, b0, g = w.column_layer(8)
            act_ahead(act, n0, 0, 0)
            act_rstd(act, w, 4 * (g ^ 1), EPS_2)
            for u in range(8):
                if u:
                    act_ahead(act, n0, 0, u)
                act.wait_ge(s_free, b0 + u + 5)
                nc.scalar.activation(ff_gate[:, u % 2, :], ff_gate[:, u % 2, :], ACT.Sigmoid).then_inc(s_gact, 1)
            if gain is not None:
                act.wait_ge(s_used, n0 + 8)
                act_prep(act, w, range(8), gain, lambda m: act.wait_ge(s_hup, w.hups + m + 1))
            w.hups += 8

        def dve_embed(dve, w, ch, gain):
            dve.wait_ge(s_phi, w.plo + 2)
            for k in range(2):
                nc.vector.tensor_tensor(mid_lo[:, 10 + k, :], p_f[:, k, :], mid_hi[:, 10 + k, :].bitcast(F32), ALU.subtract).then_inc(s_plo, 1)
            w.plo += 2
            for side in range(2):
                layer = w.square_layer(1)
                for m in range(4):
                    wait_square(dve, layer, 1, m)
                    nc.vector.tensor_copy(p_part[:, 4 * side + m, :], ps[:, 4 * layer[2] + m, :]).then_inc(s_free, 1)
            n0, b0, g = w.column_layer(8)
            dve.wait_ge(s_rstd, w.norms + 1)
            w.norms += 1
            for u in range(8):
                dve.wait_ge(s_used, n0 + u + 1)
                nc.vector.tensor_tensor(ff_gate[:, u % 2, :], ps[:, 4 * g + u % 4, :], rstd[:, :], ALU.mult).then_inc(s_free, 1)
                dve.wait_ge(s_gact, (w.plo // 2 - 1) * 8 + u + 1)
                ch.link(nc.vector.tensor_tensor(ff_gate[:, u % 2, :], ff_gate[:, u % 2, :], p_part[:, u, :], ALU.mult))
                nc.vector.tensor_tensor(h[:, u, :], h[:, u, :], ff_gate[:, u % 2, :], ALU.add).then_inc(s_hup, 1)
            if gain is not None:
                dve_prep(dve, w, range(8), gain)
            w.hups += 8

        s_sstk = sem("sb_keys_staged")
        s_sstv = sem("sb_values_staged")
        s_sz = sem("sb_scores")
        s_ssp = sem("sb_softplus")
        s_sln = sem("sb_steps")
        s_slw = sem("sb_log_weights")
        s_sw = sem("sb_weights")
        s_swc = sem("sb_diagonal_clamped")
        s_swm = sem("sb_weights_masked")
        s_so = sem("sb_out")

        def pe_mixer3(pe, w):
            w.tiles += DK
            pe_column_layer(pe, w, 8, lambda bank: pe_norm_sum(pe, w, bank))
            w.norms += 1
            pe_rstd_columns(pe, w)
            pe.wait_ge(s_rcol, 2)
            pe_square_tokens(pe, w)
            pe_square_tokens(pe, w)
            w.tiles += DK
            pe_column_layer(pe, w, 8)
            pe.wait_ge(s_free, w.bank + 4)
            pe_keep_warm(7, 3)
            pe_tile_norm(pe, w)
            pe_tile_norm(pe, w)
            pe.wait_ge(s_tln, w.batches)
            pe_keep_warm(7, 8)
            with pe.Fori(0, 4) as i:
                for j in range(2):
                    b = 3 * j
                    q_ = lambda lo_, hi_: q3[:, bass.ds(i * 2 + j, 1), lo_ * P:hi_ * P].rearrange("p a t -> p (a t)")
                    pe.wait_ge(s_sstk, i * 2 + (j + 1))
                    pe.wait_ge(s_sw, i * 2 + 1)
                    for a in range(NB - 1):
                        bk, at = divmod(b * T + OFF[a] * P, T)
                        nc.tensor.matmul(ps[:, bk, at:at + (NB - 1 - a) * P], sb_k[:, j, a * P:(a + 1) * P], q_(a + 1, NB),
                                         start=(a != 2), stop=False, skip_group_check=True)
                    for a in range(NB):
                        last = nc.tensor.matmul(ps[:, b, a * P:(a + 1) * P], sb_k[:, j, a * P:(a + 1) * P], q_(a, a + 1),
                                                start=(a == 0), stop=False, skip_group_check=True)
                    last.then_inc(s_sz, 1)
                pe.wait_ge(s_mlo, i * 2 + w.mids)
                pe_keep_warm(6, 4)
                for j in range(2):
                    pe.wait_ge(s_ssp, i * 2 + (j + 1))
                    for name, src, dst, n_ in sb_pairs():
                        bk, at = divmod(3 * j * T + dst * P, T)
                        last = nc.tensor.matmul(ps[:, bk, at:at + n_ * P], mask[name], sb_sp[:, j, src:src + n_, :],
                                                start=False, stop=True, skip_group_check=True)
                    last.then_inc(s_slw, 1)
                pe_keep_warm(7, 2)
                for j in range(2):
                    pe.wait_ge(s_swm, i * 2 + (j + 1))
                    pe.wait_ge(s_sstv, i * 2 + (j + 1))
                    for a in range(NB - 1):
                        nc.tensor.matmul(ps[:, 6 + j, a * P:(a + 1) * P], sb_v[:, j, a, :], sb_l[:, j, a, :],
                                         start=(a == 0), stop=False, skip_group_check=True)
                        nc.tensor.matmul(ps[:, 6 + j, (a + 1) * P:T], sb_v[:, j, a, :], sb_l[:, j, OFF[a]:OFF[a] + NB - 1 - a, :],
                                         start=False, stop=False, skip_group_check=True)
                    nc.tensor.matmul(ps[:, 6 + j, (NB - 1) * P:T], sb_v[:, j, NB - 1, :], sb_l[:, j, NB - 1, :],
                                     start=False, stop=True, skip_group_check=True).then_inc(s_so, 1)
            mids = w.mids
            for side in range(2):
                pe_square_half(pe, w, 8, lambda k: (mid_hi[:, k, :], mid_lo[:, k, :]), lambda k: pe.wait_ge(s_mlo, mids + k + 1))
            w.mids += 8

        def sb_pairs():
            terms = []
            for a in range(NB):
                terms.append(("neg_tri", a, a, 1))
                if a < NB - 1:
                    terms.append(("neg_tri", OFF[a], OFF[a], NB - 1 - a))
                for c in range(a + 1, NB):
                    terms.append(("neg_ones", c, OFF[a] + c - a - 1, 1))
                    if c < NB - 1:
                        terms.append(("neg_ones", OFF[c], OFF[a] + c - a, NB - 1 - c))
            return terms

        def act_mixer3(act, w, gain):
            n0, b0, g = w.column_layer(8)
            act_ahead(act, n0, 0, 0)
            act_rstd(act, w, 4 * (g ^ 1), EPS_2)
            for u in range(1, 8):
                act_ahead(act, n0, 0, u)
            for side in range(2):
                layer = w.square_layer(4)
                for kp in range(4):
                    act_ahead(act, layer[0], 0, kp)
            act.wait_ge(s_used, layer[0] + 4)
            act_prep(act, w, range(8), "ln_mix1", lambda m: None, squares=False)
            n0, b0, g = w.column_layer(8)
            for u in range(8):
                act_ahead(act, n0, 0, u)
            act.wait_ge(s_free, w.bank + 4)
            act_tile_norm(act, w, 1.0 / P, EPS_2)
            act_tile_norm(act, w, 1.0, P * EPS_2)
            act.wait_ge(s_tn, 4 * w.batches)
            ch = w.act_steps
            with ch.loop(4, 4) as i:
                for j in range(2):
                    act.wait_ge(s_sz, i * 2 + (j + 1))
                    act.wait_ge(s_so, i * 2 + 1)
                    l_ = sb_l[:, j, :, :].rearrange("p a t -> p (a t)")
                    z_ = ps[:, 3 * j:3 * j + 3, :].rearrange("p a t -> p (a t)")[:, 0:10 * P]
                    ch.link(nc.scalar.activation(l_, z_, ACT.Abs))
                    ch.step(nc.scalar.activation(l_, l_, ACT.Exp, scale=-1.0))
                ch.wait()
                for j in range(2):
                    l_ = sb_l[:, j, :, :].rearrange("p a t -> p (a t)")
                    nc.scalar.activation(l_, l_, ACT.Ln, bias=1.0).then_inc(s_sln, 1)
                for j in range(2):
                    act.wait_ge(s_slw, i * 2 + (j + 1))
                    l_ = sb_l[:, j, :, :].rearrange("p a t -> p (a t)")
                    z_ = ps[:, 3 * j + 1:3 * j + 3, :].rearrange("p a t -> p (a t)")[:, 0:6 * P]
                    nc.scalar.activation(l_[:, 4 * P:10 * P], z_, ACT.Exp)
                    act.wait_ge(s_swc, i * 2 + (j + 1))
                    nc.scalar.activation(l_[:, 0:4 * P], l_[:, 0:4 * P], ACT.Exp).then_inc(s_sw, 1)
                for j in range(2):
                    act.wait_ge(s_so, i * 2 + (j + 2))
                    nc.scalar.activation(tile_at(mid_hi, i * 2 + j), ps[:, 6 + j, :], ACT.Copy).then_inc(s_mhi, 1)
            w.mids += 8
            for side in range(2):
                layer = w.square_layer(4)
                for kp in range(4):
                    act_ahead(act, layer[0], 0, kp)
                act_prep(act, w, range(4 * side, 4 * side + 4), gain, lambda m: act.wait_ge(s_free, layer[1] + m % 4 + 5))

        def dve_mixer3(dve, w, ch, gain):
            def take(dest):
                n0, b0, g = w.column_layer(8)
                def body(i, j):
                    dve.wait_ge(s_used, i * 4 + (n0 + j + 1))
                    nc.vector.tensor_tensor(tile_at(dest, i * 4 + j), ps[:, 4 * g + j % 4, :], rstd[:, :], ALU.mult).then_inc(s_free, 1)
                each(dve, 8, body)

            dve.wait_ge(s_rstd, w.norms + 1)
            w.norms += 1
            take(k3)
            dve_rstd_columns(dve, w, 2)
            dve.wait_ge(s_rcol, 2)
            for half in range(2):
                dve_tokens_out(dve, w, v3[:, :, half * T:(half + 1) * T])
            dve_prep(dve, w, range(8), "ln_mix1", squares=False)
            take(q3)
            dve.wait_ge(s_free, w.bank + 4)
            dve_tile_squares(dve, w, k3)
            dve_tile_squares(dve, w, q3)
            dve_tile_norm(dve, w, ch, k3, "k_norm")
            dve_tile_norm(dve, w, ch, q3, "sb_q_norm")
            strict = mask["strict"].rearrange("p (a t) -> p a t", a=1).to_broadcast([P, NB, P])
            mids = w.mids
            with ch.loop(4, 2) as i:
                for j in range(2):
                    z_ = ps[:, 3 * j:3 * j + 3, :].rearrange("p a t -> p (a t)")[:, 0:10 * P]
                    dve.wait_ge(s_sln, i * 2 + (j + 1))
                    ch.link(nc.vector.scalar_tensor_tensor(out=sb_sp[:, j, :, :].rearrange("p a t -> p (a t)"), in0=z_, scalar=0.0,
                                                           in1=sb_l[:, j, :, :].rearrange("p a t -> p (a t)"), op0=ALU.max, op1=ALU.add))
                    nc.vector.tensor_tensor(sb_sp[:, j, 0:NB, :], sb_sp[:, j, 0:NB, :], strict, ALU.mult).then_inc(s_ssp, 1)
                for j in range(2):
                    dve.wait_ge(s_slw, i * 2 + (j + 1))
                    nc.vector.tensor_scalar(sb_l[:, j, 0:NB, :].rearrange("p a t -> p (a t)"), ps[:, 3 * j, :], 0.0, None, ALU.min).then_inc(s_swc, 1)
                for j in range(2):
                    dve.wait_ge(s_sw, i * 2 + (j + 2))
                    nc.vector.tensor_tensor(sb_l[:, j, 0:NB, :], sb_l[:, j, 0:NB, :], strict, ALU.mult).then_inc(s_swm, 1)
                for j in range(2):
                    dve.wait_ge(s_mhi, i * 2 + (mids + j + 1))
                    nc.vector.tensor_tensor(tile_at(mid_lo, i * 2 + j), ps[:, 6 + j, :], tile_at(mid_hi, i * 2 + j).bitcast(F32), ALU.subtract).then_inc(s_mlo, 1)
            w.mids += 8
            for side in range(2):
                dve_add_to_h(dve, w, 4, side, 1.0, gain)

        def pool_mixer3(pool, w):
            pool.wait_ge(s_free, w.bank + 4)
            pool_tile_norm(pool, w, k3)
            pool_tile_norm(pool, w, q3)
            pool.wait_ge(s_tn, 4 * w.batches)

            def stage_k(pair):
                for j in range(2):
                    nc.gpsimd.tensor_copy(sb_k[:, j, :], tile_at(k3, pair * 2 + j)).then_inc(s_sstk, 1)

            def stage_v(pair):
                for j in range(2):
                    col = (2 * pair + j) * P if isinstance(pair, int) else pair * 2 * P + j * P
                    cols = slice(col, col + P) if isinstance(pair, int) else bass.ds(col, P)
                    nc.gpsimd.tensor_copy(sb_v[:, j, :, :], v3[:, :, cols]).then_inc(s_sstv, 1)

            stage_k(0)
            stage_v(0)
            with pool.Fori(0, 3) as i:
                pool.wait_ge(s_sz, i * 2 + 2)
                pool.sem_inc(s_tick["pool"], 1)
                stage_k(i + 1)
                pool.wait_ge(s_so, i * 2 + 3)
                pool.sem_inc(s_tick["pool"], 1)
                stage_v(i + 1)

        def pe_final_norm(pe, w):
            pe_norm_sum(pe, w, 4 * w.group)
            w.norms += 1

        def act_final_norm(act, w):
            act_rstd(act, w, 4 * w.group, EPS_1)
            act_prep(act, w, range(8), "ln_mix0", lambda m: act.wait_ge(s_hup, w.hups + m + 1))
            w.hups += 8

        def dve_final_norm(dve, w):
            dve.wait_ge(s_rstd, w.norms + 1)
            w.norms += 1
            c = COL["final_norm"][0]
            for m in range(8):
                nc.vector.scalar_tensor_tensor(out=h[:, m, :], in0=h[:, m, :], scalar=vec[:, c + m:c + m + 1], in1=rstd[:, :],
                                               op0=ALU.mult, op1=ALU.mult).then_inc(s_hup, 1)
            dve_prep(dve, w, range(8), "ln_mix0")
            w.hups += 8

        from_one = [s_o, s_sfree, s_ptp, s_pt, s_zact, s_convact, s_gateact, s_go, s_so, s_sw]
        block = ctx.enter_context(nc.Block())

        @block.sync
        def _(sp):
            def load(i, n):
                unit = units[n] if isinstance(i, int) else units[bass.ds(i * 2 + n, 1), :, :].rearrange("a p n -> (a p) n")
                sp.dma_start(raw[:, n % 2, :], unit).then_inc(s_w[n % 2], 16)

            sp.dma_start(vec[:, :], vectors[:, :]).then_inc(s_const, 16)
            load(0, 0)
            for part in range(4):
                rows = slice(2 * part * P, 2 * (part + 1) * P)
                sp.dma_start(h[:, 2 * part:2 * part + 2, :], x_t[rows, :].rearrange("(k p) t -> p k t", p=P)).then_inc(s_x[part], 16)
            sp.dma_start(const[:, :, :], constants[:, :, :]).then_inc(s_const2, 16)
            load(0, 1)
            with sp.Fori(0, N_UNITS // 2 - 1) as i:
                for n in (2, 3):
                    sp.wait_ge(s_wlo, i * 2 + (n - 1))
                    load(i, n)
            for part in range(4):
                sp.wait_ge(s_hup, 16 + 2 * (part + 1))
                rows = slice(2 * part * P, 2 * (part + 1) * P)
                sp.dma_start(out_t[rows, :].rearrange("(k p) t -> p k t", p=P), h[:, 2 * part:2 * part + 2, :]).then_inc(s_out, 16)
            sp.wait_ge(s_out, 64)

        @block.gpsimd
        def _(pool):
            w = Walk()
            for one in from_one:
                pool.sem_inc(one, 1)
            pool.sem_inc(s_y, Y0)
            pool.sem_inc(s_yg, YG0)
            pool_at = [0]

            def split_to(end):
                n0 = pool_at[0]

                def body(i, j):
                    n = n0 + j
                    pool.wait_ge(s_whi, i * 4 + (n + 1))
                    nc.gpsimd.tensor_tensor(w_lo[:, n % W_SLOTS, :], raw[:, n % RAW_SLOTS, :], w_hi[:, n % W_SLOTS, :].bitcast(F32), ALU.subtract).then_inc(s_wlo, 1)

                each(pool, end - n0, body)
                pool_at[0] = end

            def ffn_walk():
                for tiles in HALVES:
                    w.column_layer(2 * tiles)
                    w.square_layer(tiles // 2)
                    w.square_layer(tiles // 2)

            ffn_walk()
            w.column_layer(U_END)
            w.square_layer(4)
            split_to(w.unit + AHEAD)
            pool_mixer1(pool, w)
            w.square_layer(6)
            w.square_layer(6)
            ffn_walk()
            w.column_layer(U_END2)
            split_to(w.unit + AHEAD)
            w.convs = 36
            pool_mixer2(pool, w)
            pool.wait_ge(s_go, 9)
            pool_tile_norm(pool, w, v2)
            w.square_layer(4)
            w.square_layer(4)
            ffn_walk()
            for units_ in (1, 1):
                w.square_layer(units_)
            w.column_layer(8)
            w.column_layer(8)
            w.square_layer(4)
            w.square_layer(4)
            w.column_layer(8)
            split_to(w.unit + AHEAD)
            pool_mixer3(pool, w)
            split_to(NREAL + AHEAD)

        @block.tensor
        def _(pe):
            w = Walk()
            pe.wait_ge(s_const2, 16)
            pe_ffn(pe, w)
            pe_mixer1(pe, w)
            pe_ffn(pe, w)
            pe_final_norm(pe, w)
            pe_mixer2(pe, w)
            pe_ffn(pe, w)
            pe_embed(pe, w)
            pe_mixer3(pe, w)
            pe_ffn(pe, w)
            pe_embed(pe, w)
            assert w.unit == NREAL, (w.unit, NREAL)

        @block.scalar
        def _(act):
            w = Walk()
            act_round(act, 0, 0)
            act.wait_ge(s_const, 16)
            act_prep(act, w, range(8), "ffn1_norm", lambda m: act.wait_ge(s_x[m // 2], 16))
            for n in range(1, AHEAD):
                act_round(act, 0, n)
            act_ffn(act, w, EPS_1, "mix_norm")
            act_mixer1(act, w, "ffn2_norm")
            act_ffn(act, w, EPS_1, None)
            act_final_norm(act, w)
            act_mixer2(act, w, "ln_ffn0")
            act_ffn(act, w, EPS_2, "ln_ple0", 0)
            act_embed(act, w, "kv_norm")
            act_mixer3(act, w, "ln_ffn1")
            act_ffn(act, w, EPS_2, "ln_ple1", 1)
            act_embed(act, w, None)

        @block.vector
        def _(dve):
            w = Walk()
            ch = Chain(dve, s_dve)
            for b in range(4):
                nc.vector.memset(rcol[:, b:b + 1], 0.0).then_inc(s_free, 1)
            dve.wait_ge(s_const, 16)
            dve_prep(dve, w, range(8), "ffn1_norm")
            dve.wait_ge(s_const2, 16)
            dve_ffn(dve, w, 0.5, "mix_norm")
            dve_mixer1(dve, w, ch, "ffn2_norm")
            dve_ffn(dve, w, 0.5, None)
            dve_final_norm(dve, w)
            dve_mixer2(dve, w, ch, "ln_ffn0")
            dve_ffn(dve, w, 1.0, "ln_ple0")
            dve_embed(dve, w, ch, "kv_norm")
            dve_mixer3(dve, w, ch, "ln_ffn1")
            dve_ffn(dve, w, 1.0, "ln_ple1")
            dve_embed(dve, w, ch, None)


def kernel(**inputs):
    import concourse.bacc as _bacc
    from concourse import mybir as _mybir
    from concourse.bass_utils import run_bass_kernel_spmd as _run

    a = {k: np.asarray(v) for k, v in inputs.items()}

    def column_units(wt):
        n = -(-wt.shape[1] // P)
        full = np.zeros((D, n * P), np.float32)
        full[:, :wt.shape[1]] = wt
        return full.reshape(DK, P, n, P).transpose(2, 1, 0, 3).reshape(n, P, UNIT)

    def square_units(wt):
        k, n = wt.shape
        return wt.reshape(k // 256, 2, P, n // T, T).transpose(3, 0, 2, 1, 4).reshape(-1, P, UNIT)

    def ffn_units(gate, up, down):
        parts, at = [], 0
        for tiles in HALVES:
            cols = slice(at * P, (at + tiles) * P)
            g, u = column_units(gate[:, cols]), column_units(up[:, cols])
            parts.append(np.stack([g, u], axis=1).reshape(2 * tiles, P, UNIT))
            parts.append(square_units(down[cols]))
            at += tiles
        return parts

    def ffn2(i):
        wt = a["ffn_w_in_2"][i]
        return ffn_units(wt[:, :D_FF], wt[:, D_FF:], a["ffn_w_out_2"][i])

    w1, g2 = a["w_in"][0], a["gdn_w_in_2"][0]
    ab = np.zeros((D, P), np.float32)
    ab[:, 0:8], ab[:, 32:40] = g2[:, 4096:4104], g2[:, 4104:4112]
    w_out = a["w_out"][0]
    units = np.concatenate(
        ffn_units(a["ffn1_w_gate"][0], a["ffn1_w_up"][0], a["ffn1_w_down"][0])
        + [column_units(w1[:, 2576:3600]), column_units(w1[:, 2560:2576]), column_units(w1[:, 1024:2560]),
           column_units(w1[:, 0:1024]), square_units(w1[:, 3600:4112]),
           square_units(np.concatenate([w_out[1024:], w_out[:1024]]))]
        + ffn_units(a["ffn2_w_gate"][0], a["ffn2_w_up"][0], a["ffn2_w_down"][0])
        + [column_units(g2[:, 0:3072]), column_units(ab), column_units(g2[:, 3072:4096]), square_units(a["gdn_w_out_2"][0])]
        + ffn2(0) + [square_units(a["ple_w_proj_2"][0]), column_units(a["ple_w_gate_2"][0])]
        + [column_units(a["w_kv_2"][:, 0:1024]), square_units(a["w_kv_2"][:, 1024:2048]), column_units(a["sb_w_q_2"][0]),
           square_units(a["sb_w_out_2"][0])]
        + ffn2(1) + [square_units(a["ple_w_proj_2"][1]), column_units(a["ple_w_gate_2"][1])]
        + [np.zeros((4, P, UNIT), np.float32)])

    vec = np.zeros((P, N_COL), np.float32)

    def put(name, block):
        at, n = COL[name]
        vec[:block.shape[0], at:at + n] = block

    def tiles_of(v):
        return v.reshape(-1, P).T

    for name, v in (("ffn1_norm", a["ffn1_norm"][0]), ("mix_norm", a["mix_norm"][0]), ("ffn2_norm", a["ffn2_norm"][0]),
                    ("final_norm", a["final_norm"]), ("ssd_norm", a["ssd_norm"][0]), ("conv_b", a["conv_b"][0]),
                    ("ln_mix0", a["ln_mix_2"][0]), ("ln_mix1", a["ln_mix_2"][1]), ("ln_ffn0", a["ln_ffn_2"][0]),
                    ("ln_ffn1", a["ln_ffn_2"][1]), ("ln_ple0", a["ln_ple_2"][0]), ("ln_ple1", a["ln_ple_2"][1]),
                    ("gdn_norm", a["gdn_norm_2"][0]), ("kv_norm", a["kv_norm_2"]), ("k_norm", a["k_norm_2"]),
                    ("sb_q_norm", a["sb_q_norm_2"][0]), ("d_skip", np.repeat(a["d_skip"][0], SSD_DIM))):
        put(name, tiles_of(v))
    for name, v in (("conv_w", a["conv_w"][0]), ("gdn_conv", a["gdn_conv_2"][0])):
        put(name, v.reshape(CONV, -1, P).transpose(2, 1, 0).reshape(P, -1))
    for name, v in (("dt_bias", a["dt_bias"][0]), ("a_log", a["a_log"][0]), ("gdn_a_log", a["gdn_a_log_2"][0]),
                    ("gdn_dt_bias", a["gdn_dt_bias_2"][0])):
        put(name, v.reshape(-1, 1))

    distance = np.arange(P)[:, None] - np.arange(T)[None, :] + (T - P)
    rel = a["rel_bias"][0][:, np.clip(distance, -REL, REL) + REL].transpose(1, 0, 2)

    arrays = {
        "units": units, "x_t": a["x"][0].T, "p_t": a["p_2"][:, 0].transpose(0, 2, 1), "vectors": vec,
        "constants": constant_tiles(), "rel_table": rel,
    }
    arrays = {f"in_{k}_dram": np.ascontiguousarray(v) for k, v in arrays.items()}
    nc = _bacc.Bacc("TRN2", target_bir_lowering=False, num_devices=1)
    args = [nc.dram_tensor(k, v.shape, _mybir.dt.from_np(v.dtype), kind="ExternalInput").ap() for k, v in arrays.items()]
    out = nc.dram_tensor("out_0_dram", (D, T), F32, kind="ExternalOutput").ap()
    build(nc, *args, out)
    r = _run(nc, [arrays], core_ids=[0])
    return np.ascontiguousarray(r.results[0]["out_0_dram"].T)[None]
```
